# Optimizing a Trainium2 kernel written in Bass

```python
import jax, jax.numpy as jnp
from jax import lax
import numpy as np

D_MODEL = 2048
BATCH = 1
SEQ = 512
DEPTH = 1
DEC_BATCH = 8
DEC_SEQ = 4
PAST_LEN = 2048
PAGE_SIZE = 128

D_MIX = D_MODEL
MLSTM_HEADS = 4
MLSTM_W = D_MIX // 2
MLSTM_DH = MLSTM_W // MLSTM_HEADS
DSA_HEADS = 4
DSA_W = D_MIX // 4
DSA_DH = DSA_W // DSA_HEADS
MEM_HEADS = 4
MEM_W = D_MIX // 4
MEM_DH = MEM_W // MEM_HEADS
N_MEM = 256
IDX_HEADS = 16
IDX_DH = 64
TOPK_MAX = 256
ROPE_THETA = 500000.0
ROPE_FRACTION = 4
CONV_W = 4
MLSTM_CHUNK = 64
Q_BLOCK = 128
RMS_EPS = 1e-6
LN_EPS = 1e-5
F_BIAS = 3.0
IN_SIZES = (2 * MLSTM_W, MLSTM_W, MLSTM_W, MLSTM_W, 2 * MLSTM_HEADS,
            DSA_W, DSA_W, DSA_W, DSA_W, IDX_HEADS * IDX_DH, IDX_HEADS, IDX_DH,
            MEM_W, MEM_W)
D_IN = sum(IN_SIZES)

kernel_name = 'hymba_mlstm_dsa_memxattn_step'

F32 = jnp.float32

def rms_norm(x, g):
    xf = x.astype(F32)
    y = xf * lax.rsqrt(jnp.mean(xf * xf, axis=-1, keepdims=True) + RMS_EPS)
    return (y * g.astype(F32)).astype(x.dtype)

def rope_partial(x, pos):
    dh = x.shape[-1]
    rot = dh // ROPE_FRACTION
    half = rot // 2
    inv = ROPE_THETA ** (-jnp.arange(half, dtype=F32) / half)
    ang = pos[:, None] * inv[None, :]
    ang = ang.reshape((ang.shape[0],) + (1,) * (x.ndim - 3) + (half,))
    cos, sin = jnp.cos(ang), jnp.sin(ang)
    xf = x.astype(F32)
    x1, x2 = xf[..., :half], xf[..., half:rot]
    out = jnp.concatenate([x1 * cos - x2 * sin, x1 * sin + x2 * cos, xf[..., rot:]], axis=-1)
    return out.astype(x.dtype)

def split_in(z):
    outs, o = [], 0
    for s in IN_SIZES:
        outs.append(z[..., o:o + s])
        o += s
    return outs

def causal_conv(x_pre, hist, w, b):
    xp = jnp.concatenate([hist.astype(x_pre.dtype), x_pre], axis=1)
    c = x_pre.shape[-1]
    y = lax.conv_general_dilated(xp, w[:, None, :].astype(x_pre.dtype), window_strides=(1,),
                                 padding='VALID', dimension_numbers=('NWC', 'WIO', 'NWC'),
                                 feature_group_count=c)
    return jax.nn.silu(y + b.astype(y.dtype)).astype(x_pre.dtype), xp[:, -(CONV_W - 1):]

def mlstm_chunk(carry, inp):
    C, n, m = carry
    q, k, v, ig, lf = inp
    L = q.shape[2]
    b = jnp.cumsum(lf, axis=-1)
    causal = jnp.tril(jnp.ones((L, L), dtype=bool))
    dmat = jnp.where(causal, b[..., :, None] - b[..., None, :] + ig[..., None, :], -jnp.inf)
    inter = b + m[..., None]
    m_t = jnp.maximum(inter, jnp.max(dmat, axis=-1))
    w_intra = jnp.exp(dmat - m_t[..., None])
    a_inter = jnp.exp(inter - m_t)
    s = jnp.einsum('bhtd,bhsd->bhts', q, k) * w_intra
    num = jnp.einsum('bhts,bhsd->bhtd', s, v) + a_inter[..., None] * jnp.einsum('bhed,bhtd->bhte', C, q)
    den = jnp.sum(s, axis=-1) + a_inter * jnp.einsum('bhd,bhtd->bht', n, q)
    h = num / jnp.maximum(jnp.abs(den), jnp.exp(-m_t))[..., None]
    m_new = m_t[..., -1]
    w_s = jnp.exp(b[..., -1:] - b + ig - m_new[..., None])
    a = jnp.exp(b[..., -1] + m - m_new)
    C_new = a[..., None, None] * C + jnp.einsum('bhs,bhse,bhsd->bhed', w_s, v, k)
    n_new = a[..., None] * n + jnp.einsum('bhs,bhsd->bhd', w_s, k)
    return (C_new, n_new, m_new), h

def mlstm_mixer(qk_conv, v_pre, o_pre, if_pre, b_if, head_norm, carry, chunk):
    B, T, _ = v_pre.shape

    def heads(t):
        return t.reshape(B, T, MLSTM_HEADS, MLSTM_DH).transpose(0, 2, 1, 3).astype(F32)

    q = heads(qk_conv[..., :MLSTM_W])
    k = heads(qk_conv[..., MLSTM_W:]) * (MLSTM_DH ** -0.5)
    v = heads(v_pre)
    g = (if_pre.astype(F32) + b_if.astype(F32)).transpose(0, 2, 1)
    ig = g[:, :MLSTM_HEADS]
    lf = jax.nn.log_sigmoid(g[:, MLSTM_HEADS:])
    nc = T // chunk

    def to_chunks(t):
        t = t.reshape(t.shape[:2] + (nc, chunk) + t.shape[3:])
        return jnp.moveaxis(t, 2, 0)

    carry, h = lax.scan(mlstm_chunk, carry, (to_chunks(q), to_chunks(k), to_chunks(v),
                                             to_chunks(ig), to_chunks(lf)))
    h = jnp.moveaxis(h, 0, 2).reshape(B, MLSTM_HEADS, T, MLSTM_DH).transpose(0, 2, 1, 3)
    mu = jnp.mean(h, axis=-1, keepdims=True)
    var = jnp.mean(jnp.square(h - mu), axis=-1, keepdims=True)
    h = (h - mu) * lax.rsqrt(var + LN_EPS) * head_norm.reshape(MLSTM_HEADS, MLSTM_DH).astype(F32)
    h = h.reshape(B, T, MLSTM_W) * jax.nn.sigmoid(o_pre.astype(F32))
    return h.astype(v_pre.dtype), carry

def indexer_scores(iq, iw, ik, causal):
    sc = jax.nn.relu(jnp.einsum('bqhd,bld->bqhl', iq.astype(F32), ik.astype(F32)))
    I = jnp.einsum('bqhl,bqh->bql', sc, iw.astype(F32)) * (IDX_DH ** -0.5 * IDX_HEADS ** -0.5)
    return jnp.where(causal, I, -jnp.inf)

def sparse_attend(q, kg, vg, valid):
    logits = jnp.einsum('bqhd,bqkhd->bhqk', q.astype(F32), kg.astype(F32)) * (DSA_DH ** -0.5)
    logits = jnp.where(valid[:, None], logits, -jnp.inf)
    p = jax.nn.softmax(logits, axis=-1)
    return jnp.einsum('bhqk,bqkhd->bqhd', p, vg.astype(F32)).astype(q.dtype)

def mem_kv(mem, g, w):
    B, M, _ = mem.shape
    kv = rms_norm(mem, g) @ w
    return (kv[..., :MEM_W].reshape(B, M, MEM_HEADS, MEM_DH),
            kv[..., MEM_W:].reshape(B, M, MEM_HEADS, MEM_DH))

def mem_attend(q, mk, mv):
    B, T = q.shape[:2]
    logits = jnp.einsum('bthd,bmhd->bhtm', q.astype(F32), mk.astype(F32)) * (MEM_DH ** -0.5)
    p = jax.nn.softmax(logits, axis=-1)
    out = jnp.einsum('bhtm,bmhd->bthd', p, mv.astype(F32))
    return out.reshape(B, T, MEM_W).astype(q.dtype)

def merge(x, m_out, m_gate, a_out, a_gate, c_out, c_gate, w_out, g_post):
    mix = jnp.concatenate([m_out * jax.nn.silu(m_gate), a_out * jax.nn.silu(a_gate),
                           c_out * jax.nn.silu(c_gate)], axis=-1)
    return x + rms_norm(mix @ w_out, g_post)

def gather_rows(t, idx):
    return jax.vmap(lambda tb, ib: tb[ib])(t, idx)

def prompt_layer(x, mem, g_pre, w_in, b_if, conv_w, conv_b, head_norm, g_mem, w_mem_kv, w_out, g_post):
    B, S, _ = x.shape
    pos = jnp.arange(S, dtype=F32)
    (m_qk, m_v, m_o, m_gate, m_if, a_q, a_k, a_v, a_gate,
     i_q, i_w, i_k, c_q, c_gate) = split_in(rms_norm(x, g_pre) @ w_in)
    qk, conv_state = causal_conv(m_qk, jnp.zeros((B, CONV_W - 1, 2 * MLSTM_W), x.dtype), conv_w, conv_b)
    carry0 = (jnp.zeros((B, MLSTM_HEADS, MLSTM_DH, MLSTM_DH), F32),
              jnp.zeros((B, MLSTM_HEADS, MLSTM_DH), F32), jnp.zeros((B, MLSTM_HEADS), F32))
    m_out, (C, n, m) = mlstm_mixer(qk, m_v, m_o, m_if, b_if, head_norm, carry0, MLSTM_CHUNK)
    q = rope_partial(a_q.reshape(B, S, DSA_HEADS, DSA_DH), pos)
    k = rope_partial(a_k.reshape(B, S, DSA_HEADS, DSA_DH), pos)
    v = a_v.reshape(B, S, DSA_HEADS, DSA_DH)
    iq = rope_partial(i_q.reshape(B, S, IDX_HEADS, IDX_DH), pos)
    ik = rope_partial(i_k, pos)
    top_k = min(TOPK_MAX, S // 4)
    kpos = jnp.arange(S)

    def block(qb):
        t0 = qb * Q_BLOCK
        sl = lambda t: lax.dynamic_slice_in_dim(t, t0, Q_BLOCK, axis=1)
        tpos = t0 + jnp.arange(Q_BLOCK)
        I = indexer_scores(sl(iq), sl(i_w), ik, kpos[None, :] <= tpos[:, None])
        _, idx = lax.top_k(I, top_k)
        valid = idx <= tpos[None, :, None]
        return sparse_attend(sl(q), gather_rows(k, idx), gather_rows(v, idx), valid)

    a_out = lax.map(block, jnp.arange(S // Q_BLOCK))
    a_out = jnp.moveaxis(a_out, 0, 1).reshape(B, S, DSA_W)
    mk, mv = mem_kv(mem, g_mem, w_mem_kv)
    c_out = mem_attend(c_q.reshape(B, S, MEM_HEADS, MEM_DH), mk, mv)
    y = merge(x, m_out, m_gate, a_out, a_gate, c_out, c_gate, w_out, g_post)
    return y, (k, v, ik, C, n, m, conv_state, mk, mv)

def sample_layer(x, c_k, c_v, c_ik, C0, n0, m0, conv_hist, mk, mv, page_table,
                 g_pre, w_in, b_if, conv_w, conv_b, head_norm, w_out, g_post):
    B, T, _ = x.shape
    past = page_table.shape[1] * PAGE_SIZE
    tpos = past + jnp.arange(T)
    pos = tpos.astype(F32)
    (m_qk, m_v, m_o, m_gate, m_if, a_q, a_k, a_v, a_gate,
     i_q, i_w, i_k, c_q, c_gate) = split_in(rms_norm(x, g_pre) @ w_in)
    qk, conv_new = causal_conv(m_qk, conv_hist, conv_w, conv_b)
    carry0 = (C0.astype(F32), n0.astype(F32), m0.astype(F32))
    m_out, (C, n, m) = mlstm_mixer(qk, m_v, m_o, m_if, b_if, head_norm, carry0, T)
    q = rope_partial(a_q.reshape(B, T, DSA_HEADS, DSA_DH), pos)
    k = rope_partial(a_k.reshape(B, T, DSA_HEADS, DSA_DH), pos)
    v = a_v.reshape(B, T, DSA_HEADS, DSA_DH)
    iq = rope_partial(i_q.reshape(B, T, IDX_HEADS, IDX_DH), pos)
    ik = rope_partial(i_k, pos)
    ik_past = c_ik[page_table].reshape(B, past, IDX_DH)
    ik_all = jnp.concatenate([ik_past.astype(ik.dtype), ik], axis=1)
    kpos = jnp.arange(past + T)
    I = indexer_scores(iq, i_w, ik_all, kpos[None, :] <= tpos[:, None])
    top_k = min(TOPK_MAX, (past + T) // 4)
    _, idx = lax.top_k(I, top_k)
    valid = idx <= tpos[None, :, None]
    in_past = (idx < past)[..., None, None]
    pidx = jnp.minimum(idx, past - 1)
    phys = jax.vmap(lambda pt, i: pt[i])(page_table, pidx // PAGE_SIZE)
    off = pidx % PAGE_SIZE
    nidx = jnp.clip(idx - past, 0, T - 1)
    kg = jnp.where(in_past, c_k[phys, off].astype(k.dtype), gather_rows(k, nidx))
    vg = jnp.where(in_past, c_v[phys, off].astype(v.dtype), gather_rows(v, nidx))
    a_out = sparse_attend(q, kg, vg, valid).reshape(B, T, DSA_W)
    c_out = mem_attend(c_q.reshape(B, T, MEM_HEADS, MEM_DH), mk, mv)
    y = merge(x, m_out, m_gate, a_out, a_gate, c_out, c_gate, w_out, g_post)
    return y, (k, v, ik, C, n, m, conv_new)

def setup_inputs(seed: int = 0) -> dict:
    key = jax.random.key(seed)
    ks = jax.random.split(key, 24)
    n_pages = PAST_LEN // PAGE_SIZE
    n_used = DEC_BATCH * n_pages
    n_pool = n_used + max(1, n_used // 4)
    page_table = jax.random.permutation(ks[0], n_pool)[:n_used].reshape(DEC_BATCH, n_pages).astype(jnp.int32)

    def nrm(k, shape, s=1.0):
        return jax.random.normal(k, shape, F32) * s

    b_if = jnp.concatenate([nrm(ks[13], (DEPTH, MLSTM_HEADS), 0.1),
                            F_BIAS + nrm(ks[14], (DEPTH, MLSTM_HEADS), 0.1)], axis=-1)
    return {
        'x_prompt': nrm(ks[1], (BATCH, SEQ, D_MODEL)),
        'x_sample': nrm(ks[2], (DEC_BATCH, DEC_SEQ, D_MODEL)),
        'cache_attn_k': nrm(ks[4], (DEPTH, n_pool, PAGE_SIZE, DSA_HEADS, DSA_DH)),
        'cache_attn_v': nrm(ks[5], (DEPTH, n_pool, PAGE_SIZE, DSA_HEADS, DSA_DH)),
        'cache_idx_k': nrm(ks[6], (DEPTH, n_pool, PAGE_SIZE, IDX_DH)),
        'state_mlstm_C': nrm(ks[7], (DEPTH, DEC_BATCH, MLSTM_HEADS, MLSTM_DH, MLSTM_DH), MLSTM_DH ** -0.5),
        'state_mlstm_n': nrm(ks[8], (DEPTH, DEC_BATCH, MLSTM_HEADS, MLSTM_DH), MLSTM_DH ** -0.5),
        'state_mlstm_m': nrm(ks[9], (DEPTH, DEC_BATCH, MLSTM_HEADS)),
        'state_conv': nrm(ks[10], (DEPTH, DEC_BATCH, CONV_W - 1, 2 * MLSTM_W)),
        'cache_mem_k': nrm(ks[11], (DEPTH, DEC_BATCH, N_MEM, MEM_HEADS, MEM_DH)),
        'cache_mem_v': nrm(ks[12], (DEPTH, DEC_BATCH, N_MEM, MEM_HEADS, MEM_DH)),
        'page_table': page_table,
        'mem_prompt': nrm(ks[3], (BATCH, N_MEM, D_MODEL)),
        'norm_pre': 1.0 + nrm(ks[15], (DEPTH, D_MODEL), 0.02),
        'w_in': nrm(ks[16], (DEPTH, D_MODEL, D_IN), D_MODEL ** -0.5),
        'b_if': b_if,
        'conv_w': nrm(ks[17], (DEPTH, CONV_W, 2 * MLSTM_W), CONV_W ** -0.5),
        'conv_b': nrm(ks[18], (DEPTH, 2 * MLSTM_W), 0.01),
        'mlstm_head_norm': 1.0 + nrm(ks[19], (DEPTH, MLSTM_W), 0.02),
        'mem_norm': 1.0 + nrm(ks[20], (DEPTH, D_MODEL), 0.02),
        'w_mem_kv': nrm(ks[21], (DEPTH, D_MODEL, 2 * MEM_W), D_MODEL ** -0.5),
        'w_out': nrm(ks[22], (DEPTH, D_MIX, D_MODEL), D_MIX ** -0.5),
        'norm_post': 1.0 + nrm(ks[23], (DEPTH, D_MODEL), 0.02),
    }

def reference(x_prompt, x_sample, cache_attn_k, cache_attn_v, cache_idx_k, state_mlstm_C, state_mlstm_n,
              state_mlstm_m, state_conv, cache_mem_k, cache_mem_v, page_table, mem_prompt,
              norm_pre, w_in, b_if, conv_w, conv_b, mlstm_head_norm, mem_norm, w_mem_kv, w_out, norm_post):
    yp, ys = x_prompt, x_sample
    p_states, s_states = [], []
    for l in range(DEPTH):
        yp, sp = prompt_layer(yp, mem_prompt, norm_pre[l], w_in[l], b_if[l], conv_w[l], conv_b[l],
                              mlstm_head_norm[l], mem_norm[l], w_mem_kv[l], w_out[l], norm_post[l])
        ys, ss = sample_layer(ys, cache_attn_k[l], cache_attn_v[l], cache_idx_k[l], state_mlstm_C[l],
                              state_mlstm_n[l], state_mlstm_m[l], state_conv[l], cache_mem_k[l],
                              cache_mem_v[l], page_table, norm_pre[l], w_in[l], b_if[l], conv_w[l],
                              conv_b[l], mlstm_head_norm[l], w_out[l], norm_post[l])
        p_states.append(sp)
        s_states.append(ss)
    p_k, p_v, p_ik, p_C, p_n, p_m, p_conv, p_mk, p_mv = [jnp.stack(t, axis=0) for t in zip(*p_states)]
    s_k, s_v, s_ik, s_C, s_n, s_m, s_conv = [jnp.stack(t, axis=0) for t in zip(*s_states)]
    return (yp, ys, p_k, p_v, p_ik, p_C, p_n, p_m, p_conv, p_mk, p_mv,
            s_k, s_v, s_ik, s_C, s_n, s_m, s_conv)


_drawn_inputs = setup_inputs


def setup_inputs(seed=0):
    import zlib

    import numpy as np

    out = dict(_drawn_inputs(seed))
    spreads = {}
    factors = {'conv_b': 2.765, 'mlstm_head_norm': 4.258, 'mem_norm': 2.865, 'norm_post': 4.046}
    for name, (base, spread) in spreads.items():
        noise = np.random.default_rng([zlib.crc32(name.encode()), seed]).standard_normal(out[name].shape)
        drawn = base * np.exp(spread * noise) if base else spread * noise
        out[name] = __import__('jax').numpy.asarray(drawn.astype(out[name].dtype))
    for name, factor in factors.items():
        out[name] = (out[name] * factor).astype(out[name].dtype)
    return out
```

```python
import concourse.bass as bass
from concourse import mybir
from contextlib import ExitStack


def hybrid_decoder_step(nc, I, C, O):
    F32, F32R, U32, I32 = mybir.dt.float32, mybir.dt.float32r, mybir.dt.uint32, mybir.dt.int32
    ALU, ACT, AX = mybir.AluOpType, mybir.ActivationFunctionType, mybir.AxisListType

    P = 128
    D = I["x_prompt"].shape[2]
    S = I["x_prompt"].shape[1]
    NB, NQ = I["x_sample"].shape[0], I["x_sample"].shape[1]
    R = NB * NQ
    KT = D // P
    MT = S // P
    H = I["state_mlstm_C"].shape[2]
    MD = I["state_mlstm_C"].shape[3]
    MW = H * MD
    AD = I["cache_attn_k"].shape[4]
    AW = H * AD
    ID = I["cache_idx_k"].shape[3]
    IH = 16
    NMEM = I["mem_prompt"].shape[1]
    NPG = I["page_table"].shape[1]
    PG = I["cache_idx_k"].shape[2]
    PAST = NPG * PG
    NPOOL = I["cache_idx_k"].shape[1]
    KSEL_P = min(256, S // 4)
    KSEL_S = min(256, (PAST + NQ) // 4)
    W_IN = I["w_in"].shape[2]
    C_QK, C_V, C_O, C_G = 0, 2 * MW, 3 * MW, 4 * MW
    C_IF = 5 * MW
    C_AQ = C_IF + 2 * H
    C_AK, C_AV, C_AG = C_AQ + AW, C_AQ + 2 * AW, C_AQ + 3 * AW
    C_IQ = C_AQ + 4 * AW
    C_IW = C_IQ + IH * ID
    C_IK = C_IW + IH
    C_CQ = C_IK + ID
    C_CG = C_CQ + AW
    assert C_CG + AW == W_IN
    NEG, TAKEN = -1.0e30, -3.0e38
    RMS_EPS, LN_EPS = 1e-6, 1e-5

    TN = 512
    N_MEM0 = 0
    N_A0 = 2
    NA = (W_IN - C_IF) // TN
    IX0 = (C_IQ - C_IF) // TN
    IXT = -(-(C_CQ - C_IF) // TN) - IX0
    N_REST = N_A0 + NA
    REST = (W_IN - C_IF) % TN
    N_B0 = N_REST + 1
    NBT = C_IF // TN
    N_Y0 = N_B0 + NBT
    NY = D // TN
    N_END = N_Y0 + NY
    CH = 8
    KC = KT // CH
    RAWS = 4

    ctx = ExitStack()
    with ctx:
        def sb(name, shape, dt=F32, c=ctx):
            return c.enter_context(nc.sbuf_tensor(name, shape, dt))

        def sem(name):
            return ctx.enter_context(nc.semaphore(name))

        def scratch(name, shape):
            return nc.dram_tensor(name, shape, F32, kind="Internal").ap()

        z_p = scratch("z_prompt", [S, W_IN])
        z_s = scratch("z_sample", [2 * R, W_IN])
        mix_p = scratch("mix_prompt", [S, D])
        mix_s = scratch("mix_sample", [R, D])
        q_s = scratch("q_sample", [R, AW])
        k_s = scratch("k_sample", [R, AW])
        v_s = scratch("v_sample", [R, AW])
        iw_s = scratch("iw_sample", [R, IH])

        ident = sb("ident", [P, P])
        x_hi = sb("x_hi", [P, KT, S + 2 * R], F32R)
        x_lo = sb("x_lo", [P, KT, S], F32R)
        w_raw = sb("w_raw", [P, RAWS, KC, TN])
        w_hi = sb("w_hi", [P, 2, KC, TN], F32R)
        w_lo = sb("w_lo", [P, 2, KC, TN], F32R)
        z_tile = sb("z_tile", [P, MT + 1, TN])
        mem_kv = sb("mem_kv", [P, NMEM // P, 2 * AW])
        small = sb("small", [P, 64])
        pro = ExitStack()
        with pro:
            m_hi = sb("m_hi", [P, KT, NMEM], F32R, pro)
            m_lo = sb("m_lo", [P, KT, NMEM], F32R, pro)
            x_in = sb("x_in", [P, 2, D], F32, pro)
            g_row = sb("g_row", [P, D], F32, pro)
            junk = sb("junk", [P, D], F32, pro)
        AR_N = 20960
        arena = sb("arena", [P, AR_N])
        acc = [ctx.enter_context(nc.psum_tensor(f"acc{m}", [P, TN], F32)) for m in range(MT + 1)]
        ps_a, ps_b, ps_c = (ctx.enter_context(nc.psum_tensor(f"ps_{x}", [P, TN], F32)) for x in "abc")

        POINTS = {
            "vector": (
                        "idx_ready", "pick_ready", "za_ready", "gate_in", "phys_ready", "phys_u_ready",
                        "max_s", "probs_copied", "ot_copied", "mixed_s", "cq_ready", "gate_c_in",
                        "qs_ready", "cmax", "ps_ready", "mixed_c", "ifs_ready", "g_abs", "g_rows",
                        "sm_ready", "scv_ready", "ks_scaled", "bc_copied", "qspr_ready", "pws_ready",
                        "y_joined",),
            "scalar": (
                        "new_copied", "gate_ready", "exp_s", "gate_c_ready", "cexp", "conv_w_c",
                        "g_exp", "g_ln", "g_we", "g_cols", "scv_silu", "sw_exp",),
            "tensor": (
                        "new_turned", "phys_turned", "sc_turned", "probs_turned", "o_turned", "cq_turned",
                        "cp_turned", "conv_w_t", "g_colt", "bc_done", "ss_done",),
        }
        point_sem = {e: sem(f"{e}_points") for e in POINTS}
        passed = {e: 0 for e in POINTS}
        point_of = {n: (e, i) for e, names in POINTS.items() for i, n in enumerate(names)}

        def at(name):
            e, i = point_of[name]
            return point_sem[e], i + 1

        def reached(name):
            e, i = point_of[name]
            assert passed[e] == i, (name, passed[e])
            passed[e] += 1
            return point_sem[e]

        unit_rows = [P] * (NMEM // P) + [P] * MT + [R]
        NU_MEM, NU_NORM = NMEM // P, NMEM // P + MT + 1
        NU_ALL = NU_NORM + MT + 1
        unit_rows += [P] * MT + [R]
        x_loaded = [sem("x_loaded0"), sem("x_loaded1")]
        g_loaded, consts_in = sem("g_loaded"), sem("consts_in")
        (squares_done, var_done, std_done, row_scaled) = (
            sem(n) for n in ("squares_done", "var_done", "std_done", "row_scaled"))
        rows_turned, hi_taken, lo_taken = sem("rows_turned"), sem("hi_taken"), sem("lo_taken")
        dve_step, act_step = sem("dve_step"), sem("act_step")
        steps = {"dve": 0, "act": 0}

        def dlink(ins):
            steps["dve"] += 1
            ins.then_inc(dve_step, 1)
            nc.vector.wait_ge(dve_step, steps["dve"])

        def alink(ins):
            steps["act"] += 1
            ins.then_inc(act_step, 1)
            nc.scalar.wait_ge(act_step, steps["act"])

        def unit_source(u):
            if u < NU_MEM:
                return I["mem_prompt"][0, u * P:(u + 1) * P, :]
            if u < NU_NORM - 1:
                return I["x_prompt"][0, (u - NU_MEM) * P:(u - NU_MEM + 1) * P, :]
            if u == NU_NORM - 1:
                return I["x_sample"].rearrange("b t d -> (b t) d")
            if u < NU_ALL - 1:
                return mix_p[(u - NU_NORM) * P:(u - NU_NORM + 1) * P, :]
            return mix_s

        def unit_dest(u, k0, n):
            ks = slice(k0, k0 + n)
            if u < NU_MEM:
                return m_hi[:, ks, u * P:(u + 1) * P], m_lo[:, ks, u * P:(u + 1) * P]
            i = u - NU_MEM if u < NU_NORM else u - NU_NORM
            if i < MT:
                return x_hi[:, ks, i * P:(i + 1) * P], x_lo[:, ks, i * P:(i + 1) * P]
            return x_hi[:, ks, S:S + R], x_hi[:, ks, S + R:S + 2 * R]

        def rows_buffer(u):
            return x_in[:, u % 2, :] if u < NU_NORM else y_in(u)

        TG = 4
        NGRP = KT // TG

        def sync_rows(sp, u0, u1):
            for u in range(u0, u1):
                if u >= 2:
                    sp.wait_ge(rows_turned, NGRP * (u - 1))
                sp.dma_start(rows_buffer(u)[0:unit_rows[u], :], unit_source(u)).then_inc(x_loaded[u % 2], 16)
                if u == 1:
                    sp.wait_ge(row_scaled, NU_MEM)
                    sp.dma_start(g_row[:, :], I["norm_pre"][0:1, :].broadcast_to([P, D])).then_inc(g_loaded, 16)

        def scalar_row_scale(act, u):
            n = unit_rows[u]
            act.wait_ge(x_loaded[u % 2], 16 * (u // 2 + 1))
            if u:
                act.wait_ge(squares_done, u)
            nc.scalar.activation(junk[0:n, :], rows_buffer(u)[0:n, :], ACT.Square,
                                 accum_out=small[0:n, u:u + 1]).then_inc(squares_done, 1)
            act.wait_ge(var_done, u + 1)
            nc.scalar.activation(small[0:n, 16 + u:17 + u], small[0:n, 8 + u:9 + u], ACT.Sqrt).then_inc(std_done, 1)

        def rsqrt_refined(var, root, out):
            dlink(nc.vector.reciprocal(out, root))
            dlink(nc.vector.scalar_tensor_tensor(out=root, in0=out, scalar=out, in1=var, op0=ALU.mult, op1=ALU.mult))
            dlink(nc.vector.tensor_scalar(root, root, -0.5, 1.5, ALU.mult, ALU.add))
            dlink(nc.vector.tensor_tensor(out=out, in0=out, in1=root, op=ALU.mult))

        def vector_row_scale(dve, u):
            n = unit_rows[u]
            dve.wait_ge(squares_done, u + 1)
            nc.vector.tensor_scalar(small[0:n, 8 + u:9 + u], small[0:n, u:u + 1], 1.0 / D, RMS_EPS,
                                    ALU.mult, ALU.add).then_inc(var_done, 1)
            dve.wait_ge(std_done, u + 1)
            rsqrt_refined(small[0:n, 8 + u:9 + u], small[0:n, 16 + u:17 + u], small[0:n, 24 + u:25 + u])
            dve.wait_ge(g_loaded, 16 if u < NU_MEM else 32)
            nc.vector.scalar_tensor_tensor(out=rows_buffer(u)[0:n, :], in0=rows_buffer(u)[0:n, :],
                                           scalar=small[0:n, 24 + u:25 + u], in1=g_row[0:n, :],
                                           op0=ALU.mult, op1=ALU.mult).then_inc(row_scaled, 1)

        def tensor_turn(pe, u):
            n = unit_rows[u]
            if u < NU_NORM:
                pe.wait_ge(row_scaled, u + 1)
            else:
                pe.wait_ge(x_loaded[u % 2], 16 * (u // 2 + 1))
            for j in range(NGRP):
                g = NGRP * u + j
                if g >= 2:
                    pe.wait_ge(lo_taken, g - 1)
                if j:
                    yield
                bank = (ps_a, ps_b)[g % 2]
                for i in range(TG):
                    k = j * TG + i
                    last = nc.tensor.transpose(bank[:, i * n:(i + 1) * n], rows_buffer(u)[0:n, k * P:(k + 1) * P],
                                               ident[0:n, 0:n])
                last.then_inc(rows_turned, 1)
            yield

        def scalar_take_hi(act, u):
            n = unit_rows[u]
            if u == NU_NORM:
                act.wait_ge(chunk_used, CH * N_Y0)
            for j in range(NGRP):
                g = NGRP * u + j
                bank = (ps_a, ps_b)[g % 2][:, 0:TG * n].rearrange("p (k r) -> p k r", k=TG)
                act.wait_ge(rows_turned, g + 1)
                nc.scalar.copy(unit_dest(u, j * TG, TG)[0], bank).then_inc(hi_taken, 1)
                if j == 1 and NU_MEM <= u < NU_NORM - 1:
                    scalar_row_scale(act, u + 1)
                yield

        def vector_take_lo(dve, u):
            n = unit_rows[u]
            for j in range(NGRP):
                if j == 2 and NU_MEM <= u < NU_NORM - 1:
                    vector_row_scale(dve, u + 1)
                g = NGRP * u + j
                bank = (ps_a, ps_b)[g % 2][:, 0:TG * n].rearrange("p (k r) -> p k r", k=TG)
                hi, lo = unit_dest(u, j * TG, TG)
                dve.wait_ge(hi_taken, g + 1)
                nc.vector.tensor_tensor(out=lo, in0=bank, in1=hi.bitcast(F32), op=ALU.subtract).then_inc(lo_taken, 1)

        w_loaded = [sem(f"w_loaded{s}") for s in range(RAWS)]
        chunk_hi, chunk_lo, chunk_used = sem("chunk_hi"), sem("chunk_lo"), sem("chunk_used")
        acc_ready, acc_read = sem("acc_ready"), sem("acc_read")
        z_stored = [sem(f"z_stored{m}") for m in range(MT + 1)]

        def width(n):
            return REST if isinstance(n, int) and n == N_REST else TN

        def acc_base(n):
            return (MT + 1) * n - (MT + 1 - NU_MEM) * N_A0 if not isinstance(n, int) or n >= N_A0 else NU_MEM * n

        w_mem_v = I["w_mem_kv"][0].rearrange("(k p) n -> p k n", p=P)
        w_in_v = I["w_in"][0].rearrange("(k p) n -> p k n", p=P)
        w_out_v = I["w_out"][0].rearrange("(k p) n -> p k n", p=P)

        def tile_source(n):
            if not isinstance(n, int) or n >= N_Y0:
                return w_out_v, TN * (n - N_Y0)
            if n < N_A0:
                return w_mem_v, TN * n
            if n >= N_B0:
                return w_in_v, TN * (n - N_B0)
            i = n - N_A0
            return w_in_v, C_IF + TN * (i + IX0 if i < IXT else i - IXT if i < IX0 + IXT else i)

        def scalar_load(act, n, c):
            if c >= CH:
                n, c = n + 1, c - CH
            if isinstance(n, int) and n >= N_END:
                return
            src, col = tile_source(n)
            w = width(n)
            cols = slice(col, col + w) if isinstance(n, int) else bass.ds(col, w)
            s = c % RAWS
            act.dma_start(w_raw[:, s, :, 0:w], src[:, c * KC:(c + 1) * KC, cols]).then_inc(w_loaded[s], 16)

        def scalar_hi(act, n, c, w=TN):
            j = CH * n + c
            if not (isinstance(n, int) and j < 2):
                act.wait_ge(chunk_used, j - 1)
            scalar_load(act, n, c + 2)
            act.wait_ge(w_loaded[c % RAWS], 16 * (CH // RAWS * n + c // RAWS + 1))
            nc.scalar.copy(w_hi[:, c % 2, :, 0:w], w_raw[:, c % RAWS, :, 0:w]).then_inc(chunk_hi, 1)

        def gpsimd_lo(pool, n, c, w=TN):
            pool.wait_ge(chunk_hi, CH * n + c + 1)
            nc.gpsimd.tensor_tensor(out=w_lo[:, c % 2, :, 0:w], in0=w_raw[:, c % RAWS, :, 0:w],
                                    in1=w_hi[:, c % 2, :, 0:w].bitcast(F32), op=ALU.subtract).then_inc(chunk_lo, 1)

        NO_STEPS = (iter(()), iter(()))

        def hosted_pause(pieces):
            for _ in range(pieces):
                yield

        def tensor_tile(pe, n, kind, steps=NO_STEPS):
            w = width(n)
            nm = NU_MEM if kind == "mem" else MT + 1
            for c in range(CH):
                pe.wait_ge(chunk_lo, CH * n + c + 1)
                if isinstance(n, int) and n == 0 and c == 0:
                    pe.wait_ge(lo_taken, NGRP * NU_MEM)
                if isinstance(n, int) and n == N_A0 and c == 0:
                    pe.wait_ge(lo_taken, NGRP * NU_NORM)
                if isinstance(n, int) and n == N_Y0 and c == 0:
                    pe.wait_ge(lo_taken, NGRP * NU_ALL)
                for m in range(nm):
                    if c == 0 and not (isinstance(n, int) and n == 0):
                        before = acc_base(n) if not (isinstance(n, int) and n == N_A0) else acc_base(N_A0)
                        back = nm if not (isinstance(n, int) and n == N_A0) else NU_MEM
                        if m < back:
                            pe.wait_ge(acc_read, before - back + m + 1)
                    for i in range(KC):
                        k = c * KC + i
                        first, end = (k == 0), (k == KT - 1)
                        wh, wl = w_hi[:, c % 2, i, 0:w], w_lo[:, c % 2, i, 0:w]
                        if m == MT:
                            xs = x_hi[:, k, S:S + 2 * R]
                            nc.tensor.matmul(acc[m][0:2 * R, 0:w], xs, wh, start=first, stop=False)
                            last = nc.tensor.matmul(acc[m][0:2 * R, 0:w], xs, wl, start=False, stop=end)
                        else:
                            hi_t, lo_t = (m_hi, m_lo) if kind == "mem" else (x_hi, x_lo)
                            xh, xl = hi_t[:, k, m * P:(m + 1) * P], lo_t[:, k, m * P:(m + 1) * P]
                            nc.tensor.matmul(acc[m][:, 0:w], xh, wh, start=first, stop=False)
                            nc.tensor.matmul(acc[m][:, 0:w], xh, wl, start=False, stop=False)
                            last = nc.tensor.matmul(acc[m][:, 0:w], xl, wh, start=False, stop=end)
                    if m == nm - 1:
                        last.then_inc(chunk_used, 1)
                    if c == CH - 1 and m < nm - 1:
                        last.then_inc(acc_ready, 1)
                    if m == nm - 1:
                        next(steps[1], None)
                    if m == (nm - 1) // 2 or m == nm - 1:
                        next(steps[0], None)

        def scalar_evacuate(act, n, kind):
            w = width(n)
            nm = NU_MEM if kind == "mem" else MT + 1
            for m in range(nm):
                rows = P if m < MT else 2 * R
                if m < nm - 1:
                    act.wait_ge(acc_ready, acc_ready_base(n) + m + 1)
                else:
                    act.wait_ge(chunk_used, CH * n + CH)
                if kind == "mem":
                    nc.scalar.copy(mem_kv[:, m, n * TN:(n + 1) * TN], acc[m][:, :]).then_inc(acc_read, 1)
                    continue
                if kind == "y":
                    nc.scalar.copy(y_rows(m)[0:rows, bass.ds((n - N_Y0) * TN, TN)],
                                   acc[m][0:rows, :]).then_inc(acc_read, 1)
                    continue
                if not (isinstance(n, int) and n == N_A0):
                    act.wait_ge(z_stored[m], 16 * (n - N_A0))
                nc.scalar.copy(z_tile[0:rows, m, 0:w], acc[m][0:rows, 0:w]).then_inc(acc_read, 1)
                act.wait_ge(acc_read, acc_base(n) + m + 1)
                cols = slice(tile_source(n)[1], tile_source(n)[1] + w)
                dst = z_p[m * P:(m + 1) * P, cols] if m < MT else z_s[:, cols]
                act.dma_start(dst, z_tile[0:rows, m, 0:w]).then_inc(z_stored[m], 16)

        def acc_ready_base(n):
            if isinstance(n, int) and n < N_A0:
                return (NU_MEM - 1) * n
            return MT * n - (MT + 1 - NU_MEM) * N_A0

        def tile_loop(eng, n0, n1, body):
            body(n0)
            if n1 - n0 > 2:
                with eng.Fori(n0 + 1, n1) as n:
                    body(n)
            elif n1 - n0 == 2:
                body(n0 + 1)

        def scalar_tile(act, n, kind, steps=NO_STEPS):
            for c in range(1, CH + 1):
                if c < CH:
                    scalar_hi(act, n, c, width(n))
                elif not (isinstance(n, int) and n == N_END - 1):
                    scalar_hi(act, n + 1, 0, REST if isinstance(n, int) and n + 1 == N_REST else TN)
                next(steps[1], None)
                next(steps[0], None)
                next(steps[0], None)
            scalar_evacuate(act, n, kind)

        def gpsimd_tile(pool, n, steps=iter(())):
            for c in range(CH):
                gpsimd_lo(pool, n, c, width(n))
                next(steps, None)

        def place(off, shape, rows=P):
            n = 1
            for s in shape:
                n *= s
            assert off + n <= AR_N
            v = arena[0:rows, off:off + n]
            if len(shape) == 1:
                return v
            names = "abcd"[:len(shape)]
            return v.rearrange(f"p ({' '.join(names)}) -> p {' '.join(names)}", **dict(zip(names, shape)))

        ZW = W_IN - C_IF
        zo = lambda c: c - C_IF
        IK_OFF = 0
        idx_pages = place(IK_OFF, [NB * NPG, ID])
        ZA_OFF = NB * NPG * ID
        z_a = place(ZA_OFF, [ZW], R)
        W_OFF = ZA_OFF + ZW
        z_low = place(W_OFF, [ZW], R)
        aq_low = place(ZA_OFF - (C_IQ - C_AQ), [C_IQ - C_AQ], R)
        score = place(W_OFF, [PAST + NQ], R)
        X_OFF = W_OFF + ZW
        ik_t = place(X_OFF, [2, TN], ID)
        relu_sc = place(X_OFF + 1024, [2, TN], IH * NQ)
        w_pick = place(X_OFF + 2048, [NB, R], IH * NQ)
        pick = place(X_OFF + 2304, [NB, R], IH * NQ)
        iq_t = place(X_OFF + 2560, [NB, IH, NQ], ID)
        ik_new = place(X_OFF + 3072, [R], ID)
        w_rows = place(X_OFF + 3104, [NB], IH * NQ)
        rope_tmp = [place(X_OFF + 3112 + 128 * i, [128]) for i in range(4)]
        XS_OFF = X_OFF + 3112 + 512
        sel_idx = place(XS_OFF, [KSEL_S], R).bitcast(U32)
        sel_f = place(XS_OFF + 256, [KSEL_S], R)
        phys_f = place(XS_OFF + 512, [KSEL_S], R)
        ZS_END = XS_OFF + 768
        keep = sb("keep", [P, 1056])
        rope_tab = keep[:, 0:240].rearrange("p (m c) -> p m c", m=MT + 1)
        fut = keep[:, 240:368]
        fut_s = keep[0:R, 368:372]
        top8 = keep[0:R, 372:380]
        phys_u = keep[:, 384:448].bitcast(U32).rearrange("p (c r) -> p c r", c=2)
        pages_i = keep[0:R, 448:464].bitcast(I32)
        pages_f = keep[0:R, 464:480]
        page_step = keep[0:R, 480:496]
        new_pen = keep[0:R, 496:500]
        page_list = keep[0:1, 512:640].bitcast(I32)
        pen_q = keep[:, 640:900]
        soft = keep[:, 900:912]
        gate_s = keep[:, 912:1040]

        pages_in, tables_in, idx_loaded = sem("pages_in"), sem("tables_in"), sem("idx_loaded")
        za_in, za_stored, wrows_in = sem("za_in"), sem("za_stored"), sem("wrows_in")

        (idx_turned, ikt_copied, scored, relu_done, weighted, score_copied) = (
            sem(n) for n in ("idx_turned", "ikt_copied", "scored", "relu_done", "weighted", "score_copied"))
        n_idx_units = NB * (PAST // TN)
        PPC = TN // PG

        def sync_tables(sp):
            for m in range(MT):
                sp.dma_start(rope_tab[:, m, :], C["rope"][m * P:(m + 1) * P, :]).then_inc(tables_in, 16)
            sp.dma_start(rope_tab[0:R, MT, :], C["rope"][S:S + R, :]).then_inc(tables_in, 16)
            sp.dma_start(fut, C["future"]).then_inc(tables_in, 16)
            sp.dma_start(fut_s, C["future_s"]).then_inc(tables_in, 16)
            sp.dma_start(pages_i, I["page_table"].unsqueeze(1).broadcast_to([NB, NQ, NPG])).then_inc(tables_in, 16)
            sp.dma_start(page_list, I["page_table"].rearrange("(o b) n -> o (b n)", o=1)).then_inc(pages_in, 16)
        N_TABLES = MT + 4

        def sync_idx_pages(sp, i0, n):
            with sp.Fori(0, n) as j:
                page = sp.value_load(page_list[:, bass.ds(i0 + j, 1)], min_val=0, max_val=NPOOL - 1)
                sp.dma_start(arena[:, bass.ds(IK_OFF + (i0 + j) * ID, ID)],
                             I["cache_idx_k"][0, bass.ds(page, 1), :, :].rearrange("o t d -> (o t) d")
                             ).then_inc(idx_loaded, 16)

        def sync_index_in(sp):
            sp.wait_ge(z_stored[MT], 16 * IXT)
            sp.dma_start(z_a[:, zo(C_IQ):zo(C_CQ)], z_s[0:R, C_IQ:C_CQ]).then_inc(za_in, 16)
            sp.dma_start(z_low[:, 0:C_CQ - C_IQ], z_s[R:2 * R, C_IQ:C_CQ]).then_inc(za_in, 16)
            sp.dma_start(pick, C["pick"].rearrange("p (b r) -> p b r", b=NB)).then_inc(za_in, 16)
            sp.wait_ge(*at("idx_ready"))
            for dst, c, w in ((O["s_idx_k"].rearrange("o b t d -> (o b t) d"), C_IK, ID), (iw_s, C_IW, IH)):
                sp.dma_start(dst, z_a[:, zo(c):zo(c) + w]).then_inc(za_stored, 16)
            sp.wait_ge(za_stored, 16 * 2)
            wr = iw_s.rearrange("(b q) h -> h q b", q=NQ)
            for h in range(IH):
                sp.dma_start(w_rows[h * NQ:(h + 1) * NQ, :], wr[h], allow_slow_non_contiguous=True).then_inc(wrows_in, 16)

        def sync_sample_in(sp):
            sp.wait_ge(z_stored[MT], 16 * (N_B0 - N_A0))
            sp.wait_ge(idx_turned, n_idx_units)
            sp.dma_start(z_a[:, zo(C_AQ):zo(C_IQ)], z_s[0:R, C_AQ:C_IQ]).then_inc(za_in, 16)
            sp.dma_start(aq_low, z_s[R:2 * R, C_AQ:C_IQ]).then_inc(za_in, 16)
            sp.wait_ge(*at("gate_in"))
            for dst, c, w in ((O["s_attn_k"].rearrange("o b t h d -> (o b t) (h d)"), C_AK, AW),
                              (O["s_attn_v"].rearrange("o b t h d -> (o b t) (h d)"), C_AV, AW),
                              (q_s, C_AQ, AW), (k_s, C_AK, AW), (v_s, C_AV, AW)):
                sp.dma_start(dst, z_a[:, zo(c):zo(c) + w]).then_inc(za_stored, 16)
            sp.wait_ge(za_stored, 16 * 7)

        def rotate(rows, cols_ap, heads, width_, tab, half):
            x = cols_ap.rearrange("p (h d) -> p h d", h=heads)
            x1, x2 = x[:, :, 0:half], x[:, :, half:2 * half]
            t = [r[0:rows, 0:heads * half].rearrange("p (h d) -> p h d", h=heads) for r in rope_tmp]
            base = 0 if half == 16 else 32
            cos = tab[:, base:base + half].unsqueeze(1).broadcast_to([rows, heads, half])
            sin = tab[:, base + half:base + 2 * half].unsqueeze(1).broadcast_to([rows, heads, half])
            nc.vector.tensor_tensor(out=t[0], in0=x1, in1=cos, op=ALU.mult)
            nc.vector.tensor_tensor(out=t[1], in0=x2, in1=sin, op=ALU.mult)
            nc.vector.tensor_tensor(out=t[2], in0=x1, in1=sin, op=ALU.mult)
            dlink(nc.vector.tensor_tensor(out=t[3], in0=x2, in1=cos, op=ALU.mult))
            nc.vector.tensor_tensor(out=x1, in0=t[0], in1=t[1], op=ALU.subtract)
            return nc.vector.tensor_tensor(out=x2, in0=t[2], in1=t[3], op=ALU.add)

        def vector_index_prep(dve):
            dve.wait_ge(za_in, 48)
            dve.wait_ge(tables_in, 16 * N_TABLES)
            part = z_a[:, zo(C_IQ):zo(C_CQ)]
            dlink(nc.vector.tensor_tensor(out=part, in0=part, in1=z_low[:, 0:C_CQ - C_IQ], op=ALU.add))
            tab = rope_tab[0:R, MT, :]
            dlink(rotate(R, z_a[:, zo(C_IQ):zo(C_IQ) + IH * ID], IH, ID, tab, ID // 8))
            rotate(R, z_a[:, zo(C_IK):zo(C_IK) + ID], 1, ID, tab, ID // 8).then_inc(reached("idx_ready"), 1)
            dve.wait_ge(wrows_in, 16 * IH)
            nc.vector.scalar_tensor_tensor(out=w_pick, in0=pick, scalar=float(ID ** -0.5 * IH ** -0.5),
                                           in1=w_rows.unsqueeze(2).broadcast_to([IH * NQ, NB, R]),
                                           op0=ALU.mult, op1=ALU.mult).then_inc(reached("pick_ready"), 1)

        def vector_sample_prep(dve):
            dve.wait_ge(za_in, 16 * 5)
            part = z_a[:, zo(C_AQ):zo(C_IQ)]
            dlink(nc.vector.tensor_tensor(out=part, in0=part, in1=aq_low, op=ALU.add))
            tab = rope_tab[0:R, MT, :]
            dlink(rotate(R, z_a[:, zo(C_AQ):zo(C_AQ) + AW], H, AD, tab, AD // 8))
            rotate(R, z_a[:, zo(C_AK):zo(C_AK) + AW], H, AD, tab, AD // 8).then_inc(reached("za_ready"), 1)
            for h in range(H):
                c = zo(C_AG) + h * AD
                last = nc.vector.tensor_copy(gate_s[h * R:(h + 1) * R, :], z_a[:, c:c + AD])
            last.then_inc(reached("gate_in"), 1)

        def tensor_sample_turn(pe):
            pe.wait_ge(*at("idx_ready"))
            for h in range(IH):
                c = zo(C_IQ) + h * ID
                nc.tensor.transpose(ps_a[0:ID, h * R:(h + 1) * R], z_a[:, c:c + ID], ident[0:R, 0:R])
            nc.tensor.transpose(ps_b[0:ID, 0:R], z_a[:, zo(C_IK):zo(C_IK) + ID], ident[0:R, 0:R]).then_inc(reached("new_turned"), 1)
            yield

        def scalar_sample_turn(act):
            act.wait_ge(*at("new_turned"))
            nc.scalar.copy(iq_t, ps_a[0:ID, :].rearrange("p (h b q) -> p b h q", h=IH, b=NB))
            nc.scalar.copy(ik_new, ps_b[0:ID, 0:R]).then_inc(reached("new_copied"), 1)
            yield

        def tensor_indexer(pe):
            pe.wait_ge(*at("new_copied"))
            pe.wait_ge(*at("pick_ready"))
            pe.wait_ge(idx_loaded, 16 * NB * NPG)
            n = n_idx_units

            def turn(u):
                c, b = u // NB, u % NB
                if u:
                    pe.wait_ge(ikt_copied, u)
                for j in range(PPC):
                    last = nc.tensor.transpose(ps_a[0:ID, j * PG:(j + 1) * PG],
                                               idx_pages[:, b * NPG + c * PPC + j, :], ident[:, :])
                last.then_inc(idx_turned, 1)

            def score_of(u):
                b = u % NB
                pe.wait_ge(ikt_copied, u + 1)
                if u:
                    pe.wait_ge(relu_done, u)
                nc.tensor.matmul(ps_b[0:IH * NQ, :], iq_t[:, b, :, :].rearrange("p h q -> p (h q)"), ik_t[:, u % 2, :],
                                 start=True, stop=True).then_inc(scored, 1)

            def weigh(u):
                c, b = u // NB, u % NB
                pe.wait_ge(relu_done, u + 1)
                if b == 0 and c:
                    pe.wait_ge(score_copied, c)
                nc.tensor.matmul(ps_c[0:R, :], w_pick[:, b, :], relu_sc[:, u % 2, :],
                                 start=b == 0, stop=b == NB - 1).then_inc(weighted, 1)

            turn(0)
            for u in range(n + 1):
                if u + 1 < n:
                    turn(u + 1)
                if u < n:
                    score_of(u)
                if u:
                    weigh(u - 1)
                yield
            pe.wait_ge(relu_done, n)
            for b in range(NB):
                last = nc.tensor.matmul(ps_b[0:IH * NQ, b * NQ:(b + 1) * NQ], iq_t[:, b, :, :].rearrange("p h q -> p (h q)"),
                                        ik_new[:, b * NQ:(b + 1) * NQ], start=True, stop=True)
            last.then_inc(scored, 1)
            pe.wait_ge(relu_done, n + 1)
            pe.wait_ge(score_copied, n // NB)
            for b in range(NB):
                last = nc.tensor.matmul(ps_c[0:R, 0:NQ], w_pick[:, b, :], relu_sc[:, n % 2, b * NQ:(b + 1) * NQ],
                                        start=b == 0, stop=b == NB - 1)
            last.then_inc(weighted, 1)
            yield

        def scalar_indexer(act):
            n = n_idx_units

            def copy_keys(u):
                act.wait_ge(idx_turned, u + 1)
                if u >= 2:
                    act.wait_ge(scored, u - 1)
                nc.scalar.copy(ik_t[:, u % 2, :], ps_a[0:ID, :]).then_inc(ikt_copied, 1)

            def relu(u, w):
                act.wait_ge(scored, u + 1)
                if u >= 2:
                    act.wait_ge(weighted, u - 1)
                nc.scalar.activation(relu_sc[:, u % 2, 0:w], ps_b[0:IH * NQ, 0:w], ACT.Relu).then_inc(relu_done, 1)

            copy_keys(0)
            for u in range(n):
                if u + 1 < n:
                    copy_keys(u + 1)
                relu(u, TN)
                yield
            yield
            relu(n, R)
            yield

        def vector_scores(dve):
            for c in range(n_idx_units // NB):
                dve.wait_ge(weighted, NB * (c + 1))
                nc.vector.tensor_copy(score[:, c * TN:(c + 1) * TN], ps_c[0:R, :]).then_inc(score_copied, 1)
            dve.wait_ge(weighted, n_idx_units + 1)
            dlink(nc.vector.tensor_tensor(out=score[:, PAST:PAST + NQ], in0=ps_c[0:R, 0:NQ], in1=fut_s, op=ALU.add))

        def vector_topk_sample(dve, i0, i1):
            for i in range(i0, i1):
                dlink(nc.vector.max(top8, score))
                dlink(nc.vector.max_index(sel_idx[:, 8 * i:8 * i + 8], top8, score))
                dlink(nc.vector.match_replace(score, top8, score, TAKEN))

        def vector_physical(dve):
            dlink(nc.vector.tensor_copy(sel_f, sel_idx))
            dlink(nc.vector.tensor_copy(pages_f, pages_i))
            nc.vector.tensor_scalar(pen_q[0:R, 0:KSEL_S], sel_f, float(PAST), NEG, ALU.is_ge, ALU.mult)
            nc.vector.tensor_scalar(pen_q[0:R, KSEL_S:KSEL_S + NQ], score[:, PAST:PAST + NQ], TAKEN, NEG,
                                    ALU.not_equal, ALU.mult)
            dlink(nc.vector.tensor_scalar(sel_f, sel_f, float(PAST - 1), None, ALU.min))
            dlink(nc.vector.tensor_tensor(out=page_step[:, 1:NPG], in0=pages_f[:, 1:NPG], in1=pages_f[:, 0:NPG - 1],
                                          op=ALU.subtract))
            dlink(nc.vector.tensor_scalar(page_step[:, 1:NPG], page_step[:, 1:NPG], -1.0, float(PG), ALU.add, ALU.mult))
            dlink(nc.vector.tensor_scalar(page_step[:, 0:1], pages_f[:, 0:1], float(PG), None, ALU.mult))
            dlink(nc.vector.tensor_scalar(phys_f, sel_f, page_step[:, 0:1], None, ALU.add))
            for h in range(1, H):
                nc.vector.tensor_copy(pen_q[h * R:(h + 1) * R, :], pen_q[0:R, :])
            for j in range(1, NPG):
                dlink(nc.vector.tensor_scalar(sel_term, sel_f, float(PG * j), page_step[:, j:j + 1], ALU.is_ge, ALU.mult))
                add = nc.vector.tensor_tensor(out=phys_f, in0=phys_f, in1=sel_term, op=ALU.add)
                if j < NPG - 1:
                    dlink(add)
            add.then_inc(reached("phys_ready"), 1)
            yield
            dve.wait_ge(*at("phys_turned"))
            nc.vector.tensor_copy(phys_u, ps_c[:, PC_O:PC_O + 2 * R].rearrange("p (c r) -> p c r", c=2)).then_inc(reached("phys_u_ready"), 1)
            yield

        sel_term = place(W_OFF + PAST + NQ, [KSEL_S], R)

        def tensor_physical(pe):
            pe.wait_ge(*at("phys_ready"))
            prompt_sums_read(pe)
            for c in range(2):
                last = nc.tensor.transpose(ps_c[:, PC_O + c * R:PC_O + (c + 1) * R], phys_f[:, c * P:(c + 1) * P], ident[0:R, 0:R])
            last.then_inc(reached("phys_turned"), 1)
            pe.wait_ge(*at("phys_u_ready"))
            yield

        GS = 2
        SC = KSEL_S // P
        got = place(W_OFF, [GS, SC, AW])
        ot = place(W_OFF, [P])
        G0 = W_OFF + GS * SC * AW
        g_sc = place(G0, [SC, H, R])
        probs_t = place(G0, [SC, H, R])
        q_bc = place(G0 + 256, [GS, AW])
        nt = place(G0 + 256, [NQ, AD])
        lg = place(G0 + 256 + AW, [KSEL_S + NQ])
        kn = place(G0 + 256 + GS * AW, [NQ, AD])
        qn = place(G0 + 768 + GS * AW, [AD])
        o_s = place(G0 + 896 + GS * AW, [AD])
        assert G0 + 1024 + GS * AW <= X_OFF
        pr = place(XS_OFF, [KSEL_S + NQ])
        vn = place(XS_OFF + KSEL_S + NQ + 4, [NQ, AD])
        PC_T, PC_O = P, 3 * P
        got_in = [sem(f"got_in{i}") for i in range(GS)]
        qbc_in = [sem(f"qbc_in{i}") for i in range(GS)]
        (row_scored, new_in, probs_s) = (
            sem(n) for n in ("row_scored", "new_in", "probs_s"))
        (row_summed, mix_stored) = (
            sem(n) for n in ("row_summed", "mix_stored"))
        k_rows = I["cache_attn_k"].rearrange("o n t h d -> (o n t) (h d)")
        v_rows = I["cache_attn_v"].rearrange("o n t h d -> (o n t) (h d)")

        def gpsimd_gather(pool, r, values):
            s = r % GS
            if not values and r == 0:
                pool.wait_ge(*at("phys_u_ready"))
            if values and r == 0:
                pool.wait_ge(row_scored, R)
            if r >= GS:
                pool.wait_ge(row_summed if values else row_scored, r - GS + 1)
            if not values:
                pool.dma_start(q_bc[:, s, :], q_s[r:r + 1, :].broadcast_to([P, AW])).then_inc(qbc_in[s], 16)
            for c in range(SC):
                pool.indirect_dma_start(out=got[:, s, c, :], out_offset=None, in_=v_rows if values else k_rows,
                                        in_offset=bass.IndirectOffsetOnAxis(ap=phys_u[:, c, r:r + 1], axis=0)
                                        ).then_inc(got_in[s], 16)

        def got_count(r, values):
            return 16 * SC * (r // GS + 1 + (R // GS if values else 0))

        def sync_new_keys(sp):
            sp.wait_ge(*at("phys_u_ready"))
            for h in range(H):
                for dst, src in ((kn, k_s), (vn, v_s)):
                    for b in range(NB):
                        v = src[b * NQ:(b + 1) * NQ, h * AD:(h + 1) * AD].unsqueeze(0)
                        sp.dma_start(dst[h * R + b * NQ:h * R + (b + 1) * NQ, :, :],
                                     v.broadcast_to([NQ, NQ, AD])).then_inc(new_in, 16)
                sp.dma_start(qn[h * R:(h + 1) * R, :], q_s[:, h * AD:(h + 1) * AD]).then_inc(new_in, 16)

        def vector_row_scores(dve, r):
            s = r % GS
            dve.wait_ge(got_in[s], got_count(r, False))
            dve.wait_ge(qbc_in[s], 16 * (r // GS + 1))
            dlink(nc.vector.tensor_tensor(out=got[:, s, :, :], in0=got[:, s, :, :],
                                          in1=q_bc[:, s, :].unsqueeze(1).broadcast_to([P, SC, AW]), op=ALU.mult))
            nc.vector.tensor_reduce(out=g_sc[:, :, :, r], in_=got[:, s, :, :].rearrange("p c (h d) -> p c h d", h=H),
                                    axis=AX.X, op=ALU.add).then_inc(row_scored, 1)

        def vector_gather(dve):
            for r in range(R):
                vector_row_scores(dve, r)
                yield
            dve.wait_ge(new_in, 16 * H * (2 * NB + 1))
            dlink(nc.vector.tensor_tensor(out=nt, in0=kn, in1=qn.unsqueeze(1).broadcast_to([P, NQ, AD]), op=ALU.mult))
            dlink(nc.vector.tensor_reduce(out=lg[:, KSEL_S:KSEL_S + NQ], in_=nt, axis=AX.X, op=ALU.add))
            nc.vector.scalar_tensor_tensor(out=lg[:, KSEL_S:KSEL_S + NQ], in0=lg[:, KSEL_S:KSEL_S + NQ],
                                           scalar=AD ** -0.5, in1=pen_q[:, KSEL_S:KSEL_S + NQ], op0=ALU.mult, op1=ALU.add)
            dve.wait_ge(*at("sc_turned"))
            dlink(nc.vector.scalar_tensor_tensor(out=lg[:, 0:KSEL_S], in0=ps_c[:, PC_T:PC_T + KSEL_S], scalar=AD ** -0.5,
                                                 in1=pen_q[:, 0:KSEL_S], op0=ALU.mult, op1=ALU.add))
            dlink(nc.vector.tensor_reduce(out=soft[:, 0:1], in_=lg, axis=AX.X, op=ALU.max))
            nc.vector.tensor_scalar(soft[:, 1:2], soft[:, 0:1], -1.0, None, ALU.mult).then_inc(reached("max_s"), 1)
            yield
            yield
            dve.wait_ge(*at("exp_s"))
            dlink(nc.vector.reciprocal(soft[:, 3:4], soft[:, 2:3]))
            dve.wait_ge(*at("probs_turned"))
            nc.vector.tensor_copy(probs_t.rearrange("p c h r -> p (c h r)"), ps_c[:, PC_T:PC_T + KSEL_S]
                                  ).then_inc(reached("probs_copied"), 1)
            yield

        def tensor_gather(pe):
            yield from hosted_pause(1 + R)
            pe.wait_ge(row_scored, R)
            prompt_sums_read(pe)
            for c in range(SC):
                last = nc.tensor.transpose(ps_c[:, PC_T + c * P:PC_T + (c + 1) * P],
                                           g_sc[:, c, :, :].rearrange("p h r -> p (h r)"), ident[:, :])
            last.then_inc(reached("sc_turned"), 1)
            pe.wait_ge(*at("max_s"))
            yield
            yield
            pe.wait_ge(*at("exp_s"))
            prompt_sums_read(pe)
            for c in range(SC):
                last = nc.tensor.transpose(ps_c[:, PC_T + c * P:PC_T + (c + 1) * P], pr[:, c * P:(c + 1) * P], ident[:, :])
            last.then_inc(reached("probs_turned"), 1)
            pe.wait_ge(*at("probs_copied"))
            yield
            for r in range(R):
                tensor_row_sum(pe, r)
                yield

        def scalar_gather(act):
            yield from hosted_pause(CK0)
            act.wait_ge(*at("gate_in"))
            nc.scalar.activation(gate_s, gate_s, ACT.Silu).then_inc(reached("gate_ready"), 1)
            yield from hosted_pause(R + 1)
            act.wait_ge(*at("max_s"))
            nc.scalar.activation(pr, lg, ACT.Exp, bias=soft[:, 1:2], accum_out=soft[:, 2:3]).then_inc(reached("exp_s"), 1)
            yield

        def gpsimd_gathers(pool):
            yield from hosted_pause(CK0)
            for r in range(R):
                gpsimd_gather(pool, r, False)
                yield
            yield from hosted_pause(2)
            for r in range(R):
                gpsimd_gather(pool, r, True)
                yield

        def prompt_sums_read(pe):
            if counts["pv"]:
                pe.wait_ge(o_read, counts["pv"])

        counts = {"norm": 0, "sqrt": 0, "pv": 0}

        def tensor_row_sum(pe, r):
            s = r % GS
            if r == 0:
                pe.wait_ge(*at("probs_copied"))
            pe.wait_ge(got_in[s], got_count(r, True))
            prompt_sums_read(pe)
            for h in range(H):
                for c in range(SC):
                    last = nc.tensor.matmul(ps_c[:, PC_O + h * R + r:PC_O + h * R + r + 1],
                                            got[:, s, c, h * AD:(h + 1) * AD], probs_t[:, c, h, r:r + 1],
                                            start=c == 0, stop=c == SC - 1)
            last.then_inc(row_summed, 1)

        def tensor_gather_out(pe):
            pe.wait_ge(*at("ot_copied"))
            nc.tensor.transpose(ps_c[:, PC_T:PC_T + P], ot, ident[:, :]).then_inc(reached("o_turned"), 1)

        def vector_gather_out(dve):
            dve.wait_ge(row_summed, R)
            nc.vector.tensor_copy(ot, ps_c[:, PC_O:PC_O + P]).then_inc(reached("ot_copied"), 1)
            dve.wait_ge(*at("o_turned"))
            dlink(nc.vector.tensor_copy(o_s, ps_c[:, PC_T:PC_T + P]))
            for j in range(NQ):
                dlink(nc.vector.scalar_tensor_tensor(out=o_s, in0=vn[:, j, :], scalar=pr[:, KSEL_S + j:KSEL_S + j + 1],
                                                     in1=o_s, op0=ALU.mult, op1=ALU.add))
            dve.wait_ge(*at("gate_ready"))
            nc.vector.scalar_tensor_tensor(out=o_s, in0=o_s, scalar=soft[:, 3:4], in1=gate_s,
                                           op0=ALU.mult, op1=ALU.mult).then_inc(reached("mixed_s"), 1)

        def store_mix_s(eng, o, col):
            for h in range(H):
                eng.dma_start(mix_s[:, col + h * AD:col + (h + 1) * AD], o[h * R:(h + 1) * R, :]).then_inc(mix_stored, 16)

        k_t = place(0, [H, S])
        v_p = place(2048, [MT, AW])
        ikt_p = place(4096, [S])
        mk_t = place(4608, [H, NMEM])
        ZP = W_IN - C_AQ
        z_t = place(5632, [ZP])
        q_t = place(5632 + ZP, [H, P])
        iqt_p = place(5632 + ZP + 512, [IH // 2, P])
        cq_t = place(5632 + ZP + 1536, [H, P])
        lg_p = place(5632 + ZP + 2048, [S])
        assert 5632 + ZP + 2560 <= W_OFF
        sc_p = place(X_OFF, [S])
        relu_p = place(X_OFF + 512, [2, S])
        pr_p = place(X_OFF + 1536, [S])
        pt_p = place(X_OFF + 2048, [MT, P])
        o_p = place(X_OFF + 2560, [AW])
        ik_pair = place(X_OFF + 2560, [2, ID])
        keep_p = sb("keep_p", [P, 40])
        top8_p = keep_p[:, 0:8]
        st_p = keep_p[:, 24:40].rearrange("p (s c) -> p s c", s=4)
        iw_p = keep_p[:, 8:24]
        zq = lambda c: c - C_AQ

        (zt_in, rotated_p, kv_stored, turned_p, turned_copied, mem_turned, mem_copied, gates_p,
            v_kept, pairs_ready) = (
            sem(n) for n in ("zt_in", "rotated_p", "kv_stored", "turned_p", "turned_copied", "mem_turned",
            "mem_copied", "gates_p", "v_kept", "pairs_ready"))
        (ix_scored, ix_relu, ix_added, pen_ready, qk_done, lg_read, mx_ready, exp_done,
            pt_turned, pt_copied, pv_done, o_read, o_stored) = (
            sem(n) for n in ("ix_scored", "ix_relu", "ix_added", "pen_ready", "qk_done", "lg_read", "mx_ready",
            "exp_done", "pt_turned", "pt_copied", "pv_done", "o_read", "o_stored"))
        JT = 2 * H
        PREP_PIECES, TOPK_PIECES = 5, 16
        TURNS = 5

        def sync_prompt_in(sp, m):
            if m:
                sp.wait_ge(o_read, JT * m)
                sp.wait_ge(kv_stored, 48 * m)
            else:
                for i in range(MT + 1):
                    sp.wait_ge(z_stored[i], 16 * (N_B0 - N_A0))
                sp.wait_ge(weighted, n_idx_units + 1)
                sp.wait_ge(za_stored, 16 * 7)
                sp.wait_ge(*at("gate_in"))
            sp.dma_start(z_t, z_p[m * P:(m + 1) * P, C_AQ:W_IN]).then_inc(zt_in, 16)

        def sync_prompt_kv(sp, m):
            sp.wait_ge(rotated_p, m + 1)
            rows = slice(m * P, (m + 1) * P)
            sp.dma_start(O["p_attn_k"].rearrange("l b s h d -> (l b s) (h d)")[rows, :],
                         z_t[:, zq(C_AK):zq(C_AK) + AW]).then_inc(kv_stored, 16)
            sp.dma_start(O["p_attn_v"].rearrange("l b s h d -> (l b s) (h d)")[rows, :],
                         z_t[:, zq(C_AV):zq(C_AV) + AW]).then_inc(kv_stored, 16)
            sp.dma_start(O["p_idx_k"].rearrange("l b s d -> (l b s) d")[rows, :],
                         z_t[:, zq(C_IK):zq(C_IK) + ID]).then_inc(kv_stored, 16)

        def vector_prompt_prep(dve, m):
            yield
            dve.wait_ge(zt_in, 16 * (m + 1))
            if m:
                dve.wait_ge(o_stored, 16 * 2 * m)
            tab = rope_tab[:, m, :]
            dlink(rotate(P, z_t[:, zq(C_AQ):zq(C_AQ) + AW], H, AD, tab, AD // 8))
            yield
            dlink(rotate(P, z_t[:, zq(C_AK):zq(C_AK) + AW], H, AD, tab, AD // 8))
            yield
            dlink(rotate(P, z_t[:, zq(C_IQ):zq(C_IQ) + IH * ID], IH, ID, tab, ID // 8))
            yield
            rotate(P, z_t[:, zq(C_IK):zq(C_IK) + ID], 1, ID, tab, ID // 8).then_inc(rotated_p, 1)
            dve.wait_ge(rotated_p, m + 1)
            nc.vector.tensor_scalar(iw_p, z_t[:, zq(C_IW):zq(C_IW) + IH], float(ID ** -0.5 * IH ** -0.5), None, ALU.mult)
            nc.vector.tensor_copy(ik_pair, z_t[:, zq(C_IK):zq(C_IK) + ID].unsqueeze(1).broadcast_to([P, 2, ID])
                                  ).then_inc(pairs_ready, 1)
            yield
            yield from hosted_pause(4 if m == 0 else 3)

        def tensor_prompt_turn(pe, m):
            yield from hosted_pause(PREP_PIECES)
            if m == 0:
                for b in range(2):
                    for i in range(4):
                        h, t = 2 * b + i // 2, i % 2
                        last = nc.tensor.transpose((ps_a, ps_b)[b][:, i * P:(i + 1) * P],
                                                   mem_kv[:, t, h * AD:(h + 1) * AD], ident[:, :])
                    last.then_inc(mem_turned, 1)
                yield
                pe.wait_ge(mem_copied, 2)
            else:
                pe.wait_ge(o_read, JT * m)
            pe.wait_ge(pairs_ready, m + 1)
            groups = [[(zq(C_AQ) + h * AD) for h in range(H)], [(zq(C_AK) + h * AD) for h in range(H)],
                      [(zq(C_IQ) + h * P) for h in range(4)], [(zq(C_IQ) + h * P) for h in range(4, 8)],
                      [(zq(C_CQ) + h * AD) for h in range(H)]]
            for g, cols in enumerate(groups):
                if g >= 2:
                    pe.wait_ge(turned_copied, (TURNS + 1) * m + g - 1)
                bank = (ps_a, ps_b)[g % 2]
                for i, c in enumerate(cols):
                    last = nc.tensor.transpose(bank[:, i * P:(i + 1) * P], z_t[:, c:c + P], ident[:, :])
                last.then_inc(turned_p, 1)
                if g % 2:
                    yield
            pe.wait_ge(turned_copied, (TURNS + 1) * m + 4)
            nc.tensor.transpose(ps_b[:, 0:P], ik_pair.rearrange("p a d -> p (a d)"), ident[:, :]).then_inc(turned_p, 1)
            yield

        def scalar_prompt_turn(act, m):
            yield from hosted_pause(PREP_PIECES)
            if m == 0:
                for b in range(2):
                    act.wait_ge(mem_turned, b + 1)
                    nc.scalar.copy(mk_t[:, 2 * b:2 * b + 2, :],
                                   (ps_a, ps_b)[b][:, :].rearrange("p (h m) -> p h m", h=2)).then_inc(mem_copied, 1)
                yield
            rows = slice(m * P, (m + 1) * P)
            dsts = [q_t, k_t[:, :, rows], iqt_p[:, 0:4, :], iqt_p[:, 4:8, :], cq_t]
            for g, dst in enumerate(dsts):
                act.wait_ge(turned_p, (TURNS + 1) * m + g + 1)
                nc.scalar.copy(dst, (ps_a, ps_b)[g % 2][:, :].rearrange("p (h m) -> p h m", h=4)).then_inc(turned_copied, 1)
                if g % 2:
                    yield
            act.wait_ge(turned_p, (TURNS + 1) * (m + 1))
            nc.scalar.copy(ikt_p[:, rows], ps_b[:, 0:P]).then_inc(turned_copied, 1)
            nc.scalar.copy(v_p[:, m, :], z_t[:, zq(C_AV):zq(C_AV) + AW]).then_inc(v_kept, 1)
            nc.scalar.activation(z_t[:, zq(C_AG):zq(C_AG) + AW], z_t[:, zq(C_AG):zq(C_AG) + AW], ACT.Silu).then_inc(gates_p, 1)
            nc.scalar.activation(z_t[:, zq(C_CG):zq(C_CG) + AW], z_t[:, zq(C_CG):zq(C_CG) + AW], ACT.Silu).then_inc(gates_p, 1)
            yield

        def tensor_prompt_index(pe, m):
            nk = P * (m + 1)
            pe.wait_ge(turned_copied, (TURNS + 1) * (m + 1))
            for h in range(IH):
                g = IH * (m - 1) + h
                if g >= 2:
                    pe.wait_ge(ix_relu, g - 1)
                half = slice((h % 2) * ID, (h % 2 + 1) * ID)
                nc.tensor.matmul((ps_a, ps_b)[h % 2][:, 0:nk], iqt_p[half, h // 2, :], ikt_p[half, 0:nk],
                                 start=True, stop=True).then_inc(ix_scored, 1)
                if h % 2:
                    yield
            yield from hosted_pause(TOPK_PIECES)

        def scalar_prompt_index(act, m):
            nk = P * (m + 1)
            for h in range(IH):
                g = IH * (m - 1) + h
                act.wait_ge(ix_scored, g + 1)
                if g >= 2:
                    act.wait_ge(ix_added, g - 1)
                nc.scalar.activation(relu_p[:, h % 2, 0:nk], (ps_a, ps_b)[h % 2][:, 0:nk], ACT.Relu).then_inc(ix_relu, 1)
                if h % 2:
                    yield
            yield from hosted_pause(TOPK_PIECES)

        def vector_prompt_select(dve, m):
            nk = P * (m + 1)
            if m == 0:
                nc.vector.tensor_copy(sc_p[:, 0:P], fut).then_inc(pen_ready, 1)
                dve.wait_ge(pen_ready, 1)
                return
            for h in range(IH):
                g = IH * (m - 1) + h
                dve.wait_ge(ix_relu, g + 1)
                if h == 0:
                    add = nc.vector.tensor_scalar(sc_p[:, 0:nk], relu_p[:, 0, 0:nk], iw_p[:, 0:1], None, ALU.mult)
                else:
                    add = nc.vector.scalar_tensor_tensor(out=sc_p[:, 0:nk], in0=relu_p[:, h % 2, 0:nk],
                                                         scalar=iw_p[:, h:h + 1], in1=sc_p[:, 0:nk],
                                                         op0=ALU.mult, op1=ALU.add)
                add.then_inc(ix_added, 1)
                dve.wait_ge(ix_added, g + 1)
                if h % 2:
                    yield
            dlink(nc.vector.tensor_tensor(out=sc_p[:, nk - P:nk], in0=sc_p[:, nk - P:nk], in1=fut, op=ALU.add))
            rounds = KSEL_P // 8
            for i in range(rounds):
                dlink(nc.vector.max(top8_p, sc_p[:, 0:nk]))
                dlink(nc.vector.match_replace(sc_p[:, 0:nk], top8_p, sc_p[:, 0:nk], TAKEN))
                if (i + 1) * TOPK_PIECES // rounds > i * TOPK_PIECES // rounds and i < rounds - 1:
                    yield
            nc.vector.tensor_scalar(sc_p[:, 0:nk], sc_p[:, 0:nk], TAKEN, NEG, ALU.not_equal, ALU.mult).then_inc(pen_ready, 1)
            dve.wait_ge(pen_ready, m + 1)
            yield

        def job(m, j):
            if j < H:
                return P * (m + 1), q_t[:, j, :], k_t[:, j, 0:P * (m + 1)], lambda i: v_p[:, i, j * AD:(j + 1) * AD]
            h = j - H
            return NMEM, cq_t[:, h, :], mk_t[:, h, :], lambda i: mem_kv[:, i, AW + h * AD:AW + (h + 1) * AD]

        def tensor_prompt_attend(pe, m):
            for s in range(JT + 3):
                if s < JT:
                    J = JT * m + s
                    nk, q, k, _ = job(m, s)
                    if s == 0:
                        pe.wait_ge(turned_copied, (TURNS + 1) * (m + 1))
                        pe.wait_ge(v_kept, m + 1)
                        if m:
                            pe.wait_ge(ix_relu, IH * m)
                    if J:
                        pe.wait_ge(lg_read, J)
                    nc.tensor.matmul(ps_a[:, 0:nk], q, k, start=True, stop=True).then_inc(qk_done, 1)
                if s >= 3:
                    J = JT * m + s - 3
                    nk, _, _, v = job(m, s - 3)
                    pe.wait_ge(pt_copied, J + 1)
                    if J:
                        pe.wait_ge(o_read, J)
                    for i in range(nk // P):
                        last = nc.tensor.matmul(ps_c[:, 0:AD], pt_p[:, i, :], v(i), start=i == 0, stop=i == nk // P - 1)
                    last.then_inc(pv_done, 1)
                    counts["pv"] = J + 1
                if 2 <= s < JT + 2:
                    J = JT * m + s - 2
                    nk = job(m, s - 2)[0]
                    pe.wait_ge(exp_done, J + 1)
                    if J:
                        pe.wait_ge(pt_copied, J)
                    for i in range(nk // P):
                        last = nc.tensor.transpose(ps_b[:, i * P:(i + 1) * P], pr_p[:, i * P:(i + 1) * P], ident[:, :])
                    last.then_inc(pt_turned, 1)
                yield

        def scalar_prompt_attend(act, m):
            for s in range(JT + 3):
                if 2 <= s < JT + 2:
                    J = JT * m + s - 2
                    nk = job(m, s - 2)[0]
                    act.wait_ge(pt_turned, J + 1)
                    if J:
                        act.wait_ge(pv_done, J)
                    nc.scalar.copy(pt_p[:, 0:nk // P, :], ps_b[:, 0:nk].rearrange("p (i t) -> p i t", t=P)).then_inc(pt_copied, 1)
                if 1 <= s < JT + 1:
                    J = JT * m + s - 1
                    nk = job(m, s - 1)[0]
                    act.wait_ge(mx_ready, J + 1)
                    if J:
                        act.wait_ge(pt_turned, J)
                    nc.scalar.activation(pr_p[:, 0:nk], lg_p[:, 0:nk], ACT.Exp, bias=st_p[:, J % 4, 1:2],
                                         accum_out=st_p[:, J % 4, 2:3]).then_inc(exp_done, 1)
                yield

        def vector_prompt_attend(dve, m):
            for s in range(JT + 3):
                if s >= 3:
                    j = s - 3
                    J = JT * m + j
                    if j == 0:
                        dve.wait_ge(gates_p, 2 * (m + 1))
                    if j % H == 0 and (m or j):
                        dve.wait_ge(o_stored, 16 * (2 * m + j // H))
                    dve.wait_ge(pv_done, J + 1)
                    dlink(nc.vector.reciprocal(st_p[:, J % 4, 3:4], st_p[:, J % 4, 2:3]))
                    g = zq(C_AG if j < H else C_CG) + (j % H) * AD
                    nc.vector.scalar_tensor_tensor(out=o_p[:, (j % H) * AD:(j % H + 1) * AD], in0=ps_c[:, 0:AD],
                                                   scalar=st_p[:, J % 4, 3:4], in1=z_t[:, g:g + AD],
                                                   op0=ALU.mult, op1=ALU.mult).then_inc(o_read, 1)
                if s < JT:
                    J = JT * m + s
                    nk = job(m, s)[0]
                    dve.wait_ge(qk_done, J + 1)
                    if J:
                        dve.wait_ge(exp_done, J)
                    scale = float(AD ** -0.5)
                    if s < H:
                        out = nc.vector.scalar_tensor_tensor(out=lg_p[:, 0:nk], in0=ps_a[:, 0:nk], scalar=scale,
                                                             in1=sc_p[:, 0:nk], op0=ALU.mult, op1=ALU.add)
                    else:
                        out = nc.vector.tensor_scalar(lg_p[:, 0:nk], ps_a[:, 0:nk], scale, None, ALU.mult)
                    out.then_inc(lg_read, 1)
                    dve.wait_ge(lg_read, J + 1)
                    dlink(nc.vector.tensor_reduce(out=st_p[:, J % 4, 0:1], in_=lg_p[:, 0:nk], axis=AX.X, op=ALU.max))
                    nc.vector.tensor_scalar(st_p[:, J % 4, 1:2], st_p[:, J % 4, 0:1], -1.0, None, ALU.mult).then_inc(mx_ready, 1)
                yield

        def sync_prompt_out(sp, m):
            for g in range(2):
                sp.wait_ge(o_read, JT * m + H * (g + 1))
                sp.dma_start(mix_p[m * P:(m + 1) * P, MW + g * AW:MW + (g + 1) * AW], o_p).then_inc(o_stored, 16)

        CQ = 0
        cq_in = place(CQ, [2, AW], R)
        cq_low = place(CQ + 1024, [2, AW], R)
        q_spread = place(CQ + 2048, [H * NB * (P + NQ)])
        k_mem = place(CQ + 2048 + 4224, [2, NMEM // P, AW])
        kt_mem = place(CQ + 2048 + 4224 + 2048, [2, H, NMEM])
        lg_c = place(CQ + 10368, [NMEM])
        pr_c = place(CQ + 10624, [NMEM])
        p_spread = [place(CQ + 10880 + i * 1056, [NB * (P + NQ)]) for i in range(2)]
        o_c = place(CQ + 12992, [AD])
        gate_c = place(CQ + 13120, [AD])
        (cq_loaded, km_turned, kt_ready, cv_done) = (
            sem(n) for n in ("cq_loaded", "km_turned", "kt_ready", "cv_done"))
        km_in = [sem("km_in0"), sem("km_in1")]

        def sync_mem_s(sp):
            sp.wait_ge(mix_stored, 16 * H)
            sp.wait_ge(o_stored, 16 * 2 * MT)
            sp.wait_ge(kv_stored, 48 * MT)
            sp.dma_start(cq_in, z_s[0:R, C_CQ:C_CQ + 2 * AW].rearrange("r (a c) -> r a c", a=2)).then_inc(cq_loaded, 16)
            sp.dma_start(cq_low, z_s[R:2 * R, C_CQ:C_CQ + 2 * AW].rearrange("r (a c) -> r a c", a=2)).then_inc(cq_loaded, 16)
            for i in range(2 * NB):
                b = i % NB
                if i >= 2:
                    sp.wait_ge(cv_done if i >= NB + 2 else km_turned, i - NB - 1 if i >= NB + 2 else 2 * (i - 1))
                src = (I["cache_mem_k"] if i < NB else I["cache_mem_v"])[0, b].rearrange("(t p) h d -> p t (h d)", p=P)
                sp.dma_start(k_mem[:, i % 2, :, :], src).then_inc(km_in[i % 2], 16)

        def vector_mem_s(dve):
            dve.wait_ge(cq_loaded, 32)
            nc.vector.memset(q_spread, 0.0)
            for t in range(2):
                last = nc.vector.memset(p_spread[t], 0.0)
            nc.vector.tensor_tensor(out=cq_in, in0=cq_in, in1=cq_low, op=ALU.add).then_inc(reached("cq_ready"), 1)
            dve.wait_ge(*at("cq_ready"))
            for h in range(H):
                last = nc.vector.tensor_copy(gate_c[h * R:(h + 1) * R, :], cq_in[:, 1, h * AD:(h + 1) * AD])
            last.then_inc(reached("gate_c_in"), 1)
            dve.wait_ge(*at("cq_turned"))
            nc.vector.tensor_copy(q_spread.rearrange("p (i x) -> p i x", x=P + NQ)[:, :, 0:NQ],
                                  ps_a[:, 0:P].rearrange("p (i q) -> p i q", q=NQ)).then_inc(reached("qs_ready"), 1)
            dve.wait_ge(cl_used, NB)
            dlink(nc.vector.tensor_scalar(lg_c, ps_c[:, 0:NMEM], float(AD ** -0.5), None, ALU.mult))
            dlink(nc.vector.tensor_reduce(out=soft[:, 4:5], in_=lg_c, axis=AX.X, op=ALU.max))
            nc.vector.tensor_scalar(soft[:, 5:6], soft[:, 4:5], -1.0, None, ALU.mult).then_inc(reached("cmax"), 1)
            dve.wait_ge(*at("cexp"))
            dlink(nc.vector.reciprocal(soft[:, 7:8], soft[:, 6:7]))
            dve.wait_ge(*at("cp_turned"))
            for t in range(2):
                dst = p_spread[t].rearrange("p (b x) -> p b x", x=P + NQ)[:, :, 0:P].rearrange(
                    "p b (h y) -> p h b y", h=H)[:, :, :, 0:NQ]
                last = nc.vector.tensor_copy(dst, ps_a[:, t * P:(t + 1) * P].rearrange("p (h b q) -> p h b q", h=H, b=NB))
            last.then_inc(reached("ps_ready"), 1)
            dve.wait_ge(cv_done, NB)
            for h in range(H):
                hs = slice(h * R, (h + 1) * R)
                last = nc.vector.tensor_copy(o_c[hs, :], ps_c[hs, h * AD:(h + 1) * AD])
            dlink(last)
            dve.wait_ge(*at("gate_c_ready"))
            nc.vector.scalar_tensor_tensor(out=o_c, in0=o_c, scalar=soft[:, 7:8], in1=gate_c,
                                           op0=ALU.mult, op1=ALU.mult).then_inc(reached("mixed_c"), 1)

        def tensor_mem_s(pe):
            pe.wait_ge(*at("cq_ready"))
            for h in range(H):
                last = nc.tensor.transpose(ps_a[:, h * R:(h + 1) * R], cq_in[:, 0, h * AD:(h + 1) * AD], ident[0:R, 0:R])
            last.then_inc(reached("cq_turned"), 1)
            yield
            pe.wait_ge(*at("qs_ready"))

            def turn(b):
                pe.wait_ge(km_in[b % 2], 16 * (b // 2 + 1))
                for g in range(2):
                    if b:
                        pe.wait_ge(kt_ready, 2 * (b - 1) + g + 1)
                    for i in range(4):
                        h, t = 2 * g + i // 2, i % 2
                        last = nc.tensor.transpose((ps_a, ps_b)[g][:, i * P:(i + 1) * P],
                                                   k_mem[:, b % 2, t, h * AD:(h + 1) * AD], ident[:, :])
                    last.then_inc(km_turned, 1)

            turn(0)
            yield
            for b in range(NB):
                if b + 1 < NB:
                    turn(b + 1)
                pe.wait_ge(kt_ready, 2 * (b + 1))
                for h in range(H):
                    i = h * NB + b
                    last = nc.tensor.matmul(ps_c[:, 0:NMEM], q_spread[:, i * P:(i + 1) * P], kt_mem[:, b % 2, h, :],
                                            start=b == 0 and h == 0, stop=b == NB - 1 and h == H - 1)
                last.then_inc(cl_used, 1)
                yield
            yield
            pe.wait_ge(*at("cexp"))
            for t in range(2):
                last = nc.tensor.transpose(ps_a[:, t * P:(t + 1) * P], pr_c[:, t * P:(t + 1) * P], ident[:, :])
            last.then_inc(reached("cp_turned"), 1)
            yield
            pe.wait_ge(*at("ps_ready"))
            for b in range(NB):
                i = NB + b
                pe.wait_ge(km_in[i % 2], 16 * (i // 2 + 1))
                for t in range(2):
                    last = nc.tensor.matmul(ps_c[:, :], p_spread[t][:, b * P:(b + 1) * P], k_mem[:, i % 2, t, :],
                                            start=b == 0 and t == 0, stop=b == NB - 1 and t == 1)
                last.then_inc(cv_done, 1)
                if b % 2:
                    yield

        cl_used = sem("cl_used")

        def scalar_mem_s(act):
            act.wait_ge(*at("gate_c_in"))
            nc.scalar.activation(gate_c, gate_c, ACT.Silu).then_inc(reached("gate_c_ready"), 1)
            yield
            act.wait_ge(*at("qs_ready"))
            for b in range(NB):
                for g in range(2):
                    act.wait_ge(km_turned, 2 * b + g + 1)
                    if b >= 2:
                        act.wait_ge(cl_used, b - 1)
                    nc.scalar.copy(kt_mem[:, b % 2, 2 * g:2 * g + 2, :],
                                   (ps_a, ps_b)[g][:, :].rearrange("p (h m) -> p h m", h=2)).then_inc(kt_ready, 1)
                yield
            yield
            act.wait_ge(*at("cmax"))
            nc.scalar.activation(pr_c, lg_c, ACT.Exp, bias=soft[:, 5:6], accum_out=soft[:, 6:7]).then_inc(reached("cexp"), 1)
            yield from hosted_pause(2 + NB // 2)

        GW = S + R
        CK = 4
        row = lambda i: place(GW * i, [GW], H)
        g_f, g_i, g_t, g_b, g_M, g_m, g_w, g_e, g_one, g_zero = (row(i) for i in range(10))
        M0 = 10 * GW
        keep_m = sb("keep_m", [P, 232])
        c_a = keep_m[:, 0:20].rearrange("p (m h) -> p m h", h=H)
        c_w = keep_m[:, 20:40].rearrange("p (m h) -> p m h", h=H)
        c_e = keep_m[:, 40:60].rearrange("p (m h) -> p m h", h=H)
        conv_c = keep_m[:, 60:140].rearrange("p (k j) -> p k j", j=CK + 1)
        mx_T = keep_m[0:H, 140:150]
        bias_g = keep_m[0:H, 150:152]
        m0_s = keep_m[0:H, 152:160]
        a_T = keep_m[0:H, 160:168]
        bn_o = keep_m[:, 168:176]
        st_m = keep_m[:, 176:184]
        aT8 = keep_m[0:NB, 184:188]
        w_b = keep_m[0:R, 188:220].rearrange("p (h b) -> p h b", h=H)
        batch_of = keep_m[0:R, 220:228]
        hr = sb("head_rows", [H, H * P])
        z_h = place(M0, [5, MT, MD])
        va = place(M0 + 5120, [MT, MD + 2])
        xc = place(M0 + 6152, [S + CK])
        cv = place(M0 + 6668, [S])
        qk_t = place(M0 + 7180, [2, 2, S])
        k_n = place(M0 + 9228, [MT, MD])
        p_w = place(M0 + 10252, [MT, S])
        w_t = place(M0 + 12300, [S])
        h_o = place(M0 + 12812, [2, MD])
        hn = place(M0 + 13324, [H * MD])
        c_o = place(M0 + 14348, [2, MD])
        n_o = place(M0 + 14860, [MD], 1)
        causal = place(M0 + 15116, [P])
        assert M0 + 15244 <= AR_N
        conv_nat = place(M0, [2 * MW], CK + 1)
        ifp = place(M0 + 2048, [MT, 2 * H])
        ifs = place(M0 + 2112, [2, 2 * H], R)
        m0_nat = place(M0 + 2144, [H], NB)

        (mc_in, zh_in, xc_turned, xc_done, keys_scaled, kn_turned, kn_done) = (
            sem(n) for n in ("mc_in", "zh_in", "xc_turned", "xc_done", "keys_scaled", "kn_turned", "kn_done"))
        (g_turned, g_copied, mb_done, w_arg, w_exp, s_done, w_done, h_done, h_norm, h_sqrt,
            h_out, vw_done, c_done, c_copied, c_stored, gate_m) = (
            sem(n) for n in ("g_turned", "g_copied", "mb_done", "w_arg", "w_exp", "s_done", "w_done", "h_done",
            "h_norm", "h_sqrt", "h_out", "vw_done", "c_done", "c_copied", "c_stored", "gate_m"))
        h_stored = [sem("h_stored0"), sem("h_stored1")]
        conv_out = sem("conv_out")
        N_MC = 13

        def sync_mlstm_consts(sp):
            sp.wait_ge(o_stored, 16 * 2 * MT)
            sp.wait_ge(kv_stored, 48 * MT)
            for i in range(MT + 1):
                sp.wait_ge(z_stored[i], 16 * (N_Y0 - N_A0))
            for dst, src in ((hr[:, :], C["head_row"]), (g_one, C["carry"]), (g_zero, C["zeros"]),
                             (bias_g[:, 0:1], I["b_if"][0, 0:H].unsqueeze(1)), (bias_g[:, 1:2], I["b_if"][0, H:2 * H].unsqueeze(1)),
                             (batch_of, C["batch_of"]), (causal, C["causal"]),
                             (hn, I["mlstm_head_norm"][0:1, :].broadcast_to([P, MW])),
                             (conv_nat[0:CK, :], I["conv_w"][0]), (conv_nat[CK:CK + 1, :], I["conv_b"][0:1, :]),
                             (ifp, z_p[:, C_IF:C_IF + 2 * H].rearrange("(m p) c -> p m c", p=P)),
                             (ifs, z_s[:, C_IF:C_IF + 2 * H].rearrange("(a r) c -> r a c", a=2)),
                             (m0_nat, I["state_mlstm_m"][0])):
                sp.dma_start(dst, src).then_inc(mc_in, 16)
            sp.dma_start(O["p_conv"].rearrange("l b j c -> (l b j) c"), z_p[S - CK + 1:S, 0:2 * MW]).then_inc(conv_out, 16)

        def sync_mlstm_head(sp, h):
            if h == 0:
                sp.wait_ge(*at("conv_w_t"))
            else:
                sp.wait_ge(c_copied, 2 * h)
            for i, c in enumerate((C_QK, C_QK + MW, C_V, C_O, C_G)):
                src = z_p[:, c + h * MD:c + (h + 1) * MD].rearrange("(m p) c -> p m c", p=P)
                dst = va[:, :, 0:MD] if i == 2 else z_h[:, i, :, :]
                sp.dma_start(dst, src).then_inc(zh_in, 16)

        def tensor_mlstm_gates(pe):
            pe.wait_ge(mc_in, 16 * N_MC)
            pe.wait_ge(*at("ifs_ready"))
            for half in range(2):
                bank = (ps_a, ps_b)[half]
                for m in range(MT):
                    last = nc.tensor.transpose(bank[0:H, m * P:(m + 1) * P], ifp[:, m, half * H:(half + 1) * H], ident[:, :])
                last.then_inc(g_turned, 1)
            nc.tensor.transpose(ps_c[0:H, 0:R], ifs[:, 0, 0:H], ident[0:R, 0:R])
            nc.tensor.transpose(ps_c[0:H, R:2 * R], ifs[:, 0, H:2 * H], ident[0:R, 0:R])
            nc.tensor.transpose(ps_c[0:H, 2 * R:2 * R + NB], m0_nat, ident[0:NB, 0:NB]).then_inc(g_turned, 1)
            pe.wait_ge(g_copied, 5)
            for k in range(KT):
                last = nc.tensor.transpose(ps_a[:, k * (CK + 1):(k + 1) * (CK + 1)], conv_nat[:, k * P:(k + 1) * P],
                                           ident[0:CK + 1, 0:CK + 1])
            last.then_inc(reached("conv_w_t"), 1)
            pe.wait_ge(*at("g_we"))
            for m in range(MT + 1):
                n = P if m < MT else R
                for i, r in enumerate((g_i, g_w, g_e)):
                    c = (i * (MT + 1) + m) * H
                    last = nc.tensor.transpose(ps_b[0:n, c:c + H], r[:, m * P:m * P + n], ident[0:H, 0:H])
            nc.tensor.transpose(ps_b[0:NB, 64:64 + H], a_T, ident[0:H, 0:H]).then_inc(reached("g_colt"), 1)


        def scalar_mlstm_gates(act):
            act.wait_ge(g_turned, 1)
            nc.scalar.activation(g_i[:, 0:S], ps_a[0:H, :], ACT.Identity, bias=bias_g[:, 0:1]).then_inc(g_copied, 1)
            act.wait_ge(g_turned, 2)
            nc.scalar.activation(g_f[:, 0:S], ps_b[0:H, :], ACT.Identity, bias=bias_g[:, 1:2]).then_inc(g_copied, 1)
            act.wait_ge(g_turned, 3)
            nc.scalar.activation(g_i[:, S:GW], ps_c[0:H, 0:R], ACT.Identity, bias=bias_g[:, 0:1]).then_inc(g_copied, 1)
            nc.scalar.activation(g_f[:, S:GW], ps_c[0:H, R:2 * R], ACT.Identity, bias=bias_g[:, 1:2]).then_inc(g_copied, 1)
            nc.scalar.copy(m0_s, ps_c[0:H, 2 * R:2 * R + NB]).then_inc(g_copied, 1)
            act.wait_ge(*at("conv_w_t"))
            nc.scalar.copy(conv_c, ps_a[:, 0:KT * (CK + 1)].rearrange("p (k j) -> p k j", j=CK + 1)).then_inc(reached("conv_w_c"), 1)
            act.wait_ge(*at("g_abs"))
            nc.scalar.activation(g_e, g_t, ACT.Exp, scale=-1.0).then_inc(reached("g_exp"), 1)
            act.wait_ge(*at("g_exp"))
            nc.scalar.activation(g_e, g_e, ACT.Ln, bias=1.0).then_inc(reached("g_ln"), 1)
            act.wait_ge(*at("g_rows"))
            alink(nc.scalar.activation(g_w, g_w, ACT.Exp))
            alink(nc.scalar.activation(g_e, g_m, ACT.Exp, scale=-1.0))
            nc.scalar.activation(g_t[:, S:GW], g_t[:, S:GW], ACT.Exp)
            nc.scalar.activation(a_T, a_T, ACT.Exp).then_inc(reached("g_we"), 1)
            act.wait_ge(*at("g_colt"))
            for m in (0, 1):
                n = P if m == 0 else R
                v = ps_b[0:n, 0:3 * (MT + 1) * H].rearrange("p (i m h) -> p i m h", i=3, h=H)
                ms = slice(0, MT) if m == 0 else slice(MT, MT + 1)
                for i, dst in enumerate((c_a, c_w, c_e)):
                    last = nc.scalar.copy(dst[0:n, ms, :], v[:, i, ms, :])
            nc.scalar.copy(aT8, ps_b[0:NB, 64:64 + H]).then_inc(reached("g_cols"), 1)

        def vector_mlstm_gates(dve):
            dve.wait_ge(mc_in, 16 * N_MC)
            nc.vector.tensor_tensor(out=ifs[:, 0, :], in0=ifs[:, 0, :], in1=ifs[:, 1, :], op=ALU.add).then_inc(reached("ifs_ready"), 1)
            dve.wait_ge(g_copied, 5)
            dlink(nc.vector.tensor_scalar(g_t, g_f, -1.0, None, ALU.mult))
            nc.vector.tensor_tensor(out=g_t, in0=g_t, in1=g_f, op=ALU.max).then_inc(reached("g_abs"), 1)
            dve.wait_ge(*at("g_ln"))
            dlink(nc.vector.scalar_tensor_tensor(out=g_f, in0=g_f, scalar=0.0, in1=g_e, op0=ALU.min, op1=ALU.subtract))
            dlink(nc.vector.tensor_tensor_scan(out=g_b, data0=g_one, data1=g_f, initial=0.0, op0=ALU.mult, op1=ALU.add))
            dlink(nc.vector.tensor_tensor(out=g_i, in0=g_i, in1=g_b, op=ALU.subtract))
            nc.vector.tensor_tensor_scan(out=g_M[:, 0:S], data0=g_zero[:, 0:S], data1=g_i[:, 0:S], initial=0.0,
                                         op0=ALU.add, op1=ALU.max)
            by_b = lambda r: r[:, S:GW].rearrange("p (b t) -> p b t", t=NQ)
            Ms, as_, ts_, ws = by_b(g_M), by_b(g_i), by_b(g_t), by_b(g_w)
            dlink(nc.vector.tensor_tensor(out=Ms[:, :, 0], in0=as_[:, :, 0], in1=m0_s, op=ALU.max))
            for t in range(1, NQ):
                dlink(nc.vector.tensor_tensor(out=Ms[:, :, t], in0=Ms[:, :, t - 1], in1=as_[:, :, t], op=ALU.max))
            nc.vector.tensor_tensor(out=g_m, in0=g_b, in1=g_M, op=ALU.add)
            nc.vector.tensor_scalar(g_w[:, 0:S], g_i[:, 0:S], g_M[:, S - 1:S], None, ALU.subtract)
            nc.vector.tensor_tensor(out=ws, in0=as_, in1=Ms[:, :, NQ - 1:NQ].broadcast_to([H, NB, NQ]), op=ALU.subtract)
            nc.vector.tensor_tensor(out=ts_, in0=m0_s.unsqueeze(2).broadcast_to([H, NB, NQ]), in1=Ms, op=ALU.subtract)
            nc.vector.tensor_tensor(out=a_T, in0=m0_s, in1=Ms[:, :, NQ - 1], op=ALU.subtract).then_inc(reached("g_rows"), 1)

        def sync_mlstm_m(sp):
            sp.wait_ge(*at("g_rows"))
            sp.dma_start(O["p_m"].rearrange("l b h -> (l b h)").unsqueeze(1), g_m[:, S - 1:S]).then_inc(conv_out, 16)
            sp.dma_start(O["s_m"][0].rearrange("b h -> h b"),
                         g_m[:, S:GW].rearrange("p (b t) -> p b t", t=NQ)[:, :, NQ - 1], allow_slow_non_contiguous=True
                         ).then_inc(conv_out, 16)

        def tensor_mlstm_head(pe, h):
            pe.wait_ge(zh_in, 16 * 5 * (h + 1))
            pe.wait_ge(*at("g_cols"))
            if h:
                pe.wait_ge(c_copied, 2 * h)
            for u in range(4):
                g = 4 * h + u
                if u >= 2:
                    pe.wait_ge(xc_done, g - 1)
                bank = (ps_a, ps_b)[u % 2]
                for m in range(MT):
                    last = nc.tensor.transpose(bank[:, m * P:(m + 1) * P], z_h[:, u // 2, m, (u % 2) * P:(u % 2 + 1) * P],
                                               ident[:, :])
                last.then_inc(xc_turned, 1)
            pe.wait_ge(conv_silu, 4 * (h + 1))
            pe.wait_ge(keys_scaled, 2 * (h + 1))
            nc.tensor.matmul(ps_c[:, :], hr[:, h * P:(h + 1) * P], g_M[:, 0:S], start=True, stop=True).then_inc(mb_done, 1)
            for u in range(2):
                bank = (ps_a, ps_b)[u]
                for i in range(4):
                    m, d = 2 * u + i // 2, i % 2
                    last = nc.tensor.transpose(bank[:, i * P:(i + 1) * P], qk_t[:, 1, d, m * P:(m + 1) * P], ident[:, :])
                last.then_inc(kn_turned, 1)
            for i in range(MT):
                g = MT * h + i
                bank = (ps_a, ps_b)[i % 2]
                if i < 2:
                    pe.wait_ge(kn_done, 2 * h + i + 1)
                else:
                    pe.wait_ge(w_done, g - 1)
                for d in range(2):
                    last = nc.tensor.matmul(bank[:, 0:S - i * P], qk_t[:, 1, d, i * P:(i + 1) * P],
                                            qk_t[:, 0, d, i * P:S], start=d == 0, stop=d == 1)
                last.then_inc(s_done, 1)
            pe.wait_ge(w_done, MT * (h + 1))
            for m in range(MT):
                g = MT * h + m
                bank = (ps_a, ps_b)[m % 2]
                if m >= 2:
                    pe.wait_ge(h_done, g - 1)
                for i in range(m + 1):
                    last = nc.tensor.matmul(bank[:, 0:MD + 1], p_w[:, i, m * P:(m + 1) * P], va[:, i, 0:MD + 1],
                                            start=i == 0, stop=i == m)
                last.then_inc(num_ready, 1)
            pe.wait_ge(vw_done, h + 1)
            pe.wait_ge(h_done, MT * (h + 1))
            for e in range(2):
                for i in range(MT):
                    last = nc.tensor.matmul(ps_c[:, e * MD:(e + 1) * MD], va[:, i, e * P:(e + 1) * P], k_n[:, i, :],
                                            start=i == 0, stop=i == MT - 1)
            last.then_inc(c_done, 1)
            for i in range(MT):
                last = nc.tensor.matmul(ps_a[0:1, 0:MD], c_w[:, i, h:h + 1], k_n[:, i, :], start=i == 0, stop=i == MT - 1)
            last.then_inc(c_done, 1)

        num_ready = sem("num_ready")

        def vector_mlstm_head(dve, h):
            if h == 0:
                dve.wait_ge(*at("conv_w_c"))
                nc.vector.memset(xc[:, 0:CK - 1], 0.0)
                nc.vector.memset(va[:, :, MD:MD + 1], 1.0)
            for u in range(4):
                g, k = 4 * h + u, (u // 2) * (KT // 2) + 2 * h + u % 2
                dve.wait_ge(xc_turned, g + 1)
                if g:
                    dve.wait_ge(conv_silu, g)
                dlink(nc.vector.tensor_copy(xc[:, CK - 1:CK - 1 + S], (ps_a, ps_b)[u % 2][:, :]))
                dlink(nc.vector.tensor_scalar(cv, xc[:, 0:S], conv_c[:, k, 0:1], None, ALU.mult))
                for j in range(1, CK):
                    out = nc.vector.scalar_tensor_tensor(out=cv, in0=xc[:, j:j + S], scalar=conv_c[:, k, j:j + 1], in1=cv,
                                                         op0=ALU.mult, op1=ALU.add)
                    if j < CK - 1:
                        dlink(out)
                out.then_inc(xc_done, 1)
                if u >= 2:
                    dve.wait_ge(conv_silu, g + 1)
                    nc.vector.tensor_scalar(qk_t[:, 1, u % 2, :], qk_t[:, 1, u % 2, :], float(MD ** -0.5), None,
                                            ALU.mult).then_inc(keys_scaled, 1)
            for u in range(2):
                dve.wait_ge(kn_turned, 2 * h + u + 1)
                nc.vector.tensor_copy(k_n[:, 2 * u:2 * u + 2, :],
                                      (ps_a, ps_b)[u][:, :].rearrange("p (m d) -> p m d", m=2)).then_inc(kn_done, 1)
            dve.wait_ge(mb_done, h + 1)
            for i in range(MT):
                g, n = MT * h + i, S - i * P
                if g:
                    dve.wait_ge(w_done, g)
                nc.vector.tensor_scalar(w_t[:, 0:n], ps_c[:, i * P:S], c_a[:, i, h:h + 1], 0.0,
                                        ALU.subtract, ALU.max).then_inc(w_arg, 1)
                dve.wait_ge(w_exp, g + 1)
                dlink(nc.vector.tensor_tensor(out=w_t[:, 0:P], in0=w_t[:, 0:P], in1=causal, op=ALU.mult))
                dve.wait_ge(s_done, g + 1)
                nc.vector.tensor_tensor(out=p_w[:, i, i * P:S], in0=(ps_a, ps_b)[i % 2][:, 0:n], in1=w_t[:, 0:n],
                                        op=ALU.mult).then_inc(w_done, 1)
            dve.wait_ge(gate_m, 2 * (h + 1))
            dlink(nc.vector.tensor_tensor(out=z_h[:, 3, :, :], in0=z_h[:, 3, :, :], in1=z_h[:, 4, :, :], op=ALU.mult))
            dlink(nc.vector.tensor_tensor(out=z_h[:, 3, :, :], in0=z_h[:, 3, :, :],
                                          in1=hn[:, h * MD:(h + 1) * MD].unsqueeze(1).broadcast_to([P, MT, MD]), op=ALU.mult))
            for m in range(MT):
                g = MT * h + m
                dve.wait_ge(num_ready, g + 1)
                if g >= 2:
                    dve.wait_ge(h_stored[g % 2], 16 * (g // 2))
                normalise_head(dve, (ps_a, ps_b)[m % 2], P, c_e[:, m, h:h + 1], h_o[:, g % 2, :], z_h[:, 3, m, :], h_done, g)
            for i in range(MT):
                last = nc.vector.tensor_scalar(va[:, i, 0:MD], va[:, i, 0:MD], c_w[:, i, h:h + 1], None, ALU.mult)
            last.then_inc(vw_done, 1)
            if h:
                dve.wait_ge(c_stored, 32 * h)
            dve.wait_ge(c_done, 2 * h + 1)
            nc.vector.tensor_copy(c_o, ps_c[:, :].rearrange("p (e d) -> p e d", e=2)).then_inc(c_copied, 1)
            dve.wait_ge(c_done, 2 * h + 2)
            nc.vector.tensor_copy(n_o, ps_a[0:1, 0:MD]).then_inc(c_copied, 1)

        conv_silu = sem("conv_silu")
        var_m = sem("var_m")

        def normalise_head(dve, bank, n, floor, out, gate, done, g):
            s = st_m[0:n, :]
            den = bank[0:n, MD:MD + 1]
            dlink(nc.vector.tensor_scalar(s[:, 0:1], den, -1.0, None, ALU.mult))
            dlink(nc.vector.scalar_tensor_tensor(out=s[:, 0:1], in0=den, scalar=s[:, 0:1], in1=floor,
                                                 op0=ALU.max, op1=ALU.max))
            dlink(nc.vector.reciprocal(s[:, 1:2], s[:, 0:1]))
            ins = nc.vector.tensor_scalar(out, bank[0:n, 0:MD], s[:, 1:2], None, ALU.mult)
            ins.then_inc(done, 1)
            dve.wait_ge(done, g + 1)
            dlink(nc.vector.bn_stats(bn_o[0:n, 0:6], out))
            dlink(nc.vector.bn_aggr(s[:, 2:4], bn_o[0:n, 0:6]))
            nc.vector.tensor_scalar(s[:, 4:5], s[:, 3:4], LN_EPS, None, ALU.add).then_inc(var_m, 1)
            counts["norm"] += 1
            dve.wait_ge(h_sqrt, counts["norm"])
            rsqrt_refined(s[:, 4:5], s[:, 6:7], s[:, 5:6])
            dlink(nc.vector.tensor_scalar(out, out, s[:, 2:3], s[:, 5:6], ALU.subtract, ALU.mult))
            nc.vector.tensor_tensor(out=out, in0=out, in1=gate, op=ALU.mult).then_inc(h_out, 1)

        def scalar_sqrt(act, n):
            counts["sqrt"] += 1
            act.wait_ge(var_m, counts["sqrt"])
            nc.scalar.activation(st_m[0:n, 6:7], st_m[0:n, 4:5], ACT.Sqrt).then_inc(h_sqrt, 1)

        def scalar_mlstm_head(act, h):
            act.wait_ge(zh_in, 16 * 5 * (h + 1))
            for u in range(4):
                g, k = 4 * h + u, (u // 2) * (KT // 2) + 2 * h + u % 2
                act.wait_ge(xc_done, g + 1)
                nc.scalar.activation(qk_t[:, u // 2, u % 2, :], cv, ACT.Silu, bias=conv_c[:, k, CK:CK + 1]).then_inc(conv_silu, 1)
            nc.scalar.activation(z_h[:, 3, :, :], z_h[:, 3, :, :], ACT.Sigmoid).then_inc(gate_m, 1)
            nc.scalar.activation(z_h[:, 4, :, :], z_h[:, 4, :, :], ACT.Silu).then_inc(gate_m, 1)
            for i in range(MT):
                g, n = MT * h + i, S - i * P
                act.wait_ge(w_arg, g + 1)
                nc.scalar.activation(w_t[:, 0:n], w_t[:, 0:n], ACT.Exp, scale=-1.0).then_inc(w_exp, 1)
            for m in range(MT):
                scalar_sqrt(act, P)

        def sync_mlstm_out(sp, h):
            for m in range(MT):
                g = MT * h + m
                sp.wait_ge(h_out, g + 1)
                sp.dma_start(mix_p[m * P:(m + 1) * P, h * MD:(h + 1) * MD], h_o[:, g % 2, :]).then_inc(h_stored[g % 2], 16)
            sp.wait_ge(c_copied, 2 * h + 2)
            sp.dma_start(O["p_C"][0, 0, h].rearrange("(e p) d -> p e d", p=P), c_o).then_inc(c_stored, 16)
            sp.dma_start(O["p_n"][0, 0, h:h + 1, :], n_o).then_inc(c_stored, 16)

        XW = NQ + CK - 1
        HB = H * NB
        s_nat = place(M0, [5 * MW], R)
        s_low = place(M0 + 5 * MW, [5 * MW], R)
        k_ns = place(M0, [MW], R)
        n_in8 = place(M0 + MW, [H, MD], NB)
        LO = M0 + 5 * MW
        s_hist = place(LO, [2 * MW], NB * (CK - 1))
        QS = NB * (R + NQ)
        q_spr = place(LO, [2 * H, QS])
        vwb = place(LO + 2304, [2, MD], R)
        va_s = place(LO + 2816, [H, MD + 1], R)
        hn_s = place(LO + 3844, [MW], R)
        assert 2 * H * QS == 2304 and LO + 3844 + MW <= M0 + 10 * MW
        XS0 = M0 + 10 * MW
        x_ext = place(XS0, [KT, NB, XW])
        cv_s = place(XS0 + 896, [KT, NB, NQ])
        cv_t = place(XS0 + 1408, [KT, NB, NQ])
        decay = place(XS0 + 1408, [HB])
        n_t = place(XS0 + 1440, [2, HB])
        am_bc = place(XS0 + 1504, [H, R])
        wt_s = place(XS0 + 1632, [H, R], R)
        p_ws = place(XS0 + 1760, [H, R], R)
        NCR = 4
        c_in = place(XS0 + 1920, [NCR, 2, MD])
        ct = place(XS0 + 3968, [2, 2, MD + 1])
        n_nat = place(XS0 + 4996, [MD], HB)
        assert XS0 + 4996 + MD <= AR_N
        causal_s = keep_p[0:R, 0:R]
        (sm_in, sconv_out, hist_in, sx_turned, ks_turned, ks_copied, s_gate, sw_arg, late_in,
            ctt, ct_copied, inter_done, vwb_ready, u_done, upd_done, hs_done, sn_done, sn_copied) = (
            sem(n) for n in ("sm_in", "sconv_out", "hist_in", "sx_turned", "ks_turned", "ks_copied", "s_gate",
            "sw_arg", "late_in", "ctt", "ct_copied", "inter_done", "vwb_ready", "u_done",
            "upd_done", "hs_done", "sn_done", "sn_copied"))
        cin_in = [sem(f"cin_in{i}") for i in range(NCR)]
        cst_out = [sem(f"cst_out{i}") for i in range(NCR)]
        sn_out = sem("sn_out")

        def sync_mlstm_s(sp):
            sp.wait_ge(c_stored, 32 * H)
            for i in range(2):
                sp.wait_ge(h_stored[i], 16 * MT * H // 2)
            sp.wait_ge(c_copied, 2 * H)
            sp.dma_start(s_nat, z_s[0:R, 0:5 * MW]).then_inc(sm_in, 16)
            sp.dma_start(s_low, z_s[R:2 * R, 0:5 * MW]).then_inc(sm_in, 16)
            sp.dma_start(causal_s, C["causal_s"]).then_inc(sm_in, 16)
            sp.wait_ge(*at("sm_ready"))
            sp.dma_start(s_hist, I["state_conv"][0].rearrange("b j c -> (b j) c")).then_inc(hist_in, 16)
            sp.dma_start(n_nat, I["state_mlstm_n"][0].rearrange("b h d -> (b h) d")).then_inc(hist_in, 16)
            for b in range(NB):
                sp.dma_start(O["s_conv"][0, b], s_nat[b * NQ + NQ - CK + 1:(b + 1) * NQ, 0:2 * MW]).then_inc(sconv_out, 16)
            sp.wait_ge(sx_turned, 2)
            sp.wait_ge(sconv_out, 16 * NB)
            sp.dma_start(hn_s, I["mlstm_head_norm"][0:1, :].broadcast_to([R, MW])).then_inc(late_in, 16)
            sp.dma_start(n_in8, I["state_mlstm_n"][0]).then_inc(late_in, 16)

        def sync_state_in(sp, p):
            h, b = p // NB, p % NB
            if p >= NCR:
                sp.wait_ge(cst_out[p % NCR], 16 * (p // NCR))
            sp.dma_start(c_in[:, p % NCR, :, :], I["state_mlstm_C"][0, b, h].rearrange("(e p) d -> p e d", p=P)
                         ).then_inc(cin_in[p % NCR], 16)

        def sync_state_out(sp, p):
            h, b = p // NB, p % NB
            sp.wait_ge(upd_done, p + 1)
            sp.dma_start(O["s_C"][0, b, h].rearrange("(e p) d -> p e d", p=P), c_in[:, p % NCR, :, :]
                         ).then_inc(cst_out[p % NCR], 16)

        def sync_states(sp):
            for p in range(NCR - 1):
                sync_state_in(sp, p)
            for p in range(HB):
                sync_state_out(sp, p)
                if p + NCR - 1 < HB:
                    sync_state_in(sp, p + NCR - 1)
            sp.wait_ge(sn_copied, H)
            sp.dma_start(O["s_n"][0], n_in8).then_inc(sn_out, 16)
            sp.wait_ge(h_out, MT * H + H)
            sp.dma_start(mix_s[:, 0:MW], s_nat[:, 3 * MW:4 * MW]).then_inc(sn_out, 16)

        def vector_mlstm_s_prep(dve):
            dve.wait_ge(sm_in, 48)
            nc.vector.tensor_tensor(out=s_nat, in0=s_nat, in1=s_low, op=ALU.add).then_inc(reached("sm_ready"), 1)
            dve.wait_ge(sx_turned, 2)
            nc.vector.tensor_copy(x_ext[:, :, :, CK - 1:XW], ps_a[:, :].rearrange("p (k b t) -> p k b t", k=KT, b=NB))
            dlink(nc.vector.tensor_copy(x_ext[:, :, :, 0:CK - 1],
                                        ps_b[:, 0:KT * NB * (CK - 1)].rearrange("p (k b j) -> p k b j", k=KT, b=NB)))
            tap = lambda j: conv_c[:, :, j:j + 1].unsqueeze(3).broadcast_to([P, KT, NB, NQ])
            dlink(nc.vector.tensor_tensor(out=cv_s, in0=x_ext[:, :, :, 0:NQ], in1=tap(0), op=ALU.mult))
            for j in range(1, CK):
                dlink(nc.vector.tensor_tensor(out=cv_t, in0=x_ext[:, :, :, j:j + NQ], in1=tap(j), op=ALU.mult))
                dlink(nc.vector.tensor_tensor(out=cv_s, in0=cv_s, in1=cv_t, op=ALU.add))
            nc.vector.tensor_tensor(out=cv_s, in0=cv_s, in1=tap(CK), op=ALU.add).then_inc(reached("scv_ready"), 1)
            nc.vector.memset(q_spr, 0.0)
            nc.vector.memset(va_s[:, :, MD:MD + 1], 1.0)
            nc.vector.tensor_copy(va_s[:, :, 0:MD], s_nat[:, 2 * MW:3 * MW].rearrange("p (h d) -> p h d", h=H))
            dlink(nc.vector.tensor_tensor(out=w_b, in0=batch_of.unsqueeze(1).broadcast_to([R, H, NB]),
                                          in1=c_w[0:R, MT, :].unsqueeze(2).broadcast_to([R, H, NB]), op=ALU.mult))
            dve.wait_ge(*at("scv_silu"))
            nc.vector.tensor_scalar(cv_s[:, KT // 2:KT, :, :], cv_s[:, KT // 2:KT, :, :], float(MD ** -0.5), None,
                                    ALU.mult).then_inc(reached("ks_scaled"), 1)
            dve.wait_ge(*at("bc_done"))
            nc.vector.tensor_copy(am_bc, ps_c[:, 0:H * R].rearrange("p (h r) -> p h r", h=H))
            nc.vector.tensor_copy(decay, ps_c[:, 128:128 + HB])
            nc.vector.tensor_copy(n_t, ps_c[:, 160:160 + 2 * HB].rearrange("p (d x) -> p d x", d=2))
            for h in range(H):
                last = nc.vector.tensor_scalar(wt_s[:, h, :], ps_c[0:R, 224 + h * R:224 + (h + 1) * R], c_a[0:R, MT, h:h + 1],
                                               0.0, ALU.subtract, ALU.max)
            last.then_inc(reached("bc_copied"), 1)
            dve.wait_ge(*at("bc_copied"))
            q5 = cv_s[:, 0:2 * H, :, :].rearrange("p (h d) b t -> p h d b t", d=2)
            o5 = q_spr.rearrange("p (h d) (b x) -> p h d b x", d=2, x=R + NQ)
            for h in range(H):
                for d in range(2):
                    last = nc.vector.tensor_tensor(out=o5[:, h, d, :, 0:NQ], in0=q5[:, h, d, :, :],
                                                   in1=am_bc[:, h, :].rearrange("p (b t) -> p b t", t=NQ), op=ALU.mult)
            last.then_inc(reached("qspr_ready"), 1)
            dve.wait_ge(s_gate, 2)
            dve.wait_ge(late_in, 32)
            so, sg = s_nat[:, 3 * MW:4 * MW], s_nat[:, 4 * MW:5 * MW]
            dlink(nc.vector.tensor_tensor(out=sg, in0=sg, in1=so, op=ALU.mult))
            dlink(nc.vector.tensor_tensor(out=sg, in0=sg, in1=hn_s, op=ALU.mult))
            dve.wait_ge(*at("sw_exp"))
            dlink(nc.vector.tensor_tensor(out=wt_s, in0=wt_s, in1=causal_s.unsqueeze(1).broadcast_to([R, H, R]), op=ALU.mult))
            dve.wait_ge(*at("ss_done"))
            nc.vector.tensor_tensor(out=p_ws, in0=ps_a[0:R, 0:H * R].rearrange("p (h r) -> p h r", h=H), in1=wt_s,
                                    op=ALU.mult).then_inc(reached("pws_ready"), 1)

        def scalar_mlstm_s_prep(act):
            act.wait_ge(*at("sm_ready"))
            nc.scalar.activation(s_nat[:, 3 * MW:4 * MW], s_nat[:, 3 * MW:4 * MW], ACT.Sigmoid).then_inc(s_gate, 1)
            nc.scalar.activation(s_nat[:, 4 * MW:5 * MW], s_nat[:, 4 * MW:5 * MW], ACT.Silu).then_inc(s_gate, 1)
            act.wait_ge(*at("scv_ready"))
            nc.scalar.activation(cv_s, cv_s, ACT.Silu).then_inc(reached("scv_silu"), 1)
            for u in range(2):
                act.wait_ge(ks_turned, u + 1)
                act.wait_ge(sconv_out, 16 * NB)
                nc.scalar.copy(k_ns[:, u * 512:(u + 1) * 512], (ps_a, ps_b)[u][0:R, :]).then_inc(ks_copied, 1)
            act.wait_ge(*at("bc_copied"))
            nc.scalar.activation(wt_s, wt_s, ACT.Exp, scale=-1.0).then_inc(reached("sw_exp"), 1)

        def tensor_mlstm_s_prep(pe):
            pe.wait_ge(*at("sm_ready"))
            pe.wait_ge(c_copied, 2 * H)
            for k in range(KT):
                last = nc.tensor.transpose(ps_a[:, k * R:(k + 1) * R], s_nat[:, k * P:(k + 1) * P], ident[0:R, 0:R])
            last.then_inc(sx_turned, 1)
            pe.wait_ge(hist_in, 32)
            n = NB * (CK - 1)
            for k in range(KT):
                last = nc.tensor.transpose(ps_b[:, k * n:(k + 1) * n], s_hist[:, k * P:(k + 1) * P], ident[0:n, 0:n])
            last.then_inc(sx_turned, 1)
            for h in range(H):
                nc.tensor.matmul(ps_c[:, h * R:(h + 1) * R], hr[:, h * P:(h + 1) * P], g_t[:, S:GW], start=True, stop=True)
                nc.tensor.matmul(ps_c[:, 128 + h * NB:128 + (h + 1) * NB], hr[:, h * P:(h + 1) * P], a_T,
                                 start=True, stop=True)
                nc.tensor.matmul(ps_c[0:R, 224 + h * R:224 + (h + 1) * R], hr[:, h * P:h * P + R], g_M[:, S:GW],
                                 start=True, stop=True)
            for d in range(2):
                last = nc.tensor.transpose(ps_c[:, 160 + d * HB:160 + (d + 1) * HB], n_nat[:, d * P:(d + 1) * P],
                                           ident[0:HB, 0:HB])
            last.then_inc(reached("bc_done"), 1)
            pe.wait_ge(*at("ks_scaled"))
            for u in range(2):
                for i in range(4):
                    k = KT // 2 + 4 * u + i
                    last = nc.tensor.transpose((ps_a, ps_b)[u][0:R, i * P:(i + 1) * P],
                                               cv_s[:, k, :, :].rearrange("p b t -> p (b t)"), ident[:, :])
                last.then_inc(ks_turned, 1)
            pe.wait_ge(ks_copied, 2)
            for h in range(H):
                for d in range(2):
                    last = nc.tensor.matmul(ps_a[0:R, h * R:(h + 1) * R],
                                            cv_s[:, KT // 2 + 2 * h + d, :, :].rearrange("p b t -> p (b t)"),
                                            cv_s[:, 2 * h + d, :, :].rearrange("p b t -> p (b t)"),
                                            start=d == 0, stop=d == 1)
            last.then_inc(reached("ss_done"), 1)

        def tensor_state_turn(pe, p):
            pe.wait_ge(cin_in[p % NCR], 16 * (p // NCR + 1))
            if p:
                pe.wait_ge(ct_copied, p)
            else:
                pe.wait_ge(*at("pws_ready"))
            for d in range(2):
                for e in range(2):
                    i = 2 * d + e
                    last = nc.tensor.transpose(ps_a[:, i * P:(i + 1) * P], c_in[:, p % NCR, e, d * P:(d + 1) * P],
                                               ident[:, :])
            last.then_inc(ctt, 1)

        def tensor_mlstm_s(pe):
            pe.wait_ge(*at("qspr_ready"))
            tensor_state_turn(pe, 0)
            for p in range(HB):
                h, b = p // NB, p % NB
                if p + 1 < HB:
                    tensor_state_turn(pe, p + 1)
                if b == 0:
                    if h:
                        pe.wait_ge(hs_done, h)
                    nc.tensor.matmul(ps_c[0:R, 0:MD + 1], p_ws[:, h, :], va_s[:, h, :], start=True, stop=False)
                pe.wait_ge(ct_copied, p + 1)
                for d in range(2):
                    last = nc.tensor.matmul(ps_c[0:R, 0:MD + 1], q_spr[:, 2 * h + d, b * R:(b + 1) * R], ct[:, p % 2, d, :],
                                            start=False, stop=b == NB - 1 and d == 1)
                last.then_inc(inter_done, 1)
                pe.wait_ge(vwb_ready, p + 1)
                if p:
                    pe.wait_ge(upd_done, p)
                for e in range(2):
                    last = nc.tensor.matmul(ps_b[:, e * MD:(e + 1) * MD], vwb[:, p % 2, e * P:(e + 1) * P],
                                            k_ns[:, h * MD:(h + 1) * MD], start=True, stop=True)
                last.then_inc(u_done, 1)
                if b == NB - 1:
                    pe.wait_ge(upd_done, p + 1)
                    nc.tensor.matmul(ps_b[0:NB, 0:MD], w_b[:, h, :], k_ns[:, h * MD:(h + 1) * MD],
                                     start=True, stop=True).then_inc(sn_done, 1)
                    pe.wait_ge(sn_copied, h + 1)

        def scalar_mlstm_s(act):
            for p in range(HB):
                h, b = p // NB, p % NB
                act.wait_ge(ctt, p + 1)
                if p >= 2:
                    act.wait_ge(inter_done, p - 1)
                nc.scalar.copy(ct[:, p % 2, :, 0:MD], ps_a[:, :].rearrange("p (d e) -> p d e", d=2))
                nc.scalar.copy(ct[:, p % 2, :, MD], n_t[:, :, b * H + h]).then_inc(ct_copied, 1)
                if b == NB - 1:
                    scalar_sqrt(act, R)

        def vector_mlstm_s(dve):
            for p in range(HB):
                h, b = p // NB, p % NB
                if p >= 2:
                    dve.wait_ge(u_done, p - 1)
                nc.vector.tensor_scalar(vwb[:, p % 2, :], s_nat[:, 2 * MW + h * MD:2 * MW + (h + 1) * MD],
                                        w_b[:, h, b:b + 1], None, ALU.mult).then_inc(vwb_ready, 1)
                dve.wait_ge(u_done, p + 1)
                dve.wait_ge(ctt, p + 1)
                nc.vector.scalar_tensor_tensor(out=c_in[:, p % NCR, :, :], in0=c_in[:, p % NCR, :, :],
                                               scalar=decay[:, p:p + 1],
                                               in1=ps_b[:, :].rearrange("p (e d) -> p e d", e=2),
                                               op0=ALU.mult, op1=ALU.add).then_inc(upd_done, 1)
                if b == NB - 1:
                    dve.wait_ge(inter_done, p + 1)
                    cols = slice(h * MD, (h + 1) * MD)
                    normalise_head(dve, ps_c, R, c_e[0:R, MT, h:h + 1], s_nat[:, 3 * MW:4 * MW][:, cols],
                                   s_nat[:, 4 * MW:5 * MW][:, cols], hs_done, h)
                    dve.wait_ge(sn_done, h + 1)
                    nc.vector.scalar_tensor_tensor(out=n_in8[:, h, :], in0=n_in8[:, h, :], scalar=aT8[:, h:h + 1],
                                                   in1=ps_b[0:NB, 0:MD], op0=ALU.mult, op1=ALU.add).then_inc(sn_copied, 1)

        y_t = place(0, [MT + 1, D])
        y_buf = place(10240, [2, D])
        g_post = place(14336, [D])
        x_res = place(16384, [D])
        y_tmp = place(18432, [D])
        y_rows = lambda m: y_t[:, m, :]
        y_in = lambda u: y_buf[:, u % 2, :]
        (gp_in, res_in, y_sq, y_var, y_std, y_ready, y_out) = (
            sem(n) for n in ("gp_in", "res_in", "y_sq", "y_var", "y_std", "y_ready", "y_out"))

        def sync_y_in(sp):
            sp.wait_ge(sn_out, 32)
            for i in range(NCR):
                sp.wait_ge(cst_out[i], 16 * HB // NCR)
            sp.wait_ge(mix_stored, 2 * 16 * H)
            sync_rows(sp, NU_NORM, NU_ALL)
            sp.dma_start(g_post, I["norm_post"][0:1, :].broadcast_to([P, D])).then_inc(gp_in, 16)

        def y_place(m):
            n = P if m < MT else R
            rows = slice(m * P, (m + 1) * P)
            if m < MT:
                return n, I["x_prompt"][0, rows, :], O["y_prompt"][0, rows, :]
            return n, I["x_sample"].rearrange("b t d -> (b t) d"), O["y_sample"].rearrange("b t d -> (b t) d")

        def sync_y_out(sp):
            for m in range(MT + 1):
                n, x, y = y_place(m)
                if m:
                    sp.wait_ge(y_ready, m)
                sp.dma_start(x_res[0:n, :], x).then_inc(res_in, 16)
                if m:
                    n, _, y = y_place(m - 1)
                    sp.dma_start(y, y_t[0:n, m - 1, :]).then_inc(y_out, 16)
            sp.wait_ge(y_ready, MT + 1)
            sp.dma_start(y_place(MT)[2], y_t[0:R, MT, :]).then_inc(y_out, 16)
            sp.wait_ge(y_out, 16 * (MT + 1))

        def scalar_y(act):
            act.wait_ge(acc_read, acc_base(N_END))
            for m in range(MT + 1):
                n = P if m < MT else R
                if m == MT:
                    act.wait_ge(*at("y_joined"))
                if m:
                    act.wait_ge(y_sq, m)
                nc.scalar.activation(y_tmp[0:n, :], y_t[0:n, m, :], ACT.Square,
                                     accum_out=small[0:n, m:m + 1]).then_inc(y_sq, 1)
                act.wait_ge(y_var, m + 1)
                nc.scalar.activation(small[0:n, 16 + m:17 + m], small[0:n, 8 + m:9 + m], ACT.Sqrt).then_inc(y_std, 1)


        def vector_y(dve):
            dve.wait_ge(acc_read, acc_base(N_END))
            dve.wait_ge(gp_in, 16)
            dlink(nc.vector.tensor_copy(y_buf[0:R, 0, :], y_t[R:2 * R, MT, :]))
            nc.vector.tensor_tensor(out=y_t[0:R, MT, :], in0=y_t[0:R, MT, :], in1=y_buf[0:R, 0, :], op=ALU.add).then_inc(reached("y_joined"), 1)
            for m in range(MT + 1):
                n = P if m < MT else R
                dve.wait_ge(y_sq, m + 1)
                nc.vector.tensor_scalar(small[0:n, 8 + m:9 + m], small[0:n, m:m + 1], 1.0 / D, RMS_EPS,
                                        ALU.mult, ALU.add).then_inc(y_var, 1)
                dve.wait_ge(y_std, m + 1)
                rsqrt_refined(small[0:n, 8 + m:9 + m], small[0:n, 16 + m:17 + m], small[0:n, 24 + m:25 + m])
                dlink(nc.vector.scalar_tensor_tensor(out=y_t[0:n, m, :], in0=y_t[0:n, m, :], scalar=small[0:n, 24 + m:25 + m],
                                                     in1=g_post[0:n, :], op0=ALU.mult, op1=ALU.mult))
                dve.wait_ge(res_in, 16 * (m + 1))
                nc.vector.tensor_tensor(out=y_t[0:n, m, :], in0=y_t[0:n, m, :], in1=x_res[0:n, :],
                                        op=ALU.add).then_inc(y_ready, 1)
        mem_out = sem("mem_out")
        block = ctx.enter_context(nc.Block())


        N_HOST = N_A0 + IXT
        TK0 = 22
        TKR = KSEL_S // 8
        CK0 = TKR - TK0 + 3

        def run(steps):
            for _ in steps:
                pass

        def chain(*stages):
            for s in stages:
                yield from s

        def tensor_index_stage(pe):
            yield from hosted_pause(IX_PAUSE)
            yield from tensor_sample_turn(pe)
            yield from tensor_indexer(pe)

        def scalar_index_stage(act):
            yield from hosted_pause(IX_PAUSE + 1)
            yield from scalar_sample_turn(act)
            yield from scalar_indexer(act)
        IX_PAUSE = 8

        def tensor_prompt(pe):
            yield from hosted_pause(PROMPT_PAUSE)
            for m in range(MT):
                yield from tensor_prompt_turn(pe, m)
                if m:
                    yield from tensor_prompt_index(pe, m)
                yield from tensor_prompt_attend(pe, m)

        def scalar_prompt(act):
            yield from hosted_pause(PROMPT_PAUSE)
            for m in range(MT):
                yield from scalar_prompt_turn(act, m)
                if m:
                    yield from scalar_prompt_index(act, m)
                yield from scalar_prompt_attend(act, m)

        def vector_prompt(dve):
            yield from hosted_pause(PROMPT_PAUSE)
            for m in range(MT):
                yield from vector_prompt_prep(dve, m)
                yield from vector_prompt_select(dve, m)
                yield from vector_prompt_attend(dve, m)
        PROMPT_PAUSE = 5

        def tensor_rows(pe):
            yield from hosted_pause(TKR - TK0 + 1)
            yield from tensor_physical(pe)

        def vector_rows(dve):
            for i in range(TK0, TKR):
                vector_topk_sample(dve, i, i + 1)
                yield
            yield from vector_physical(dve)

        @block.sync
        def _(sp):
            sp.dma_start(ident[:, :], C["ident"]).then_inc(consts_in, 16)
            sp.dma_start(g_row[:, :], I["mem_norm"][0:1, :].broadcast_to([P, D])).then_inc(g_loaded, 16)
            sync_rows(sp, 0, NU_NORM)
            sync_tables(sp)
            sp.wait_ge(pages_in, 16)
            sp.wait_ge(chunk_used, CH * N_A0)
            sp.wait_ge(lo_taken, NGRP * NU_NORM)
            sync_idx_pages(sp, 0, NB * NPG)
            sp.wait_ge(acc_read, acc_base(N_A0))
            for t in range(NMEM // P):
                rows = slice(t * P, (t + 1) * P)
                sp.dma_start(O["p_mem_k"].rearrange("l b m h d -> (l b m) (h d)")[rows, :], mem_kv[:, t, 0:AW]).then_inc(mem_out, 16)
                sp.dma_start(O["p_mem_v"].rearrange("l b m h d -> (l b m) (h d)")[rows, :], mem_kv[:, t, AW:2 * AW]).then_inc(mem_out, 16)
            sync_index_in(sp)
            sync_sample_in(sp)
            for m in range(MT):
                sync_prompt_in(sp, m)
                sync_prompt_kv(sp, m)
                sync_prompt_out(sp, m)
                if m == 0:
                    sync_new_keys(sp)
            sp.wait_ge(*at("mixed_s"))
            store_mix_s(sp, o_s, MW)
            sync_mem_s(sp)
            sp.wait_ge(*at("mixed_c"))
            store_mix_s(sp, o_c, MW + AW)
            sp.wait_ge(mix_stored, 2 * 16 * H)
            sync_mlstm_consts(sp)
            for h in range(H):
                sync_mlstm_head(sp, h)
                if h == 0:
                    sync_mlstm_m(sp)
                sync_mlstm_out(sp, h)
            sync_mlstm_s(sp)
            sync_states(sp)
            sync_y_in(sp)
            sync_y_out(sp)
            sp.wait_ge(mem_out, 16 * 2 * NMEM // P)
            sp.wait_ge(conv_out, 48)

        @block.gpsimd
        def _(pool):
            tile_loop(pool, 0, N_B0 - 1, lambda n: gpsimd_tile(pool, n))
            gpsimd_tile(pool, N_REST)
            gathers = gpsimd_gathers(pool)
            for n in range(N_B0, N_Y0):
                gpsimd_tile(pool, n, gathers)
            run(gathers)
            tile_loop(pool, N_Y0, N_END, lambda n: gpsimd_tile(pool, n))

        @block.scalar
        def _(act):
            scalar_load(act, 0, 0)
            scalar_load(act, 0, 1)
            for u in range(NU_MEM):
                scalar_row_scale(act, u)
                run(scalar_take_hi(act, u))
            scalar_hi(act, 0, 0)
            scalar_row_scale(act, NU_MEM)
            norms = (chain(hosted_pause(1), *(scalar_take_hi(act, u) for u in range(NU_MEM, NU_NORM))), iter(()))
            for n in range(N_A0):
                scalar_tile(act, n, "mem", norms)
            run(norms[0])
            for n in range(N_A0, N_HOST):
                scalar_tile(act, n, "a")
            index = (scalar_index_stage(act), iter(()))
            for n in range(N_HOST, N_B0):
                scalar_tile(act, n, "a", index)
            run(index[0])
            steps = (chain(hosted_pause(1), scalar_prompt(act)), chain(hosted_pause(1), scalar_gather(act)))
            for n in range(N_B0, N_Y0):
                scalar_tile(act, n, "b", steps)
            run(steps[0])
            run(steps[1])
            run(scalar_mem_s(act))
            scalar_mlstm_gates(act)
            for h in range(H):
                scalar_mlstm_head(act, h)
            scalar_mlstm_s_prep(act)
            scalar_mlstm_s(act)
            for u in range(NU_NORM, NU_ALL):
                run(scalar_take_hi(act, u))
            tile_loop(act, N_Y0, N_END - 1, lambda n: scalar_tile(act, n, "y"))
            scalar_tile(act, N_END - 1, "y")
            scalar_y(act)

        @block.vector
        def _(dve):
            for u in range(NU_MEM + 1):
                vector_row_scale(dve, u)
                if u < NU_MEM:
                    vector_take_lo(dve, u)
            for u in range(NU_MEM, NU_NORM):
                vector_take_lo(dve, u)
            vector_index_prep(dve)
            vector_scores(dve)
            vector_topk_sample(dve, 0, TK0)
            vector_sample_prep(dve)
            prompt, rows = vector_prompt(dve), chain(vector_rows(dve), hosted_pause(1), vector_gather(dve))
            for _ in range(CH * NBT):
                next(prompt, None)
                next(rows, None)
                next(prompt, None)
            run(prompt)
            run(rows)
            vector_gather_out(dve)
            vector_mem_s(dve)
            vector_mlstm_gates(dve)
            for h in range(H):
                vector_mlstm_head(dve, h)
            vector_mlstm_s_prep(dve)
            vector_mlstm_s(dve)
            for u in range(NU_NORM, NU_ALL):
                vector_take_lo(dve, u)
            vector_y(dve)

        @block.tensor
        def _(pe):
            pe.wait_ge(consts_in, 16)
            for u in range(NU_MEM):
                run(tensor_turn(pe, u))
            norms = (chain(*(tensor_turn(pe, u) for u in range(NU_MEM, NU_NORM))), iter(()))
            for n in range(N_A0):
                tensor_tile(pe, n, "mem", norms)
            run(norms[0])
            for n in range(N_A0, N_HOST):
                tensor_tile(pe, n, "a")
            index = (tensor_index_stage(pe), iter(()))
            for n in range(N_HOST, N_B0):
                tensor_tile(pe, n, "a", index)
            run(index[0])
            steps = (tensor_prompt(pe), chain(tensor_rows(pe), tensor_gather(pe)))
            for n in range(N_B0, N_Y0):
                tensor_tile(pe, n, "b", steps)
            run(steps[0])
            run(steps[1])
            tensor_gather_out(pe)
            run(tensor_mem_s(pe))
            tensor_mlstm_gates(pe)
            for h in range(H):
                tensor_mlstm_head(pe, h)
            tensor_mlstm_s_prep(pe)
            tensor_mlstm_s(pe)
            for u in range(NU_NORM, NU_ALL):
                run(tensor_turn(pe, u))
            tile_loop(pe, N_Y0, N_END, lambda n: tensor_tile(pe, n, "y"))


_INS = ["x_prompt", "x_sample", "cache_attn_k", "cache_attn_v", "cache_idx_k", "state_mlstm_C", "state_mlstm_n",
        "state_mlstm_m", "state_conv", "cache_mem_k", "cache_mem_v", "page_table", "mem_prompt", "norm_pre", "w_in",
        "b_if", "conv_w", "conv_b", "mlstm_head_norm", "mem_norm", "w_mem_kv", "w_out", "norm_post"]
_OUTS = [("y_prompt", (1, 512, 2048)), ("y_sample", (8, 4, 2048)), ("p_attn_k", (1, 1, 512, 4, 128)),
         ("p_attn_v", (1, 1, 512, 4, 128)), ("p_idx_k", (1, 1, 512, 64)), ("p_C", (1, 1, 4, 256, 256)),
         ("p_n", (1, 1, 4, 256)), ("p_m", (1, 1, 4)), ("p_conv", (1, 1, 3, 2048)), ("p_mem_k", (1, 1, 256, 4, 128)),
         ("p_mem_v", (1, 1, 256, 4, 128)), ("s_attn_k", (1, 8, 4, 4, 128)), ("s_attn_v", (1, 8, 4, 4, 128)),
         ("s_idx_k", (1, 8, 4, 64)), ("s_C", (1, 8, 4, 256, 256)), ("s_n", (1, 8, 4, 256)), ("s_m", (1, 8, 4)),
         ("s_conv", (1, 8, 3, 2048))]


def constants():
    import numpy as np
    f = np.float32
    s, nb, nq, past, heads, ih = 512, 8, 4, 2048, 4, 16
    pos = np.concatenate([np.arange(s), np.tile(past + np.arange(nq), nb)]).astype(f)

    def angles(half):
        inv = np.power(f(500000.0), -np.arange(half, dtype=f) / f(half)).astype(f)
        a = (pos[:, None] * inv[None, :]).astype(f)
        return np.cos(a).astype(f), np.sin(a).astype(f)

    r = np.arange(nb * nq)
    same = (r[:, None] // nq) == (r[None, :] // nq)
    c = {"ident": np.eye(128, dtype=f), "rope": np.concatenate(angles(16) + angles(8), axis=1)}
    t = np.arange(128)
    c["causal"] = (t[:, None] <= t[None, :]).astype(f)
    c["causal_s"] = (same & (r[:, None] <= r[None, :])).astype(f)
    c["future"] = np.where(t[None, :] <= t[:, None], f(0), f(-1e30)).astype(f)
    c["future_s"] = np.where(np.arange(nq)[None, :] <= (r % nq)[:, None], f(0), f(-1e30)).astype(f)
    row_q = np.arange(ih * nq) % nq
    e = (row_q[:, None, None] == (r % nq)[None, None, :]) & (np.arange(nb)[None, :, None] == (r // nq)[None, None, :])
    c["pick"] = e.reshape(ih * nq, nb * nb * nq).astype(f)
    c["head_row"] = np.repeat(np.eye(heads, dtype=f), 128, axis=1)
    c["batch_of"] = ((r[:, None] // nq) == np.arange(nb)[None, :]).astype(f)
    carry = np.ones((heads, s + nb * nq), f)
    carry[:, 0] = 0
    carry[:, s::nq] = 0
    c["carry"], c["zeros"] = carry, np.zeros((heads, s + nb * nq), f)
    return c


def kernel(**inputs):
    import numpy as _np
    import concourse.bacc as _bacc
    from concourse import mybir as _mybir
    from concourse.bass_utils import run_bass_kernel_spmd as _run

    nc = _bacc.Bacc("TRN2", target_bir_lowering=False, num_devices=1)
    arrays, ins, consts, outs = {}, {}, {}, {}
    for name in _INS:
        a = _np.ascontiguousarray(inputs[name])
        arrays[f"in_{name}"] = a
        ins[name] = nc.dram_tensor(f"in_{name}", a.shape, _mybir.dt.from_np(a.dtype), kind="ExternalInput").ap()
    for name, a in constants().items():
        arrays[f"const_{name}"] = _np.ascontiguousarray(a)
        consts[name] = nc.dram_tensor(f"const_{name}", a.shape, _mybir.dt.float32, kind="ExternalInput").ap()
    for name, shape in _OUTS:
        outs[name] = nc.dram_tensor(f"out_{name}", shape, _mybir.dt.float32, kind="ExternalOutput").ap()
    hybrid_decoder_step(nc, ins, consts, outs)
    r = _run(nc, [arrays], core_ids=[0])
    return tuple(r.results[0][f"out_{name}"] for name, _ in _OUTS)
```

```python
import concourse.bass as bass
from concourse import mybir
from contextlib import ExitStack

def hybrid_decoder_step(nc, I, C, O):
    F32, F32R, U32, I32 = mybir.dt.float32, mybir.dt.float32r, mybir.dt.uint32, mybir.dt.int32
    ALU, ACT, AX = mybir.AluOpType, mybir.ActivationFunctionType, mybir.AxisListType

    P = 128
    D = I["x_prompt"].shape[2]
    S = I["x_prompt"].shape[1]
    NB, NQ = I["x_sample"].shape[0], I["x_sample"].shape[1]
    R = NB * NQ
    KT = D // P
    MT = S // P
    H = I["state_mlstm_C"].shape[2]
    MD = I["state_mlstm_C"].shape[3]
    MW = H * MD
    AD = I["cache_attn_k"].shape[4]
    AW = H * AD
    ID = I["cache_idx_k"].shape[3]
    IH = 16
    NMEM = I["mem_prompt"].shape[1]
    NPG = I["page_table"].shape[1]
    PG = I["cache_idx_k"].shape[2]
    PAST = NPG * PG
    NPOOL = I["cache_idx_k"].shape[1]
    KSEL_P = min(256, S // 4)
    KSEL_S = min(256, (PAST + NQ) // 4)
    W_IN = I["w_in"].shape[2]
    C_QK, C_V, C_O, C_G = 0, 2 * MW, 3 * MW, 4 * MW
    C_IF = 5 * MW
    C_AQ = C_IF + 2 * H
    C_AK, C_AV, C_AG = C_AQ + AW, C_AQ + 2 * AW, C_AQ + 3 * AW
    C_IQ = C_AQ + 4 * AW
    C_IW = C_IQ + IH * ID
    C_IK = C_IW + IH
    C_CQ = C_IK + ID
    C_CG = C_CQ + AW
    assert C_CG + AW == W_IN
    NEG, TAKEN = -1.0e30, -3.0e38
    RMS_EPS, LN_EPS = 1e-6, 1e-5

    TN = 512
    N_MEM0 = 0
    N_A0 = 2
    NA = (W_IN - C_IF) // TN
    IX0 = (C_IQ - C_IF) // TN
    IXT = -(-(C_CQ - C_IF) // TN) - IX0
    N_REST = N_A0 + NA
    HALF = (TN + (W_IN - C_IF) % TN) // 2
    assert 2 * HALF == TN + (W_IN - C_IF) % TN
    N_B0 = N_REST + 1
    NBT = C_IF // TN
    N_Y0 = N_B0 + NBT
    NY = D // TN
    N_END = N_Y0 + NY
    CH = 8
    KC = KT // CH
    RAWS = 4

    ctx = ExitStack()
    with ctx:
        def sb(name, shape, dt=F32, c=ctx):
            return c.enter_context(nc.sbuf_tensor(name, shape, dt))

        def sem(name):
            return ctx.enter_context(nc.semaphore(name))

        def scratch(name, shape):
            return nc.dram_tensor(name, shape, F32, kind="Internal").ap()

        z_p = scratch("z_prompt", [S, W_IN])
        z_s = scratch("z_sample", [2 * R, W_IN])
        mix_p = scratch("mix_prompt", [S, D])
        mix_s = scratch("mix_sample", [R, D])
        q_s = scratch("q_sample", [R, AW])
        k_s = scratch("k_sample", [R, AW])
        v_s = scratch("v_sample", [R, AW])
        iw_s = scratch("iw_sample", [R, IH])

        ident = sb("ident", [P, P])
        split = ExitStack()
        with split:
            x_hi = sb("x_hi", [P, KT, S + 2 * R], F32R, split)
            x_lo = sb("x_lo", [P, KT, S], F32R, split)
            w_hi = sb("w_hi", [P, 2, KC, TN], F32R, split)
            w_lo = sb("w_lo", [P, 2, KC, TN], F32R, split)
        X_HI_N, X_LO_N, W_N = KT * (S + 2 * R), KT * S, 2 * KC * TN
        between = sb("between", [P, X_HI_N + X_LO_N + 2 * W_N])
        w_raw = sb("w_raw", [P, RAWS, KC, TN])
        z_tile = sb("z_tile", [P, MT + 1, TN])
        mem_kv = sb("mem_kv", [P, NMEM // P, 2 * AW])
        small = sb("small", [P, 64])
        pro = ExitStack()
        with pro:
            m_hi = sb("m_hi", [P, KT, NMEM], F32R, pro)
            m_lo = sb("m_lo", [P, KT, NMEM], F32R, pro)
            x_in = sb("x_in", [P, 2, D], F32, pro)
            g_row = sb("g_row", [P, D], F32, pro)
            junk = sb("junk", [P, D], F32, pro)
        AR_N = 20960
        arena = sb("arena", [P, AR_N])
        acc = [ctx.enter_context(nc.psum_tensor(f"acc{m}", [P, TN], F32)) for m in range(MT + 1)]
        ps_a, ps_b, ps_c = (ctx.enter_context(nc.psum_tensor(f"ps_{x}", [P, TN], F32)) for x in "abc")

        POINTS = {
            "vector": (
                        "idx_ready", "pick_ready", "za_ready", "gate_in", "phys_ready", "phys_u_ready",
                        "max_s", "probs_copied", "ot_copied", "mixed_s", "cq_ready", "gate_c_in",
                        "qs_ready", "ifs_ready", "g_abs", "g_rows", "cmax", "ps_ready", "mixed_c",
                        "sm_ready", "scv_ready", "ks_scaled", "bc_copied", "qspr_ready", "pws_ready",
                        ),
            "scalar": (
                        "new_copied", "gate_ready", "exp_s", "gate_c_ready", "conv_w_c",
                        "g_exp", "g_ln", "g_we", "g_cols", "cexp", "scv_silu", "sw_exp",),
            "tensor": (
                        "new_turned", "phys_turned", "sc_turned", "probs_turned", "o_turned", "cq_turned",
                        "conv_w_t", "g_colt", "cp_turned", "bc_done", "ss_done",),
        }
        point_sem = {e: sem(f"{e}_points") for e in POINTS}
        passed = {e: 0 for e in POINTS}
        point_of = {n: (e, i) for e, names in POINTS.items() for i, n in enumerate(names)}

        def at(name):
            e, i = point_of[name]
            return point_sem[e], i + 1

        def reached(name):
            e, i = point_of[name]
            assert passed[e] == i, (name, passed[e])
            passed[e] += 1
            return point_sem[e]

        unit_rows = [P] * (NMEM // P) + [P] * MT + [R]
        NU_MEM, NU_NORM = NMEM // P, NMEM // P + MT + 1
        NU_ALL = NU_NORM + MT + 1
        unit_rows += [P] * MT + [R]
        x_loaded = [sem("x_loaded0"), sem("x_loaded1")]
        g_loaded, consts_in = sem("g_loaded"), sem("consts_in")
        (squares_done, var_done, std_done, row_scaled) = (
            sem(n) for n in ("squares_done", "var_done", "std_done", "row_scaled"))
        rows_turned, hi_taken, lo_taken = sem("rows_turned"), sem("hi_taken"), sem("lo_taken")
        dve_step, act_step = sem("dve_step"), sem("act_step")
        steps = {"dve": 0, "act": 0}

        def dlink(ins):
            steps["dve"] += 1
            ins.then_inc(dve_step, 1)
            nc.vector.wait_ge(dve_step, steps["dve"])

        def alink(ins):
            steps["act"] += 1
            ins.then_inc(act_step, 1)
            nc.scalar.wait_ge(act_step, steps["act"])

        def unit_source(u):
            if u < NU_MEM:
                return I["mem_prompt"][0, u * P:(u + 1) * P, :]
            if u < NU_NORM - 1:
                return I["x_prompt"][0, (u - NU_MEM) * P:(u - NU_MEM + 1) * P, :]
            if u == NU_NORM - 1:
                return I["x_sample"].rearrange("b t d -> (b t) d")
            if u < NU_ALL - 1:
                return mix_p[(u - NU_NORM) * P:(u - NU_NORM + 1) * P, :]
            return mix_s

        def unit_dest(u, k0, n):
            ks = slice(k0, k0 + n)
            if u < NU_MEM:
                return m_hi[:, ks, u * P:(u + 1) * P], m_lo[:, ks, u * P:(u + 1) * P]
            i = u - NU_MEM if u < NU_NORM else u - NU_NORM
            if i < MT:
                return x_hi[:, ks, i * P:(i + 1) * P], x_lo[:, ks, i * P:(i + 1) * P]
            return x_hi[:, ks, S:S + R], x_hi[:, ks, S + R:S + 2 * R]

        def rows_buffer(u):
            return x_in[:, u % 2, :] if u < NU_NORM else y_in(u)

        TG = 4
        NGRP = KT // TG

        def sync_rows(sp, u0, u1):
            for u in range(u0, u1):
                if u >= 2:
                    sp.wait_ge(rows_turned, NGRP * (u - 1))
                sp.dma_start(rows_buffer(u)[0:unit_rows[u], :], unit_source(u)).then_inc(x_loaded[u % 2], 16)
                if u == 1:
                    sp.wait_ge(row_scaled, NU_MEM)
                    sp.dma_start(g_row[:, :], I["norm_pre"][0:1, :].broadcast_to([P, D])).then_inc(g_loaded, 16)

        def scalar_row_scale(act, u):
            n = unit_rows[u]
            act.wait_ge(x_loaded[u % 2], 16 * (u // 2 + 1))
            if u:
                act.wait_ge(squares_done, u)
            nc.scalar.activation(junk[0:n, :], rows_buffer(u)[0:n, :], ACT.Square,
                                 accum_out=small[0:n, u:u + 1]).then_inc(squares_done, 1)
            act.wait_ge(var_done, u + 1)
            nc.scalar.activation(small[0:n, 16 + u:17 + u], small[0:n, 8 + u:9 + u], ACT.Sqrt).then_inc(std_done, 1)

        def rsqrt_refined(var, root, out):
            dlink(nc.vector.reciprocal(out, root))
            if out.shape[-1] == 1:
                dlink(nc.vector.scalar_tensor_tensor(out=root, in0=out, scalar=out, in1=var, op0=ALU.mult, op1=ALU.mult))
            else:
                dlink(nc.vector.tensor_tensor(out=root, in0=out, in1=out, op=ALU.mult))
                dlink(nc.vector.tensor_tensor(out=root, in0=root, in1=var, op=ALU.mult))
            dlink(nc.vector.tensor_scalar(root, root, -0.5, 1.5, ALU.mult, ALU.add))
            dlink(nc.vector.tensor_tensor(out=out, in0=out, in1=root, op=ALU.mult))

        def vector_row_scale(dve, u):
            n = unit_rows[u]
            dve.wait_ge(squares_done, u + 1)
            nc.vector.tensor_scalar(small[0:n, 8 + u:9 + u], small[0:n, u:u + 1], 1.0 / D, RMS_EPS,
                                    ALU.mult, ALU.add).then_inc(var_done, 1)
            dve.wait_ge(std_done, u + 1)
            rsqrt_refined(small[0:n, 8 + u:9 + u], small[0:n, 16 + u:17 + u], small[0:n, 24 + u:25 + u])
            dve.wait_ge(g_loaded, 16 if u < NU_MEM else 32)
            nc.vector.scalar_tensor_tensor(out=rows_buffer(u)[0:n, :], in0=rows_buffer(u)[0:n, :],
                                           scalar=small[0:n, 24 + u:25 + u], in1=g_row[0:n, :],
                                           op0=ALU.mult, op1=ALU.mult).then_inc(row_scaled, 1)

        def tensor_turn(pe, u):
            n = unit_rows[u]
            if u < NU_NORM:
                pe.wait_ge(row_scaled, u + 1)
            else:
                pe.wait_ge(x_loaded[u % 2], 16 * (u // 2 + 1))
            for j in range(NGRP):
                g = NGRP * u + j
                if g >= 2:
                    pe.wait_ge(lo_taken, g - 1)
                if j:
                    yield
                bank = (ps_a, ps_b)[g % 2]
                for i in range(TG):
                    k = j * TG + i
                    last = nc.tensor.transpose(bank[:, i * n:(i + 1) * n], rows_buffer(u)[0:n, k * P:(k + 1) * P],
                                               ident[0:n, 0:n])
                last.then_inc(rows_turned, 1)
            yield

        def scalar_take_hi(act, u):
            n = unit_rows[u]
            if u == NU_NORM:
                act.wait_ge(chunk_used, CH * N_Y0)
                act.wait_ge(sn_out, 32)
                for i in range(NCR):
                    act.wait_ge(cst_out[i], 16 * len(range(i, HB, NCR)))
            for j in range(NGRP):
                g = NGRP * u + j
                bank = (ps_a, ps_b)[g % 2][:, 0:TG * n].rearrange("p (k r) -> p k r", k=TG)
                act.wait_ge(rows_turned, g + 1)
                nc.scalar.copy(unit_dest(u, j * TG, TG)[0], bank).then_inc(hi_taken, 1)
                if j == 1 and NU_MEM <= u < NU_NORM - 1:
                    scalar_row_scale(act, u + 1)
                yield

        def vector_take_lo(dve, u):
            n = unit_rows[u]
            for j in range(NGRP):
                if j == 2 and NU_MEM <= u < NU_NORM - 1:
                    vector_row_scale(dve, u + 1)
                g = NGRP * u + j
                bank = (ps_a, ps_b)[g % 2][:, 0:TG * n].rearrange("p (k r) -> p k r", k=TG)
                hi, lo = unit_dest(u, j * TG, TG)
                dve.wait_ge(hi_taken, g + 1)
                nc.vector.tensor_tensor(out=lo, in0=bank, in1=hi.bitcast(F32), op=ALU.subtract).then_inc(lo_taken, 1)

        w_loaded = [sem(f"w_loaded{s}") for s in range(RAWS)]
        chunk_hi, chunk_lo, chunk_used = sem("chunk_hi"), sem("chunk_lo"), sem("chunk_used")
        acc_ready, acc_read = sem("acc_ready"), sem("acc_read")
        z_stored = [sem(f"z_stored{m}") for m in range(MT + 1)]

        def width(n):
            return HALF if isinstance(n, int) and n in (N_REST - 1, N_REST) else TN

        def acc_base(n):
            return (MT + 1) * n - (MT + 1 - NU_MEM) * N_A0 if not isinstance(n, int) or n >= N_A0 else NU_MEM * n

        w_mem_v = I["w_mem_kv"][0].rearrange("(k p) n -> p k n", p=P)
        w_in_v = I["w_in"][0].rearrange("(k p) n -> p k n", p=P)
        w_out_v = I["w_out"][0].rearrange("(k p) n -> p k n", p=P)

        def tile_source(n):
            if not isinstance(n, int) or n >= N_Y0:
                return w_out_v, TN * (n - N_Y0)
            if n < N_A0:
                return w_mem_v, TN * n
            if n >= N_B0:
                return w_in_v, TN * (n - N_B0)
            i = n - N_A0
            if n == N_REST:
                return w_in_v, W_IN - HALF
            return w_in_v, C_IF + TN * (i + IX0 if i < IXT else i - IXT if i < IX0 + IXT else i)

        def scalar_load(act, n, c):
            if c >= CH:
                n, c = n + 1, c - CH
            if isinstance(n, int) and n >= N_END:
                return
            src, col = tile_source(n)
            w = width(n)
            cols = slice(col, col + w) if isinstance(n, int) else bass.ds(col, w)
            s = c % RAWS
            act.dma_start(w_raw[:, s, :, 0:w], src[:, c * KC:(c + 1) * KC, cols]).then_inc(w_loaded[s], 16)

        def scalar_hi(act, n, c, w=TN):
            j = CH * n + c
            if not (isinstance(n, int) and j < 2):
                act.wait_ge(chunk_used, j - 1)
            scalar_load(act, n, c + 2)
            act.wait_ge(w_loaded[c % RAWS], 16 * (CH // RAWS * n + c // RAWS + 1))
            nc.scalar.copy(w_hi[:, c % 2, :, 0:w], w_raw[:, c % RAWS, :, 0:w]).then_inc(chunk_hi, 1)

        def gpsimd_lo(pool, n, c, w=TN):
            pool.wait_ge(chunk_hi, CH * n + c + 1)
            nc.gpsimd.tensor_tensor(out=w_lo[:, c % 2, :, 0:w], in0=w_raw[:, c % RAWS, :, 0:w],
                                    in1=w_hi[:, c % 2, :, 0:w].bitcast(F32), op=ALU.subtract).then_inc(chunk_lo, 1)

        NO_STEPS = (iter(()), iter(()))

        def hosted_pause(pieces):
            for _ in range(pieces):
                yield

        def tensor_tile(pe, n, kind, steps=NO_STEPS, often=False):
            w = width(n)
            nm = NU_MEM if kind == "mem" else MT + 1
            for c in range(CH):
                pe.wait_ge(chunk_lo, CH * n + c + 1)
                if isinstance(n, int) and n == 0 and c == 0:
                    pe.wait_ge(lo_taken, NGRP * NU_MEM)
                if isinstance(n, int) and n == N_A0 and c == 0:
                    pe.wait_ge(lo_taken, NGRP * NU_NORM)
                if isinstance(n, int) and n == N_Y0 and c == 0:
                    pe.wait_ge(lo_taken, NGRP * NU_ALL)
                for m in range(nm):
                    if c == 0 and not (isinstance(n, int) and n == 0):
                        before = acc_base(n) if not (isinstance(n, int) and n == N_A0) else acc_base(N_A0)
                        back = nm if not (isinstance(n, int) and n == N_A0) else NU_MEM
                        if m < back:
                            pe.wait_ge(acc_read, before - back + m + 1)
                    for i in range(KC):
                        k = c * KC + i
                        first, end = (k == 0), (k == KT - 1)
                        wh, wl = w_hi[:, c % 2, i, 0:w], w_lo[:, c % 2, i, 0:w]
                        if m == MT:
                            xs = x_hi[:, k, S:S + 2 * R]
                            nc.tensor.matmul(acc[m][0:2 * R, 0:w], xs, wh, start=first, stop=False)
                            last = nc.tensor.matmul(acc[m][0:2 * R, 0:w], xs, wl, start=False, stop=end)
                        else:
                            hi_t, lo_t = (m_hi, m_lo) if kind == "mem" else (x_hi, x_lo)
                            xh, xl = hi_t[:, k, m * P:(m + 1) * P], lo_t[:, k, m * P:(m + 1) * P]
                            nc.tensor.matmul(acc[m][:, 0:w], xh, wh, start=first, stop=False)
                            nc.tensor.matmul(acc[m][:, 0:w], xh, wl, start=False, stop=False)
                            last = nc.tensor.matmul(acc[m][:, 0:w], xl, wh, start=False, stop=end)
                    if m == nm - 1:
                        last.then_inc(chunk_used, 1)
                    if c == CH - 1 and m < nm - 1:
                        last.then_inc(acc_ready, 1)
                    if m == nm - 1:
                        next(steps[1], None)
                    if m == (nm - 1) // 2 or m == nm - 1 or (often and m == 0):
                        next(steps[0], None)

        def scalar_evacuate(act, n, kind):
            w = width(n)
            nm = NU_MEM if kind == "mem" else MT + 1
            for m in range(nm):
                rows = P if m < MT else 2 * R
                if m < nm - 1:
                    act.wait_ge(acc_ready, acc_ready_base(n) + m + 1)
                else:
                    act.wait_ge(chunk_used, CH * n + CH)
                if kind == "mem":
                    nc.scalar.copy(mem_kv[:, m, n * TN:(n + 1) * TN], acc[m][:, :]).then_inc(acc_read, 1)
                    continue
                if kind == "y":
                    if m < MT:
                        act.wait_ge(acc_read, acc_base(n) + m)
                        nc.scalar.activation(z_tile[:, 0, :], acc[m][:, :], ACT.Square,
                                             accum_out=y_sum[:, m, bass.ds(n - N_Y0, 1)])
                    nc.scalar.copy(y_rows(m)[0:rows, bass.ds((n - N_Y0) * TN, TN)],
                                   acc[m][0:rows, :]).then_inc(acc_read, 1)
                    continue
                if not (isinstance(n, int) and n == N_A0):
                    act.wait_ge(z_stored[m], 16 * (n - N_A0))
                nc.scalar.copy(z_tile[0:rows, m, 0:w], acc[m][0:rows, 0:w]).then_inc(acc_read, 1)
                act.wait_ge(acc_read, acc_base(n) + m + 1)
                cols = slice(tile_source(n)[1], tile_source(n)[1] + w)
                dst = z_p[m * P:(m + 1) * P, cols] if m < MT else z_s[:, cols]
                act.dma_start(dst, z_tile[0:rows, m, 0:w]).then_inc(z_stored[m], 16)

        def acc_ready_base(n):
            if isinstance(n, int) and n < N_A0:
                return (NU_MEM - 1) * n
            return MT * n - (MT + 1 - NU_MEM) * N_A0

        def tile_loop(eng, n0, n1, body):
            body(n0)
            if n1 - n0 > 2:
                with eng.Fori(n0 + 1, n1) as n:
                    body(n)
            elif n1 - n0 == 2:
                body(n0 + 1)

        def scalar_tile(act, n, kind, steps=NO_STEPS, often=False):
            for c in range(1, CH + 1):
                if c < CH:
                    scalar_hi(act, n, c, width(n))
                elif not (isinstance(n, int) and n == N_END - 1):
                    scalar_hi(act, n + 1, 0, width(n + 1))
                next(steps[1], None)
                for _ in range(3 if often else 2):
                    next(steps[0], None)
            scalar_evacuate(act, n, kind)

        def gpsimd_tile(pool, n, steps=iter(())):
            for c in range(CH):
                gpsimd_lo(pool, n, c, width(n))
                next(steps, None)

        def place(off, shape, rows=P):
            n = 1
            for s in shape:
                n *= s
            assert off + n <= AR_N
            v = arena[0:rows, off:off + n]
            if len(shape) == 1:
                return v
            names = "abcd"[:len(shape)]
            return v.rearrange(f"p ({' '.join(names)}) -> p {' '.join(names)}", **dict(zip(names, shape)))

        ZW = W_IN - C_IF
        zo = lambda c: c - C_IF
        IK_OFF = 0
        idx_pages = place(IK_OFF, [NB * NPG, ID])
        ZA_OFF = NB * NPG * ID
        z_a = place(ZA_OFF, [ZW], R)
        W_OFF = ZA_OFF + ZW
        z_low = place(W_OFF, [ZW], R)
        aq_low = place(ZA_OFF - (C_IQ - C_AQ), [C_IQ - C_AQ], R)
        score = place(W_OFF, [PAST + NQ], R)
        X_OFF = W_OFF + ZW
        ik_t = place(X_OFF, [2, TN], ID)
        relu_sc = place(X_OFF + 1024, [2, TN], IH * NQ)
        w_pick = place(X_OFF + 2048, [NB, R], IH * NQ)
        pick = place(X_OFF + 2304, [NB, R], IH * NQ)
        iq_t = place(X_OFF + 2560, [NB, IH, NQ], ID)
        ik_new = place(X_OFF + 3072, [R], ID)
        w_rows = place(X_OFF + 3104, [NB], IH * NQ)
        rope_tmp = [place(X_OFF + 3112 + 128 * i, [128]) for i in range(4)]
        XS_OFF = X_OFF + 3112 + 512
        sel_idx = place(XS_OFF, [KSEL_S], R).bitcast(U32)
        sel_f = place(XS_OFF + 256, [KSEL_S], R)
        phys_f = place(XS_OFF + 512, [KSEL_S], R)
        ZS_END = XS_OFF + 768
        keep = sb("keep", [P, 1056])
        rope_tab = keep[:, 0:240].rearrange("p (m c) -> p m c", m=MT + 1)
        fut = keep[:, 240:368]
        fut_s = keep[0:R, 368:372]
        top8 = keep[0:R, 372:380]
        phys_u = keep[:, 384:448].bitcast(U32).rearrange("p (c r) -> p c r", c=2)
        pages_i = keep[0:R, 448:464].bitcast(I32)
        pages_f = keep[0:R, 464:480]
        page_step = keep[0:R, 480:496]
        new_pen = keep[0:R, 496:500]
        page_list = keep[0:1, 512:640].bitcast(I32)
        pen_q = keep[:, 640:900]
        soft = keep[:, 900:912]
        gate_s = keep[:, 912:1040]

        POOL_PAGES = 2 * CH * IXT
        idx_pool = sem("idx_pool")
        pages_in, tables_in, idx_loaded = sem("pages_in"), sem("tables_in"), sem("idx_loaded")
        za_in, za_stored, wrows_in = sem("za_in"), sem("za_stored"), sem("wrows_in")

        (idx_turned, ikt_copied, scored, relu_done, weighted, score_copied) = (
            sem(n) for n in ("idx_turned", "ikt_copied", "scored", "relu_done", "weighted", "score_copied"))
        n_idx_units = NB * (PAST // TN)
        PPC = TN // PG

        def sync_tables(sp):
            for m in range(MT):
                sp.dma_start(rope_tab[:, m, :], C["rope"][m * P:(m + 1) * P, :]).then_inc(tables_in, 16)
            sp.dma_start(rope_tab[0:R, MT, :], C["rope"][S:S + R, :]).then_inc(tables_in, 16)
            sp.dma_start(fut, C["future"]).then_inc(tables_in, 16)
            sp.dma_start(fut_s, C["future_s"]).then_inc(tables_in, 16)
            sp.dma_start(pages_i, I["page_table"].unsqueeze(1).broadcast_to([NB, NQ, NPG])).then_inc(tables_in, 16)
            sp.dma_start(page_list, I["page_table"].rearrange("(o b) n -> o (b n)", o=1)).then_inc(pages_in, 16)
        N_TABLES = MT + 4

        def sync_idx_pages(sp, i0, n):
            with sp.Fori(0, n) as j:
                page = sp.value_load(page_list[:, bass.ds(i0 + j, 1)], min_val=0, max_val=NPOOL - 1)
                sp.dma_start(arena[:, bass.ds(IK_OFF + (i0 + j) * ID, ID)],
                             I["cache_idx_k"][0, bass.ds(page, 1), :, :].rearrange("o t d -> (o t) d")
                             ).then_inc(idx_loaded, 16)

        def gpsimd_page(pool, i):
            page = pool.value_load(page_list[:, bass.ds(i, 1)], min_val=0, max_val=NPOOL - 1)
            pool.dma_start(arena[:, bass.ds(IK_OFF + i * ID, ID)],
                           I["cache_idx_k"][0, bass.ds(page, 1), :, :].rearrange("o t d -> (o t) d")).then_inc(idx_pool, 16)

        def sync_index_in(sp):
            sp.wait_ge(z_stored[MT], 16 * IXT)
            sp.dma_start(z_a[:, zo(C_IQ):zo(C_CQ)], z_s[0:R, C_IQ:C_CQ]).then_inc(za_in, 16)
            sp.dma_start(z_low[:, 0:C_CQ - C_IQ], z_s[R:2 * R, C_IQ:C_CQ]).then_inc(za_in, 16)
            sp.dma_start(pick, C["pick"].rearrange("p (b r) -> p b r", b=NB)).then_inc(za_in, 16)
            sp.wait_ge(*at("idx_ready"))
            for dst, c, w in ((O["s_idx_k"].rearrange("o b t d -> (o b t) d"), C_IK, ID), (iw_s, C_IW, IH)):
                sp.dma_start(dst, z_a[:, zo(c):zo(c) + w]).then_inc(za_stored, 16)
            sp.wait_ge(za_stored, 16 * 2)
            wr = iw_s.rearrange("(b q) h -> h q b", q=NQ)
            for h in range(IH):
                sp.dma_start(w_rows[h * NQ:(h + 1) * NQ, :], wr[h], allow_slow_non_contiguous=True).then_inc(wrows_in, 16)

        def sync_sample_in(sp):
            sp.wait_ge(z_stored[MT], 16 * (N_B0 - N_A0))
            sp.wait_ge(idx_turned, n_idx_units)
            sp.dma_start(z_a[:, zo(C_AQ):zo(C_IQ)], z_s[0:R, C_AQ:C_IQ]).then_inc(za_in, 16)
            sp.dma_start(aq_low, z_s[R:2 * R, C_AQ:C_IQ]).then_inc(za_in, 16)
            sp.wait_ge(*at("gate_in"))
            for dst, c, w in ((O["s_attn_k"].rearrange("o b t h d -> (o b t) (h d)"), C_AK, AW),
                              (O["s_attn_v"].rearrange("o b t h d -> (o b t) (h d)"), C_AV, AW),
                              (q_s, C_AQ, AW), (k_s, C_AK, AW), (v_s, C_AV, AW)):
                sp.dma_start(dst, z_a[:, zo(c):zo(c) + w]).then_inc(za_stored, 16)
            sp.wait_ge(za_stored, 16 * 7)

        def rotate(rows, cols_ap, heads, width_, tab, half):
            x = cols_ap.rearrange("p (h d) -> p h d", h=heads)
            x1, x2 = x[:, :, 0:half], x[:, :, half:2 * half]
            t = [r[0:rows, 0:heads * half].rearrange("p (h d) -> p h d", h=heads) for r in rope_tmp]
            base = 0 if half == 16 else 32
            cos = tab[:, base:base + half].unsqueeze(1).broadcast_to([rows, heads, half])
            sin = tab[:, base + half:base + 2 * half].unsqueeze(1).broadcast_to([rows, heads, half])
            nc.vector.tensor_tensor(out=t[0], in0=x1, in1=cos, op=ALU.mult)
            nc.vector.tensor_tensor(out=t[1], in0=x2, in1=sin, op=ALU.mult)
            nc.vector.tensor_tensor(out=t[2], in0=x1, in1=sin, op=ALU.mult)
            dlink(nc.vector.tensor_tensor(out=t[3], in0=x2, in1=cos, op=ALU.mult))
            nc.vector.tensor_tensor(out=x1, in0=t[0], in1=t[1], op=ALU.subtract)
            return nc.vector.tensor_tensor(out=x2, in0=t[2], in1=t[3], op=ALU.add)

        def vector_index_prep(dve):
            dve.wait_ge(za_in, 48)
            dve.wait_ge(tables_in, 16 * N_TABLES)
            part = z_a[:, zo(C_IQ):zo(C_CQ)]
            dlink(nc.vector.tensor_tensor(out=part, in0=part, in1=z_low[:, 0:C_CQ - C_IQ], op=ALU.add))
            tab = rope_tab[0:R, MT, :]
            dlink(rotate(R, z_a[:, zo(C_IQ):zo(C_IQ) + IH * ID], IH, ID, tab, ID // 8))
            rotate(R, z_a[:, zo(C_IK):zo(C_IK) + ID], 1, ID, tab, ID // 8).then_inc(reached("idx_ready"), 1)
            dve.wait_ge(wrows_in, 16 * IH)
            nc.vector.scalar_tensor_tensor(out=w_pick, in0=pick, scalar=float(ID ** -0.5 * IH ** -0.5),
                                           in1=w_rows.unsqueeze(2).broadcast_to([IH * NQ, NB, R]),
                                           op0=ALU.mult, op1=ALU.mult).then_inc(reached("pick_ready"), 1)

        def vector_sample_prep(dve):
            dve.wait_ge(za_in, 16 * 5)
            part = z_a[:, zo(C_AQ):zo(C_IQ)]
            dlink(nc.vector.tensor_tensor(out=part, in0=part, in1=aq_low, op=ALU.add))
            tab = rope_tab[0:R, MT, :]
            dlink(rotate(R, z_a[:, zo(C_AQ):zo(C_AQ) + AW], H, AD, tab, AD // 8))
            rotate(R, z_a[:, zo(C_AK):zo(C_AK) + AW], H, AD, tab, AD // 8).then_inc(reached("za_ready"), 1)
            for h in range(H):
                c = zo(C_AG) + h * AD
                last = nc.vector.tensor_copy(gate_s[h * R:(h + 1) * R, :], z_a[:, c:c + AD])
            last.then_inc(reached("gate_in"), 1)

        def tensor_sample_turn(pe):
            pe.wait_ge(*at("idx_ready"))
            for h in range(IH):
                c = zo(C_IQ) + h * ID
                nc.tensor.transpose(ps_a[0:ID, h * R:(h + 1) * R], z_a[:, c:c + ID], ident[0:R, 0:R])
            nc.tensor.transpose(ps_b[0:ID, 0:R], z_a[:, zo(C_IK):zo(C_IK) + ID], ident[0:R, 0:R]).then_inc(reached("new_turned"), 1)
            yield

        def scalar_sample_turn(act):
            act.wait_ge(*at("new_turned"))
            nc.scalar.copy(iq_t, ps_a[0:ID, :].rearrange("p (h b q) -> p b h q", h=IH, b=NB))
            nc.scalar.copy(ik_new, ps_b[0:ID, 0:R]).then_inc(reached("new_copied"), 1)
            yield

        def tensor_indexer(pe):
            pe.wait_ge(*at("new_copied"))
            pe.wait_ge(*at("pick_ready"))
            pe.wait_ge(idx_loaded, 16 * (NB * NPG - POOL_PAGES))
            pe.wait_ge(idx_pool, 16 * POOL_PAGES)
            n = n_idx_units

            def turn(u):
                c, b = u // NB, u % NB
                if u:
                    pe.wait_ge(ikt_copied, u)
                for j in range(PPC):
                    last = nc.tensor.transpose(ps_a[0:ID, j * PG:(j + 1) * PG],
                                               idx_pages[:, b * NPG + c * PPC + j, :], ident[:, :])
                last.then_inc(idx_turned, 1)

            def score_of(u):
                b = u % NB
                pe.wait_ge(ikt_copied, u + 1)
                if u:
                    pe.wait_ge(relu_done, u)
                nc.tensor.matmul(ps_b[0:IH * NQ, :], iq_t[:, b, :, :].rearrange("p h q -> p (h q)"), ik_t[:, u % 2, :],
                                 start=True, stop=True).then_inc(scored, 1)

            def weigh(u):
                c, b = u // NB, u % NB
                pe.wait_ge(relu_done, u + 1)
                if b == 0 and c:
                    pe.wait_ge(score_copied, c)
                nc.tensor.matmul(ps_c[0:R, :], w_pick[:, b, :], relu_sc[:, u % 2, :],
                                 start=b == 0, stop=b == NB - 1).then_inc(weighted, 1)

            turn(0)
            for u in range(n + 1):
                if u + 1 < n:
                    turn(u + 1)
                if u < n:
                    score_of(u)
                if u:
                    weigh(u - 1)
                yield
            pe.wait_ge(relu_done, n)
            for b in range(NB):
                last = nc.tensor.matmul(ps_b[0:IH * NQ, b * NQ:(b + 1) * NQ], iq_t[:, b, :, :].rearrange("p h q -> p (h q)"),
                                        ik_new[:, b * NQ:(b + 1) * NQ], start=True, stop=True)
            last.then_inc(scored, 1)
            pe.wait_ge(relu_done, n + 1)
            pe.wait_ge(score_copied, n // NB)
            for b in range(NB):
                last = nc.tensor.matmul(ps_c[0:R, 0:NQ], w_pick[:, b, :], relu_sc[:, n % 2, b * NQ:(b + 1) * NQ],
                                        start=b == 0, stop=b == NB - 1)
            last.then_inc(weighted, 1)
            yield

        def scalar_indexer(act):
            n = n_idx_units

            def copy_keys(u):
                act.wait_ge(idx_turned, u + 1)
                if u >= 2:
                    act.wait_ge(scored, u - 1)
                nc.scalar.copy(ik_t[:, u % 2, :], ps_a[0:ID, :]).then_inc(ikt_copied, 1)

            def relu(u, w):
                act.wait_ge(scored, u + 1)
                if u >= 2:
                    act.wait_ge(weighted, u - 1)
                nc.scalar.activation(relu_sc[:, u % 2, 0:w], ps_b[0:IH * NQ, 0:w], ACT.Relu).then_inc(relu_done, 1)

            copy_keys(0)
            for u in range(n):
                if u + 1 < n:
                    copy_keys(u + 1)
                relu(u, TN)
                yield
            yield
            relu(n, R)
            yield

        def vector_scores(dve):
            for c in range(n_idx_units // NB):
                dve.wait_ge(weighted, NB * (c + 1))
                nc.vector.tensor_copy(score[:, c * TN:(c + 1) * TN], ps_c[0:R, :]).then_inc(score_copied, 1)
            dve.wait_ge(weighted, n_idx_units + 1)
            dlink(nc.vector.tensor_tensor(out=score[:, PAST:PAST + NQ], in0=ps_c[0:R, 0:NQ], in1=fut_s, op=ALU.add))

        def vector_topk_sample(dve, i0, i1):
            for i in range(i0, i1):
                dlink(nc.vector.max(top8, score))
                dlink(nc.vector.max_index(sel_idx[:, 8 * i:8 * i + 8], top8, score))
                dlink(nc.vector.match_replace(score, top8, score, TAKEN))

        def vector_physical(dve):
            dlink(nc.vector.tensor_copy(sel_f, sel_idx))
            dlink(nc.vector.tensor_copy(pages_f, pages_i))
            nc.vector.tensor_scalar(pen_q[0:R, 0:KSEL_S], sel_f, float(PAST), NEG, ALU.is_ge, ALU.mult)
            nc.vector.tensor_scalar(pen_q[0:R, KSEL_S:KSEL_S + NQ], score[:, PAST:PAST + NQ], TAKEN, NEG,
                                    ALU.not_equal, ALU.mult)
            dlink(nc.vector.tensor_scalar(sel_f, sel_f, float(PAST - 1), None, ALU.min))
            dlink(nc.vector.tensor_tensor(out=page_step[:, 1:NPG], in0=pages_f[:, 1:NPG], in1=pages_f[:, 0:NPG - 1],
                                          op=ALU.subtract))
            dlink(nc.vector.tensor_scalar(page_step[:, 1:NPG], page_step[:, 1:NPG], -1.0, float(PG), ALU.add, ALU.mult))
            dlink(nc.vector.tensor_scalar(page_step[:, 0:1], pages_f[:, 0:1], float(PG), None, ALU.mult))
            dlink(nc.vector.tensor_scalar(phys_f, sel_f, page_step[:, 0:1], None, ALU.add))
            for h in range(1, H):
                nc.vector.tensor_copy(pen_q[h * R:(h + 1) * R, :], pen_q[0:R, :])
            for j in range(1, NPG):
                dlink(nc.vector.tensor_scalar(sel_term, sel_f, float(PG * j), page_step[:, j:j + 1], ALU.is_ge, ALU.mult))
                add = nc.vector.tensor_tensor(out=phys_f, in0=phys_f, in1=sel_term, op=ALU.add)
                if j < NPG - 1:
                    dlink(add)
            add.then_inc(reached("phys_ready"), 1)
            yield
            dve.wait_ge(*at("phys_turned"))
            nc.vector.tensor_copy(phys_u, ps_c[:, PC_O:PC_O + 2 * R].rearrange("p (c r) -> p c r", c=2)).then_inc(reached("phys_u_ready"), 1)
            yield

        sel_term = place(W_OFF + PAST + NQ, [KSEL_S], R)

        def tensor_physical(pe):
            pe.wait_ge(*at("phys_ready"))
            prompt_sums_read(pe)
            for c in range(2):
                last = nc.tensor.transpose(ps_c[:, PC_O + c * R:PC_O + (c + 1) * R], phys_f[:, c * P:(c + 1) * P], ident[0:R, 0:R])
            last.then_inc(reached("phys_turned"), 1)
            pe.wait_ge(*at("phys_u_ready"))
            yield

        GS = 2
        SC = KSEL_S // P
        VS = 3
        got = place(W_OFF, [GS, SC, AW])
        ot = place(W_OFF, [P])
        G0 = W_OFF + GS * SC * AW
        g_sc = place(G0, [SC, H, R])
        probs_t = place(G0, [SC, H, R])
        q_bc = place(G0 + 256, [GS, AW])
        nt = place(G0 + 256, [NQ, AD])
        lg = place(G0 + 256 + AW, [KSEL_S + NQ])
        got_v = [got[:, 0, :, :], got[:, 1, :, :], place(G0 + 256, [SC, AW])]
        kn = place(G0 + 256 + GS * AW, [NQ, AD])
        qn = place(G0 + 768 + GS * AW, [AD])
        o_s = place(G0 + 896 + GS * AW, [AD])
        assert G0 + 1024 + GS * AW <= X_OFF
        pr = place(XS_OFF, [KSEL_S + NQ])
        vn = place(XS_OFF + KSEL_S + NQ + 4, [NQ, AD])
        PC_T, PC_O = P, 3 * P
        got_in = [sem(f"got_in{i}") for i in range(VS)]
        qbc_in = [sem(f"qbc_in{i}") for i in range(GS)]
        (row_scored, new_in, probs_s) = (
            sem(n) for n in ("row_scored", "new_in", "probs_s"))
        (row_summed, mix_stored) = (
            sem(n) for n in ("row_summed", "mix_stored"))
        k_rows = I["cache_attn_k"].rearrange("o n t h d -> (o n t) (h d)")
        v_rows = I["cache_attn_v"].rearrange("o n t h d -> (o n t) (h d)")

        def gpsimd_gather(pool, r, values):
            slots = VS if values else GS
            s = r % slots
            if not values and r == 0:
                pool.wait_ge(*at("phys_u_ready"))
            if values and r == 0:
                pool.wait_ge(row_scored, R)
            if values and r == GS:
                pool.wait_ge(*at("exp_s"))
            if r >= slots:
                pool.wait_ge(row_summed if values else row_scored, r - slots + 1)
            if not values:
                pool.dma_start(q_bc[:, s, :], q_s[r:r + 1, :].broadcast_to([P, AW])).then_inc(qbc_in[s], 16)
            for c in range(SC):
                pool.indirect_dma_start(out=got_v[s][:, c, :], out_offset=None, in_=v_rows if values else k_rows,
                                        in_offset=bass.IndirectOffsetOnAxis(ap=phys_u[:, c, r:r + 1], axis=0)
                                        ).then_inc(got_in[s], 16)

        def got_count(r, values):
            if not values:
                return 16 * SC * (r // GS + 1)
            return 16 * SC * (r // VS + 1 + (R // GS if r % VS < GS else 0))

        def sync_new_keys(sp):
            sp.wait_ge(*at("phys_u_ready"))
            for h in range(H):
                for dst, src in ((kn, k_s), (vn, v_s)):
                    for b in range(NB):
                        v = src[b * NQ:(b + 1) * NQ, h * AD:(h + 1) * AD].unsqueeze(0)
                        sp.dma_start(dst[h * R + b * NQ:h * R + (b + 1) * NQ, :, :],
                                     v.broadcast_to([NQ, NQ, AD])).then_inc(new_in, 16)
                sp.dma_start(qn[h * R:(h + 1) * R, :], q_s[:, h * AD:(h + 1) * AD]).then_inc(new_in, 16)

        def vector_row_scores(dve, r):
            s = r % GS
            dve.wait_ge(got_in[s], got_count(r, False))
            dve.wait_ge(qbc_in[s], 16 * (r // GS + 1))
            dlink(nc.vector.tensor_tensor(out=got[:, s, :, :], in0=got[:, s, :, :],
                                          in1=q_bc[:, s, :].unsqueeze(1).broadcast_to([P, SC, AW]), op=ALU.mult))
            nc.vector.tensor_reduce(out=g_sc[:, :, :, r], in_=got[:, s, :, :].rearrange("p c (h d) -> p c h d", h=H),
                                    axis=AX.X, op=ALU.add).then_inc(row_scored, 1)

        def vector_gather(dve):
            for r in range(R):
                vector_row_scores(dve, r)
                yield
            dve.wait_ge(new_in, 16 * H * (2 * NB + 1))
            dlink(nc.vector.tensor_tensor(out=nt, in0=kn, in1=qn.unsqueeze(1).broadcast_to([P, NQ, AD]), op=ALU.mult))
            dlink(nc.vector.tensor_reduce(out=lg[:, KSEL_S:KSEL_S + NQ], in_=nt, axis=AX.X, op=ALU.add))
            nc.vector.scalar_tensor_tensor(out=lg[:, KSEL_S:KSEL_S + NQ], in0=lg[:, KSEL_S:KSEL_S + NQ],
                                           scalar=AD ** -0.5, in1=pen_q[:, KSEL_S:KSEL_S + NQ], op0=ALU.mult, op1=ALU.add)
            dve.wait_ge(*at("sc_turned"))
            dlink(nc.vector.scalar_tensor_tensor(out=lg[:, 0:KSEL_S], in0=ps_c[:, PC_T:PC_T + KSEL_S], scalar=AD ** -0.5,
                                                 in1=pen_q[:, 0:KSEL_S], op0=ALU.mult, op1=ALU.add))
            dlink(nc.vector.tensor_reduce(out=soft[:, 0:1], in_=lg, axis=AX.X, op=ALU.max))
            nc.vector.tensor_scalar(soft[:, 1:2], soft[:, 0:1], -1.0, None, ALU.mult).then_inc(reached("max_s"), 1)
            yield
            yield
            dve.wait_ge(*at("exp_s"))
            dlink(nc.vector.reciprocal(soft[:, 3:4], soft[:, 2:3]))
            dve.wait_ge(*at("probs_turned"))
            nc.vector.tensor_copy(probs_t.rearrange("p c h r -> p (c h r)"), ps_c[:, PC_T:PC_T + KSEL_S]
                                  ).then_inc(reached("probs_copied"), 1)
            yield

        def tensor_gather(pe):
            yield from hosted_pause(1 + R)
            pe.wait_ge(row_scored, R)
            prompt_sums_read(pe)
            for c in range(SC):
                last = nc.tensor.transpose(ps_c[:, PC_T + c * P:PC_T + (c + 1) * P],
                                           g_sc[:, c, :, :].rearrange("p h r -> p (h r)"), ident[:, :])
            last.then_inc(reached("sc_turned"), 1)
            pe.wait_ge(*at("max_s"))
            yield
            yield
            pe.wait_ge(*at("exp_s"))
            prompt_sums_read(pe)
            for c in range(SC):
                last = nc.tensor.transpose(ps_c[:, PC_T + c * P:PC_T + (c + 1) * P], pr[:, c * P:(c + 1) * P], ident[:, :])
            last.then_inc(reached("probs_turned"), 1)
            pe.wait_ge(*at("probs_copied"))
            yield
            for r in range(R):
                tensor_row_sum(pe, r)
                yield

        def scalar_gather(act):
            yield from hosted_pause(CK0)
            act.wait_ge(*at("gate_in"))
            nc.scalar.activation(gate_s, gate_s, ACT.Silu).then_inc(reached("gate_ready"), 1)
            yield from hosted_pause(R + 1)
            act.wait_ge(*at("max_s"))
            nc.scalar.activation(pr, lg, ACT.Exp, bias=soft[:, 1:2], accum_out=soft[:, 2:3]).then_inc(reached("exp_s"), 1)
            yield

        def gpsimd_gathers(pool):
            yield from hosted_pause(CK0)
            for r in range(R):
                gpsimd_gather(pool, r, False)
                yield
            yield from hosted_pause(2)
            for r in range(R):
                gpsimd_gather(pool, r, True)
                yield

        def prompt_sums_read(pe):
            if counts["pv"]:
                pe.wait_ge(o_read, counts["pv"])

        counts = {"norm": 0, "sqrt": 0, "pv": 0}

        def tensor_row_sum(pe, r):
            s = r % VS
            if r == 0:
                pe.wait_ge(*at("probs_copied"))
            pe.wait_ge(got_in[s], got_count(r, True))
            prompt_sums_read(pe)
            for h in range(H):
                for c in range(SC):
                    last = nc.tensor.matmul(ps_c[:, PC_O + h * R + r:PC_O + h * R + r + 1],
                                            got_v[s][:, c, h * AD:(h + 1) * AD], probs_t[:, c, h, r:r + 1],
                                            start=c == 0, stop=c == SC - 1)
            last.then_inc(row_summed, 1)

        def tensor_gather_out(pe):
            pe.wait_ge(*at("ot_copied"))
            nc.tensor.transpose(ps_c[:, PC_T:PC_T + P], ot, ident[:, :]).then_inc(reached("o_turned"), 1)

        def vector_gather_out(dve):
            dve.wait_ge(row_summed, R)
            nc.vector.tensor_copy(ot, ps_c[:, PC_O:PC_O + P]).then_inc(reached("ot_copied"), 1)
            dve.wait_ge(*at("o_turned"))
            dlink(nc.vector.tensor_copy(o_s, ps_c[:, PC_T:PC_T + P]))
            for j in range(NQ):
                dlink(nc.vector.scalar_tensor_tensor(out=o_s, in0=vn[:, j, :], scalar=pr[:, KSEL_S + j:KSEL_S + j + 1],
                                                     in1=o_s, op0=ALU.mult, op1=ALU.add))
            dve.wait_ge(*at("gate_ready"))
            nc.vector.scalar_tensor_tensor(out=o_s, in0=o_s, scalar=soft[:, 3:4], in1=gate_s,
                                           op0=ALU.mult, op1=ALU.mult).then_inc(reached("mixed_s"), 1)

        def store_mix_s(eng, o, col):
            for h in range(H):
                eng.dma_start(mix_s[:, col + h * AD:col + (h + 1) * AD], o[h * R:(h + 1) * R, :]).then_inc(mix_stored, 16)

        k_t = place(0, [H, S])
        v_p = place(2048, [MT, AW])
        ikt_p = place(4096, [S])
        mk_t = place(4608, [H, NMEM])
        ZP = W_IN - C_AQ
        z_t = place(5632, [ZP])
        q_t = place(5632 + ZP, [H, P])
        iqt_p = place(5632 + ZP + 512, [IH // 2, P])
        cq_t = place(5632 + ZP + 1536, [H, P])
        lg_p = place(5632 + ZP + 2048, [S])
        assert 5632 + ZP + 2560 <= W_OFF
        sc_p = place(X_OFF, [S])
        relu_p = place(X_OFF + 512, [2, S])
        pr_p = place(X_OFF + 1536, [S])
        pt_p = place(X_OFF + 2048, [MT, P])
        o_p = place(X_OFF + 2560, [AW])
        ik_pair = place(X_OFF + 2560, [2, ID])
        keep_p = sb("keep_p", [P, 40])
        top8_p = keep_p[:, 0:8]
        st_p = keep_p[:, 24:40].rearrange("p (s c) -> p s c", s=4)
        iw_p = keep_p[:, 8:24]
        zq = lambda c: c - C_AQ

        (zt_in, rotated_p, kv_stored, turned_p, turned_copied, mem_turned, mem_copied, gates_p,
            v_kept, pairs_ready) = (
            sem(n) for n in ("zt_in", "rotated_p", "kv_stored", "turned_p", "turned_copied", "mem_turned",
            "mem_copied", "gates_p", "v_kept", "pairs_ready"))
        (ix_scored, ix_relu, ix_added, pen_ready, qk_done, lg_read, mx_ready, exp_done,
            pt_turned, pt_copied, pv_done, o_read, o_stored) = (
            sem(n) for n in ("ix_scored", "ix_relu", "ix_added", "pen_ready", "qk_done", "lg_read", "mx_ready",
            "exp_done", "pt_turned", "pt_copied", "pv_done", "o_read", "o_stored"))
        JT = 2 * H
        PREP_PIECES, TOPK_PIECES = 5, 12
        TURNS = 5

        def sync_prompt_in(sp, m):
            if m:
                sp.wait_ge(o_read, JT * m)
                sp.wait_ge(kv_stored, 48 * m)
            else:
                for i in range(MT + 1):
                    sp.wait_ge(z_stored[i], 16 * (N_B0 - N_A0))
                sp.wait_ge(weighted, n_idx_units + 1)
                sp.wait_ge(za_stored, 16 * 7)
                sp.wait_ge(*at("gate_in"))
            sp.dma_start(z_t, z_p[m * P:(m + 1) * P, C_AQ:W_IN]).then_inc(zt_in, 16)

        def sync_prompt_kv(sp, m):
            sp.wait_ge(rotated_p, m + 1)
            rows = slice(m * P, (m + 1) * P)
            sp.dma_start(O["p_attn_k"].rearrange("l b s h d -> (l b s) (h d)")[rows, :],
                         z_t[:, zq(C_AK):zq(C_AK) + AW]).then_inc(kv_stored, 16)
            sp.dma_start(O["p_attn_v"].rearrange("l b s h d -> (l b s) (h d)")[rows, :],
                         z_t[:, zq(C_AV):zq(C_AV) + AW]).then_inc(kv_stored, 16)
            sp.dma_start(O["p_idx_k"].rearrange("l b s d -> (l b s) d")[rows, :],
                         z_t[:, zq(C_IK):zq(C_IK) + ID]).then_inc(kv_stored, 16)

        def vector_prompt_prep(dve, m):
            yield
            dve.wait_ge(zt_in, 16 * (m + 1))
            if m:
                dve.wait_ge(o_stored, 16 * 2 * m)
            tab = rope_tab[:, m, :]
            dlink(rotate(P, z_t[:, zq(C_AQ):zq(C_AQ) + AW], H, AD, tab, AD // 8))
            yield
            dlink(rotate(P, z_t[:, zq(C_AK):zq(C_AK) + AW], H, AD, tab, AD // 8))
            yield
            dlink(rotate(P, z_t[:, zq(C_IQ):zq(C_IQ) + IH * ID], IH, ID, tab, ID // 8))
            yield
            rotate(P, z_t[:, zq(C_IK):zq(C_IK) + ID], 1, ID, tab, ID // 8).then_inc(rotated_p, 1)
            dve.wait_ge(rotated_p, m + 1)
            nc.vector.tensor_scalar(iw_p, z_t[:, zq(C_IW):zq(C_IW) + IH], float(ID ** -0.5 * IH ** -0.5), None, ALU.mult)
            nc.vector.tensor_copy(ik_pair, z_t[:, zq(C_IK):zq(C_IK) + ID].unsqueeze(1).broadcast_to([P, 2, ID])
                                  ).then_inc(pairs_ready, 1)
            yield
            yield from hosted_pause(4 if m == 0 else 3)

        def tensor_prompt_turn(pe, m):
            yield from hosted_pause(PREP_PIECES)
            if m == 0:
                for b in range(2):
                    for i in range(4):
                        h, t = 2 * b + i // 2, i % 2
                        last = nc.tensor.transpose((ps_a, ps_b)[b][:, i * P:(i + 1) * P],
                                                   mem_kv[:, t, h * AD:(h + 1) * AD], ident[:, :])
                    last.then_inc(mem_turned, 1)
                yield
                pe.wait_ge(mem_copied, 2)
            else:
                pe.wait_ge(o_read, JT * m)
            pe.wait_ge(pairs_ready, m + 1)
            groups = [[(zq(C_AQ) + h * AD) for h in range(H)], [(zq(C_AK) + h * AD) for h in range(H)],
                      [(zq(C_IQ) + h * P) for h in range(4)], [(zq(C_IQ) + h * P) for h in range(4, 8)],
                      [(zq(C_CQ) + h * AD) for h in range(H)]]
            for g, cols in enumerate(groups):
                if g >= 2:
                    pe.wait_ge(turned_copied, (TURNS + 1) * m + g - 1)
                bank = (ps_a, ps_b)[g % 2]
                for i, c in enumerate(cols):
                    last = nc.tensor.transpose(bank[:, i * P:(i + 1) * P], z_t[:, c:c + P], ident[:, :])
                last.then_inc(turned_p, 1)
                if g % 2:
                    yield
            pe.wait_ge(turned_copied, (TURNS + 1) * m + 4)
            nc.tensor.transpose(ps_b[:, 0:P], ik_pair.rearrange("p a d -> p (a d)"), ident[:, :]).then_inc(turned_p, 1)
            yield

        def scalar_prompt_turn(act, m):
            yield from hosted_pause(PREP_PIECES)
            if m == 0:
                for b in range(2):
                    act.wait_ge(mem_turned, b + 1)
                    nc.scalar.copy(mk_t[:, 2 * b:2 * b + 2, :],
                                   (ps_a, ps_b)[b][:, :].rearrange("p (h m) -> p h m", h=2)).then_inc(mem_copied, 1)
                yield
            rows = slice(m * P, (m + 1) * P)
            dsts = [q_t, k_t[:, :, rows], iqt_p[:, 0:4, :], iqt_p[:, 4:8, :], cq_t]
            for g, dst in enumerate(dsts):
                act.wait_ge(turned_p, (TURNS + 1) * m + g + 1)
                nc.scalar.copy(dst, (ps_a, ps_b)[g % 2][:, :].rearrange("p (h m) -> p h m", h=4)).then_inc(turned_copied, 1)
                if g % 2:
                    yield
            act.wait_ge(turned_p, (TURNS + 1) * (m + 1))
            nc.scalar.copy(ikt_p[:, rows], ps_b[:, 0:P]).then_inc(turned_copied, 1)
            nc.scalar.copy(v_p[:, m, :], z_t[:, zq(C_AV):zq(C_AV) + AW]).then_inc(v_kept, 1)
            nc.scalar.activation(z_t[:, zq(C_AG):zq(C_AG) + AW], z_t[:, zq(C_AG):zq(C_AG) + AW], ACT.Silu).then_inc(gates_p, 1)
            nc.scalar.activation(z_t[:, zq(C_CG):zq(C_CG) + AW], z_t[:, zq(C_CG):zq(C_CG) + AW], ACT.Silu).then_inc(gates_p, 1)
            yield

        def tensor_prompt_index(pe, m):
            nk = P * (m + 1)
            pe.wait_ge(turned_copied, (TURNS + 1) * (m + 1))
            for h in range(IH):
                g = IH * (m - 1) + h
                if g >= 2:
                    pe.wait_ge(ix_relu, g - 1)
                half = slice((h % 2) * ID, (h % 2 + 1) * ID)
                nc.tensor.matmul((ps_a, ps_b)[h % 2][:, 0:nk], iqt_p[half, h // 2, :], ikt_p[half, 0:nk],
                                 start=True, stop=True).then_inc(ix_scored, 1)
                if h % 2:
                    yield
            yield from hosted_pause(TOPK_PIECES)

        def scalar_prompt_index(act, m):
            nk = P * (m + 1)
            for h in range(IH):
                g = IH * (m - 1) + h
                act.wait_ge(ix_scored, g + 1)
                if g >= 2:
                    act.wait_ge(ix_added, g - 1)
                nc.scalar.activation(relu_p[:, h % 2, 0:nk], (ps_a, ps_b)[h % 2][:, 0:nk], ACT.Relu).then_inc(ix_relu, 1)
                if h % 2:
                    yield
            yield from hosted_pause(TOPK_PIECES)

        def vector_prompt_select(dve, m):
            nk = P * (m + 1)
            if m == 0:
                nc.vector.tensor_copy(sc_p[:, 0:P], fut).then_inc(pen_ready, 1)
                dve.wait_ge(pen_ready, 1)
                return
            for h in range(IH):
                g = IH * (m - 1) + h
                dve.wait_ge(ix_relu, g + 1)
                if h == 0:
                    add = nc.vector.tensor_scalar(sc_p[:, 0:nk], relu_p[:, 0, 0:nk], iw_p[:, 0:1], None, ALU.mult)
                else:
                    add = nc.vector.scalar_tensor_tensor(out=sc_p[:, 0:nk], in0=relu_p[:, h % 2, 0:nk],
                                                         scalar=iw_p[:, h:h + 1], in1=sc_p[:, 0:nk],
                                                         op0=ALU.mult, op1=ALU.add)
                add.then_inc(ix_added, 1)
                dve.wait_ge(ix_added, g + 1)
                if h % 2:
                    yield
            dlink(nc.vector.tensor_tensor(out=sc_p[:, nk - P:nk], in0=sc_p[:, nk - P:nk], in1=fut, op=ALU.add))
            rounds = KSEL_P // 8
            for i in range(rounds):
                dlink(nc.vector.max(top8_p, sc_p[:, 0:nk]))
                dlink(nc.vector.match_replace(sc_p[:, 0:nk], top8_p, sc_p[:, 0:nk], TAKEN))
                if (i + 1) * TOPK_PIECES // rounds > i * TOPK_PIECES // rounds and i < rounds - 1:
                    yield
            nc.vector.tensor_scalar(sc_p[:, 0:nk], sc_p[:, 0:nk], TAKEN, NEG, ALU.not_equal, ALU.mult).then_inc(pen_ready, 1)
            dve.wait_ge(pen_ready, m + 1)
            yield

        def job(m, j):
            if j < H:
                return P * (m + 1), q_t[:, j, :], k_t[:, j, 0:P * (m + 1)], lambda i: v_p[:, i, j * AD:(j + 1) * AD]
            h = j - H
            return NMEM, cq_t[:, h, :], mk_t[:, h, :], lambda i: mem_kv[:, i, AW + h * AD:AW + (h + 1) * AD]

        def tensor_prompt_attend(pe, m):
            for s in range(JT + 3):
                if s < JT:
                    J = JT * m + s
                    nk, q, k, _ = job(m, s)
                    if s == 0:
                        pe.wait_ge(turned_copied, (TURNS + 1) * (m + 1))
                        pe.wait_ge(v_kept, m + 1)
                        if m:
                            pe.wait_ge(ix_relu, IH * m)
                    if J:
                        pe.wait_ge(lg_read, J)
                    nc.tensor.matmul(ps_a[:, 0:nk], q, k, start=True, stop=True).then_inc(qk_done, 1)
                if s >= 3:
                    J = JT * m + s - 3
                    nk, _, _, v = job(m, s - 3)
                    pe.wait_ge(pt_copied, J + 1)
                    if J:
                        pe.wait_ge(o_read, J)
                    for i in range(nk // P):
                        last = nc.tensor.matmul(ps_c[:, 0:AD], pt_p[:, i, :], v(i), start=i == 0, stop=i == nk // P - 1)
                    last.then_inc(pv_done, 1)
                    counts["pv"] = J + 1
                if 2 <= s < JT + 2:
                    J = JT * m + s - 2
                    nk = job(m, s - 2)[0]
                    pe.wait_ge(exp_done, J + 1)
                    if J:
                        pe.wait_ge(pt_copied, J)
                    for i in range(nk // P):
                        last = nc.tensor.transpose(ps_b[:, i * P:(i + 1) * P], pr_p[:, i * P:(i + 1) * P], ident[:, :])
                    last.then_inc(pt_turned, 1)
                yield

        def scalar_prompt_attend(act, m):
            for s in range(JT + 3):
                if 2 <= s < JT + 2:
                    J = JT * m + s - 2
                    nk = job(m, s - 2)[0]
                    act.wait_ge(pt_turned, J + 1)
                    if J:
                        act.wait_ge(pv_done, J)
                    nc.scalar.copy(pt_p[:, 0:nk // P, :], ps_b[:, 0:nk].rearrange("p (i t) -> p i t", t=P)).then_inc(pt_copied, 1)
                if 1 <= s < JT + 1:
                    J = JT * m + s - 1
                    nk = job(m, s - 1)[0]
                    act.wait_ge(mx_ready, J + 1)
                    if J:
                        act.wait_ge(pt_turned, J)
                    nc.scalar.activation(pr_p[:, 0:nk], lg_p[:, 0:nk], ACT.Exp, bias=st_p[:, J % 4, 1:2],
                                         accum_out=st_p[:, J % 4, 2:3]).then_inc(exp_done, 1)
                yield

        def vector_prompt_attend(dve, m):
            for s in range(JT + 3):
                if s >= 3:
                    j = s - 3
                    J = JT * m + j
                    if j == 0:
                        dve.wait_ge(gates_p, 2 * (m + 1))
                    if j % H == 0 and (m or j):
                        dve.wait_ge(o_stored, 16 * (2 * m + j // H))
                    dve.wait_ge(pv_done, J + 1)
                    dlink(nc.vector.reciprocal(st_p[:, J % 4, 3:4], st_p[:, J % 4, 2:3]))
                    g = zq(C_AG if j < H else C_CG) + (j % H) * AD
                    nc.vector.scalar_tensor_tensor(out=o_p[:, (j % H) * AD:(j % H + 1) * AD], in0=ps_c[:, 0:AD],
                                                   scalar=st_p[:, J % 4, 3:4], in1=z_t[:, g:g + AD],
                                                   op0=ALU.mult, op1=ALU.mult).then_inc(o_read, 1)
                if s < JT:
                    J = JT * m + s
                    nk = job(m, s)[0]
                    dve.wait_ge(qk_done, J + 1)
                    if J:
                        dve.wait_ge(exp_done, J)
                    scale = float(AD ** -0.5)
                    if s < H:
                        out = nc.vector.scalar_tensor_tensor(out=lg_p[:, 0:nk], in0=ps_a[:, 0:nk], scalar=scale,
                                                             in1=sc_p[:, 0:nk], op0=ALU.mult, op1=ALU.add)
                    else:
                        out = nc.vector.tensor_scalar(lg_p[:, 0:nk], ps_a[:, 0:nk], scale, None, ALU.mult)
                    out.then_inc(lg_read, 1)
                    dve.wait_ge(lg_read, J + 1)
                    dlink(nc.vector.tensor_reduce(out=st_p[:, J % 4, 0:1], in_=lg_p[:, 0:nk], axis=AX.X, op=ALU.max))
                    nc.vector.tensor_scalar(st_p[:, J % 4, 1:2], st_p[:, J % 4, 0:1], -1.0, None, ALU.mult).then_inc(mx_ready, 1)
                yield

        def sync_prompt_out(sp, m):
            for g in range(2):
                sp.wait_ge(o_read, JT * m + H * (g + 1))
                sp.dma_start(mix_p[m * P:(m + 1) * P, MW + g * AW:MW + (g + 1) * AW], o_p).then_inc(o_stored, 16)

        xh_free = between[:, 0:X_HI_N]
        xl_free = between[:, X_HI_N:X_HI_N + X_LO_N]
        zt_free = z_tile[:, :, :].rearrange("p m n -> p (m n)")

        def part(flat, off, shape):
            n = 1
            for v in shape:
                n *= v
            names = "abc"[:len(shape)]
            return flat[:, off:off + n].rearrange(f"p ({' '.join(names)}) -> p {' '.join(names)}",
                                                  **dict(zip(names, shape)))
        cq_in, cq_low = (part(between, X_HI_N + X_LO_N + i * W_N + W_N // 2, [2, AW])[0:R] for i in range(2))
        q_spread = part(xh_free, 0, [H * NB * (P + NQ)])
        k_mem = [part(xh_free, 4224, [NMEM // P, AW]), part(xh_free, 5248, [NMEM // P, AW]),
                 w_raw[:, RAWS - 1, :, :]]
        KS = len(k_mem)
        kt_mem = part(xh_free, 6272, [2 * H, NMEM]).rearrange("p (s h) c -> p s h c", s=2)
        lg_c = part(xh_free, 8320, [NMEM])
        pr_c = part(xh_free, 8320 + NMEM, [NMEM])
        o_c = part(xh_free, 8320 + 2 * NMEM, [AD])
        gate_c = part(xh_free, 8320 + 2 * NMEM + AD, [AD])
        p_spread = [part(zt_free, i * 1056, [NB * (P + NQ)]) for i in range(2)]
        (cq_loaded, km_turned, kt_ready, cv_done) = (
            sem(n) for n in ("cq_loaded", "km_turned", "kt_ready", "cv_done"))
        km_in = [sem(f"km_in{i}") for i in range(KS)]

        def gpsimd_mem_in(pool):
            pool.wait_ge(chunk_used, CH * N_Y0)
            pool.dma_start(cq_in, z_s[0:R, C_CQ:C_CQ + 2 * AW].rearrange("r (a c) -> r a c", a=2)).then_inc(cq_loaded, 16)
            pool.dma_start(cq_low, z_s[R:2 * R, C_CQ:C_CQ + 2 * AW].rearrange("r (a c) -> r a c", a=2)).then_inc(cq_loaded, 16)
            for i in range(2 * NB):
                b = i % NB
                if i >= NB + KS:
                    pool.wait_ge(cv_done, i - KS - NB + 1)
                elif i >= KS:
                    pool.wait_ge(km_turned, 2 * (i - KS + 1))
                src = (I["cache_mem_k"] if i < NB else I["cache_mem_v"])[0, b].rearrange("(t p) h d -> p t (h d)", p=P)
                pool.dma_start(k_mem[i % KS], src).then_inc(km_in[i % KS], 16)

        def vector_mem_s(dve):
            dve.wait_ge(cq_loaded, 32)
            for m in range(MT + 1):
                dve.wait_ge(z_stored[m], 16 * (N_Y0 - N_A0))
            nc.vector.tensor_tensor(out=cq_in, in0=cq_in, in1=cq_low, op=ALU.add).then_inc(reached("cq_ready"), 1)
            nc.vector.memset(q_spread, 0.0)
            for t in range(2):
                dlink(nc.vector.memset(p_spread[t], 0.0))
            dve.wait_ge(*at("cq_ready"))
            for h in range(H):
                last = nc.vector.tensor_copy(gate_c[h * R:(h + 1) * R, :], cq_in[:, 1, h * AD:(h + 1) * AD])
            last.then_inc(reached("gate_c_in"), 1)
            dve.wait_ge(*at("cq_turned"))
            nc.vector.tensor_copy(q_spread.rearrange("p (i x) -> p i x", x=P + NQ)[:, :, 0:NQ],
                                  ps_a[:, 0:P].rearrange("p (i q) -> p i q", q=NQ)).then_inc(reached("qs_ready"), 1)
            yield
            dve.wait_ge(cl_used, NB)
            dlink(nc.vector.tensor_scalar(lg_c, ps_c[:, 0:NMEM], float(AD ** -0.5), None, ALU.mult))
            dlink(nc.vector.tensor_reduce(out=soft[:, 4:5], in_=lg_c, axis=AX.X, op=ALU.max))
            nc.vector.tensor_scalar(soft[:, 5:6], soft[:, 4:5], -1.0, None, ALU.mult).then_inc(reached("cmax"), 1)
            dve.wait_ge(*at("cexp"))
            dlink(nc.vector.reciprocal(soft[:, 7:8], soft[:, 6:7]))
            dve.wait_ge(*at("cp_turned"))
            for t in range(2):
                dst = p_spread[t].rearrange("p (b x) -> p b x", x=P + NQ)[:, :, 0:P].rearrange(
                    "p b (h y) -> p h b y", h=H)[:, :, :, 0:NQ]
                last = nc.vector.tensor_copy(dst, ps_a[:, t * P:(t + 1) * P].rearrange("p (h b q) -> p h b q", h=H, b=NB))
            last.then_inc(reached("ps_ready"), 1)
            dve.wait_ge(cv_done, NB)
            for h in range(H):
                hs = slice(h * R, (h + 1) * R)
                last = nc.vector.tensor_copy(o_c[hs, :], ps_c[hs, h * AD:(h + 1) * AD])
            dlink(last)
            dve.wait_ge(*at("gate_c_ready"))
            nc.vector.scalar_tensor_tensor(out=o_c, in0=o_c, scalar=soft[:, 7:8], in1=gate_c,
                                           op0=ALU.mult, op1=ALU.mult).then_inc(reached("mixed_c"), 1)
            yield

        def tensor_mem_s(pe):
            pe.wait_ge(*at("cq_ready"))
            for h in range(H):
                last = nc.tensor.transpose(ps_a[:, h * R:(h + 1) * R], cq_in[:, 0, h * AD:(h + 1) * AD], ident[0:R, 0:R])
            last.then_inc(reached("cq_turned"), 1)
            yield
            pe.wait_ge(*at("qs_ready"))

            def turn(b):
                pe.wait_ge(km_in[b % KS], 16 * (b // KS + 1))
                for g in range(2):
                    if b:
                        pe.wait_ge(kt_ready, 2 * (b - 1) + g + 1)
                    for i in range(4):
                        h, t = 2 * g + i // 2, i % 2
                        last = nc.tensor.transpose((ps_a, ps_b)[g][:, i * P:(i + 1) * P],
                                                   k_mem[b % KS][:, t, h * AD:(h + 1) * AD], ident[:, :])
                    last.then_inc(km_turned, 1)

            turn(0)
            yield
            for b in range(NB):
                if b + 1 < NB:
                    turn(b + 1)
                pe.wait_ge(kt_ready, 2 * (b + 1))
                for h in range(H):
                    i = h * NB + b
                    last = nc.tensor.matmul(ps_c[:, 0:NMEM], q_spread[:, i * P:(i + 1) * P], kt_mem[:, b % 2, h, :],
                                            start=b == 0 and h == 0, stop=b == NB - 1 and h == H - 1)
                last.then_inc(cl_used, 1)
                yield
            yield
            pe.wait_ge(*at("cexp"))
            for t in range(2):
                last = nc.tensor.transpose(ps_a[:, t * P:(t + 1) * P], pr_c[:, t * P:(t + 1) * P], ident[:, :])
            last.then_inc(reached("cp_turned"), 1)
            yield
            pe.wait_ge(*at("ps_ready"))
            for b in range(NB):
                i = NB + b
                pe.wait_ge(km_in[i % KS], 16 * (i // KS + 1))
                for t in range(2):
                    last = nc.tensor.matmul(ps_c[:, :], p_spread[t][:, b * P:(b + 1) * P], k_mem[i % KS][:, t, :],
                                            start=b == 0 and t == 0, stop=b == NB - 1 and t == 1)
                last.then_inc(cv_done, 1)
                if b % 2:
                    yield

        cl_used = sem("cl_used")

        def scalar_mem_s(act):
            act.wait_ge(*at("gate_c_in"))
            nc.scalar.activation(gate_c, gate_c, ACT.Silu).then_inc(reached("gate_c_ready"), 1)
            yield
            act.wait_ge(*at("qs_ready"))
            for b in range(NB):
                for g in range(2):
                    act.wait_ge(km_turned, 2 * b + g + 1)
                    if b >= 2:
                        act.wait_ge(cl_used, b - 1)
                    nc.scalar.copy(kt_mem[:, b % 2, 2 * g:2 * g + 2, :],
                                   (ps_a, ps_b)[g][:, :].rearrange("p (h m) -> p h m", h=2)).then_inc(kt_ready, 1)
                yield
            yield
            act.wait_ge(*at("cmax"))
            nc.scalar.activation(pr_c, lg_c, ACT.Exp, bias=soft[:, 5:6], accum_out=soft[:, 6:7]).then_inc(reached("cexp"), 1)
            yield from hosted_pause(2 + NB // 2)

        GW = S + R
        CK = 4
        row = lambda i: place(GW * i, [GW], H)
        g_f, g_i, g_t, g_b, g_M, g_m, g_w, g_e, g_one, g_zero = (row(i) for i in range(10))
        M0 = 10 * GW
        keep_m = sb("keep_m", [P, 232])
        c_a = keep_m[:, 0:20].rearrange("p (m h) -> p m h", h=H)
        c_w = keep_m[:, 20:40].rearrange("p (m h) -> p m h", h=H)
        c_e = keep_m[:, 40:60].rearrange("p (m h) -> p m h", h=H)
        conv_c = keep_m[:, 60:140].rearrange("p (k j) -> p k j", j=CK + 1)
        mx_T = keep_m[0:H, 140:150]
        bias_g = keep_m[0:H, 150:152]
        m0_s = keep_m[0:H, 152:160]
        a_T = keep_m[0:H, 160:168]
        bn_o = keep_m[:, 168:176]
        st_m = keep_m[:, 176:184]
        aT8 = keep_m[0:NB, 184:188]
        w_b = keep_m[0:R, 188:220].rearrange("p (h b) -> p h b", h=H)
        batch_of = keep_m[0:R, 220:228]
        hr = sb("head_rows", [H, H * P])
        z_h = [place(M0, [4, MT, MD]), part(xl_free, 0, [4, MT, MD])]
        va = [place(M0 + 5120, [MT, MD + 2]), part(xl_free, 4096, [MT, MD + 2])]
        qk_t = [place(M0 + 7180, [2, 2, S]), part(xl_free, 5128, [2, 2, S])]
        cv = [place(M0 + 6152, [S]), place(M0 + 6668, [S])]
        k_n = place(M0 + 9228, [MT, MD])
        p_w = place(M0 + 10252, [MT, S])
        w_t = [place(M0 + 12300, [S]), place(M0 + 12812, [S])]
        h_o = part(xh_free, 0, [MT, MD])
        h_st = part(xh_free, 1024, [8, MT])
        h_bn = part(xh_free, 1056, [MT, 6])
        h_mv = part(xh_free, 1080, [MT, 2])
        hn = place(M0 + 13324, [H * MD])
        c_o = place(M0 + 14348, [2, MD])
        n_o = place(M0 + 14860, [MD], 1)
        causal = place(M0 + 15116, [P])
        assert M0 + 15244 <= AR_N
        conv_nat = place(M0 + 10252, [2 * MW], CK + 1)
        ifp = place(M0 + 12300, [MT, 2 * H])
        ifs = place(M0 + 12364, [2, 2 * H], R)
        m0_nat = place(M0 + 12396, [H], NB)

        (mc_in, xc_turned, xc_done, kn_turned, kn_done) = (
            sem(n) for n in ("mc_in", "xc_turned", "xc_done", "kn_turned", "kn_done"))
        (g_turned, g_copied, mb_done, w_arg, w_exp, s_done, w_done, h_done, gates_mixed, h_sqrt,
            h_out, c_done, c_copied, c_stored, gate_m) = (
            sem(n) for n in ("g_turned", "g_copied", "mb_done", "w_arg", "w_exp", "s_done", "w_done", "h_done",
            "gates_mixed", "h_sqrt", "h_out", "c_done", "c_copied", "c_stored", "gate_m"))
        h_stored = sem("h_stored")
        zh_in = [sem("zh_in0"), sem("zh_in1")]
        conv_out = sem("conv_out")
        N_MC = 13

        def sync_mlstm_consts(sp):
            sp.wait_ge(mix_stored, 16 * H)
            sp.wait_ge(o_stored, 16 * 2 * MT)
            sp.wait_ge(kv_stored, 48 * MT)
            for i in range(MT + 1):
                sp.wait_ge(z_stored[i], 16 * (N_Y0 - N_A0))
            for dst, src in ((hr[:, :], C["head_row"]), (g_one, C["carry"]), (g_zero, C["zeros"]),
                             (bias_g[:, 0:1], I["b_if"][0, 0:H].unsqueeze(1)), (bias_g[:, 1:2], I["b_if"][0, H:2 * H].unsqueeze(1)),
                             (batch_of, C["batch_of"]), (causal, C["causal"]),
                             (hn, I["mlstm_head_norm"][0:1, :].broadcast_to([P, MW])),
                             (conv_nat[0:CK, :], I["conv_w"][0]), (conv_nat[CK:CK + 1, :], I["conv_b"][0:1, :]),
                             (ifp, z_p[:, C_IF:C_IF + 2 * H].rearrange("(m p) c -> p m c", p=P)),
                             (ifs, z_s[:, C_IF:C_IF + 2 * H].rearrange("(a r) c -> r a c", a=2)),
                             (m0_nat, I["state_mlstm_m"][0])):
                sp.dma_start(dst, src).then_inc(mc_in, 16)
            sp.dma_start(O["p_conv"].rearrange("l b j c -> (l b j) c"), z_p[S - CK + 1:S, 0:2 * MW]).then_inc(conv_out, 16)

        def sync_mlstm_head(sp, h):
            if h == 0:
                sp.wait_ge(chunk_used, CH * N_Y0)
            if h >= 2:
                sp.wait_ge(c_done, 2 * (h - 1))
                sp.wait_ge(h_out, h - 1)
            for i, c in enumerate((C_QK, C_QK + MW, C_O, C_G, C_V)):
                src = z_p[:, c + h * MD:c + (h + 1) * MD].rearrange("(m p) c -> p m c", p=P)
                dst = va[h % 2][:, :, 0:MD] if i == 4 else z_h[h % 2][:, i, :, :]
                sp.dma_start(dst, src).then_inc(zh_in[h % 2], 16)

        GATES = acc[0:3]

        def tensor_mlstm_gates(pe):
            pe.wait_ge(mc_in, 16 * N_MC)
            pe.wait_ge(acc_read, acc_base(N_Y0))
            pe.wait_ge(*at("ifs_ready"))
            for half in range(2):
                bank = GATES[half]
                for m in range(MT):
                    last = nc.tensor.transpose(bank[0:H, m * P:(m + 1) * P], ifp[:, m, half * H:(half + 1) * H], ident[:, :])
                last.then_inc(g_turned, 1)
            nc.tensor.transpose(GATES[2][0:H, 0:R], ifs[:, 0, 0:H], ident[0:R, 0:R])
            nc.tensor.transpose(GATES[2][0:H, R:2 * R], ifs[:, 0, H:2 * H], ident[0:R, 0:R])
            nc.tensor.transpose(GATES[2][0:H, 2 * R:2 * R + NB], m0_nat, ident[0:NB, 0:NB]).then_inc(g_turned, 1)
            yield
            pe.wait_ge(g_copied, 5)
            for k in range(KT):
                last = nc.tensor.transpose(GATES[0][:, k * (CK + 1):(k + 1) * (CK + 1)], conv_nat[:, k * P:(k + 1) * P],
                                           ident[0:CK + 1, 0:CK + 1])
            last.then_inc(reached("conv_w_t"), 1)
            yield
            pe.wait_ge(*at("g_we"))
            for m in range(MT + 1):
                n = P if m < MT else R
                for i, r in enumerate((g_i, g_w, g_e)):
                    c = (i * (MT + 1) + m) * H
                    last = nc.tensor.transpose(GATES[1][0:n, c:c + H], r[:, m * P:m * P + n], ident[0:H, 0:H])
            nc.tensor.transpose(GATES[1][0:NB, 64:64 + H], a_T, ident[0:H, 0:H]).then_inc(reached("g_colt"), 1)
            yield

        def scalar_mlstm_gates(act):
            act.wait_ge(g_turned, 1)
            nc.scalar.activation(g_i[:, 0:S], GATES[0][0:H, :], ACT.Identity, bias=bias_g[:, 0:1]).then_inc(g_copied, 1)
            act.wait_ge(g_turned, 2)
            nc.scalar.activation(g_f[:, 0:S], GATES[1][0:H, :], ACT.Identity, bias=bias_g[:, 1:2]).then_inc(g_copied, 1)
            act.wait_ge(g_turned, 3)
            nc.scalar.activation(g_i[:, S:GW], GATES[2][0:H, 0:R], ACT.Identity, bias=bias_g[:, 0:1]).then_inc(g_copied, 1)
            nc.scalar.activation(g_f[:, S:GW], GATES[2][0:H, R:2 * R], ACT.Identity, bias=bias_g[:, 1:2]).then_inc(g_copied, 1)
            nc.scalar.copy(m0_s, GATES[2][0:H, 2 * R:2 * R + NB]).then_inc(g_copied, 1)
            yield
            act.wait_ge(*at("conv_w_t"))
            nc.scalar.copy(conv_c, GATES[0][:, 0:KT * (CK + 1)].rearrange("p (k j) -> p k j", j=CK + 1)).then_inc(reached("conv_w_c"), 1)
            act.wait_ge(*at("g_abs"))
            nc.scalar.activation(g_e, g_t, ACT.Exp, scale=-1.0).then_inc(reached("g_exp"), 1)
            act.wait_ge(*at("g_exp"))
            nc.scalar.activation(g_e, g_e, ACT.Ln, bias=1.0).then_inc(reached("g_ln"), 1)
            yield
            act.wait_ge(*at("g_rows"))
            alink(nc.scalar.activation(g_w, g_w, ACT.Exp))
            alink(nc.scalar.activation(g_e, g_m, ACT.Exp, scale=-1.0))
            nc.scalar.activation(g_t[:, S:GW], g_t[:, S:GW], ACT.Exp)
            nc.scalar.activation(a_T, a_T, ACT.Exp).then_inc(reached("g_we"), 1)
            yield
            act.wait_ge(*at("g_colt"))
            for m in (0, 1):
                n = P if m == 0 else R
                v = GATES[1][0:n, 0:3 * (MT + 1) * H].rearrange("p (i m h) -> p i m h", i=3, h=H)
                ms = slice(0, MT) if m == 0 else slice(MT, MT + 1)
                for i, dst in enumerate((c_a, c_w, c_e)):
                    nc.scalar.activation(dst[0:n, ms, :], v[:, i, ms, :], ACT.Copy,
                                         scale=float(MD ** -0.5) if i == 1 and m == 0 else 1.0)
            nc.scalar.copy(aT8, GATES[1][0:NB, 64:64 + H]).then_inc(reached("g_cols"), 1)
            yield

        def vector_mlstm_gates(dve):
            dve.wait_ge(mc_in, 16 * N_MC)
            nc.vector.tensor_tensor(out=ifs[:, 0, :], in0=ifs[:, 0, :], in1=ifs[:, 1, :], op=ALU.add).then_inc(reached("ifs_ready"), 1)
            dve.wait_ge(g_copied, 5)
            dlink(nc.vector.tensor_scalar(g_t, g_f, -1.0, None, ALU.mult))
            nc.vector.tensor_tensor(out=g_t, in0=g_t, in1=g_f, op=ALU.max).then_inc(reached("g_abs"), 1)
            dve.wait_ge(*at("g_ln"))
            dlink(nc.vector.scalar_tensor_tensor(out=g_f, in0=g_f, scalar=0.0, in1=g_e, op0=ALU.min, op1=ALU.subtract))
            dlink(nc.vector.tensor_tensor_scan(out=g_b, data0=g_one, data1=g_f, initial=0.0, op0=ALU.mult, op1=ALU.add))
            dlink(nc.vector.tensor_tensor(out=g_i, in0=g_i, in1=g_b, op=ALU.subtract))
            nc.vector.tensor_tensor_scan(out=g_M[:, 0:S], data0=g_zero[:, 0:S], data1=g_i[:, 0:S], initial=0.0,
                                         op0=ALU.add, op1=ALU.max)
            by_b = lambda r: r[:, S:GW].rearrange("p (b t) -> p b t", t=NQ)
            Ms, as_, ts_, ws = by_b(g_M), by_b(g_i), by_b(g_t), by_b(g_w)
            dlink(nc.vector.tensor_tensor(out=Ms[:, :, 0], in0=as_[:, :, 0], in1=m0_s, op=ALU.max))
            for t in range(1, NQ):
                dlink(nc.vector.tensor_tensor(out=Ms[:, :, t], in0=Ms[:, :, t - 1], in1=as_[:, :, t], op=ALU.max))
            nc.vector.tensor_tensor(out=g_m, in0=g_b, in1=g_M, op=ALU.add)
            nc.vector.tensor_scalar(g_w[:, 0:S], g_i[:, 0:S], g_M[:, S - 1:S], None, ALU.subtract)
            nc.vector.tensor_tensor(out=ws, in0=as_, in1=Ms[:, :, NQ - 1:NQ].broadcast_to([H, NB, NQ]), op=ALU.subtract)
            nc.vector.tensor_tensor(out=ts_, in0=m0_s.unsqueeze(2).broadcast_to([H, NB, NQ]), in1=Ms, op=ALU.subtract)
            nc.vector.tensor_tensor(out=a_T, in0=m0_s, in1=Ms[:, :, NQ - 1], op=ALU.subtract).then_inc(reached("g_rows"), 1)

        def sync_mlstm_m(sp):
            sp.wait_ge(*at("g_rows"))
            sp.dma_start(O["p_m"].rearrange("l b h -> (l b h)").unsqueeze(1), g_m[:, S - 1:S]).then_inc(conv_out, 16)
            sp.dma_start(O["s_m"][0].rearrange("b h -> h b"),
                         g_m[:, S:GW].rearrange("p (b t) -> p b t", t=NQ)[:, :, NQ - 1], allow_slow_non_contiguous=True
                         ).then_inc(conv_out, 16)

        SCORES, MROW, CONV, NUM = ps_a, ps_b, acc[0], acc[1:3]
        STATE, DEN = CONV, MROW
        n_row = DEN[0:1, 8:8 + MD]

        def zh_count(h):
            return 16 * 5 * (h // 2 + 1)

        def tensor_conv_turn(pe, h, u):
            g = 4 * h + u
            if u == 0:
                pe.wait_ge(zh_in[h % 2], zh_count(h))
            if g == 0:
                pe.wait_ge(*at("conv_w_c"))
            else:
                if h >= 2 and u == 0:
                    pe.wait_ge(c_copied, 2 * (h - 1) - 1)
                pe.wait_ge(xc_done, g)
            for m in range(MT):
                last = nc.tensor.transpose(CONV[:, m * P:(m + 1) * P], z_h[h % 2][:, u // 2, m, (u % 2) * P:(u % 2 + 1) * P],
                                           ident[:, :])
            last.then_inc(xc_turned, 1)

        def vector_conv(dve, h, u):
            g, k = 4 * h + u, (u // 2) * (KT // 2) + 2 * h + u % 2
            if g == 0:
                dve.wait_ge(*at("conv_w_c"))
            dve.wait_ge(xc_turned, g + 1)
            if g >= 2:
                dve.wait_ge(conv_silu, g - 1)
            out = cv[g % 2]
            dlink(nc.vector.tensor_scalar(out, CONV[:, :], conv_c[:, k, CK - 1:CK], None, ALU.mult))
            for j in range(1, CK):
                ins = nc.vector.scalar_tensor_tensor(out=out[:, j:S], in0=CONV[:, 0:S - j],
                                                     scalar=conv_c[:, k, CK - 1 - j:CK - j], in1=out[:, j:S],
                                                     op0=ALU.mult, op1=ALU.add)
                if j < CK - 1:
                    dlink(ins)
            ins.then_inc(xc_done, 1)

        def scalar_conv(act, h, u):
            g, k = 4 * h + u, (u // 2) * (KT // 2) + 2 * h + u % 2
            act.wait_ge(xc_done, g + 1)
            if h >= 2:
                act.wait_ge(w_done, MT * (h - 1))
            nc.scalar.activation(qk_t[h % 2][:, u // 2, u % 2, :], cv[g % 2], ACT.Silu,
                                 bias=conv_c[:, k, CK:CK + 1]).then_inc(conv_silu, 1)

        def tensor_mlstm_head(pe, h, side):
            q_k, v = qk_t[h % 2], va[h % 2]
            if h == 0:
                pe.wait_ge(*at("g_cols"))
            if h:
                pe.wait_ge(c_copied, 2 * h)
            nc.tensor.matmul(MROW[:, :], hr[:, h * P:(h + 1) * P], g_M[:, 0:S], start=True, stop=True).then_inc(mb_done, 1)
            pe.wait_ge(conv_silu, 4 * (h + 1))
            if h:
                pe.wait_ge(w_done, MT * h)
            for u in range(2):
                if u:
                    pe.wait_ge(kn_done, 2 * h + 1)
                for i in range(4):
                    m, d = 2 * u + i // 2, i % 2
                    last = nc.tensor.transpose(SCORES[:, i * P:(i + 1) * P], q_k[:, 1, d, m * P:(m + 1) * P], ident[:, :])
                last.then_inc(kn_turned, 1)
            for i in range(MT):
                g = MT * h + i
                if i == 0:
                    pe.wait_ge(kn_done, 2 * h + 2)
                else:
                    pe.wait_ge(w_done, g)
                for d in range(2):
                    last = nc.tensor.matmul(SCORES[:, 0:S - i * P], q_k[:, 1, d, i * P:(i + 1) * P],
                                            q_k[:, 0, d, i * P:S], start=d == 0, stop=d == 1)
                last.then_inc(s_done, 1)
                side(0)
                if h + 1 < H:
                    tensor_conv_turn(pe, h + 1, i)
                side(1)
            pe.wait_ge(w_done, MT * (h + 1))
            if h == 0:
                pe.wait_ge(ones_set, 1)
            for m in range(MT):
                for i in range(m + 1):
                    w = p_w[:, i, m * P:(m + 1) * P]
                    nc.tensor.matmul(NUM[m // 2][:, m % 2 * MD:(m % 2 + 1) * MD], w, v[:, i, 0:MD], start=i == 0, stop=i == m)
            for m in range(MT):
                for i in range(m + 1):
                    last = nc.tensor.matmul(DEN[:, m:m + 1], p_w[:, i, m * P:(m + 1) * P], v[:, i, MD:MD + 1],
                                            start=i == 0, stop=i == m)
            last.then_inc(num_ready, 1)
            pe.wait_ge(xc_done, 4 * min(h + 2, H))
            for e in range(2):
                for i in range(MT):
                    last = nc.tensor.matmul(STATE[:, e * MD:(e + 1) * MD], v[:, i, e * P:(e + 1) * P], k_n[:, i, :],
                                            start=i == 0, stop=i == MT - 1)
            last.then_inc(c_done, 1)
            pe.wait_ge(h_done, h + 1)
            for i in range(MT):
                last = nc.tensor.matmul(n_row, v[:, i, MD:MD + 1], k_n[:, i, :], start=i == 0, stop=i == MT - 1)
            last.then_inc(c_done, 1)

        num_ready, ones_set = sem("num_ready"), sem("ones_set")

        def gpsimd_mlstm_head(pool, h):
            o, g = z_h[h % 2][:, 2, :, :], z_h[h % 2][:, 3, :, :]
            pool.wait_ge(gate_m, 2 * (h + 1))
            nc.gpsimd.tensor_tensor(out=o, in0=o, in1=g, op=ALU.mult).then_inc(gates_mixed, 1)
            pool.wait_ge(gates_mixed, 2 * h + 1)
            nc.gpsimd.tensor_tensor(out=o, in0=o, in1=hn[:, h * MD:(h + 1) * MD].unsqueeze(1).broadcast_to([P, MT, MD]),
                                    op=ALU.mult).then_inc(gates_mixed, 1)

        def vector_mlstm_head(dve, h, side):
            if h == 0:
                dve.wait_ge(chunk_used, CH * N_Y0)
                for b in range(2):
                    last = nc.vector.memset(va[b][:, :, MD:MD + 1], 1.0)
                last.then_inc(ones_set, 1)
            dve.wait_ge(mb_done, h + 1)
            for i in range(MT):
                g, n = MT * h + i, S - i * P
                w = w_t[i % 2]
                if g >= 2:
                    dve.wait_ge(w_done, g - 1)
                nc.vector.tensor_scalar(w[:, 0:n], MROW[:, i * P:S], c_a[:, i, h:h + 1], 0.0,
                                        ALU.subtract, ALU.max).then_inc(w_arg, 1)
                dve.wait_ge(w_exp, g + 1)
                dlink(nc.vector.tensor_tensor(out=w[:, 0:P], in0=w[:, 0:P], in1=causal, op=ALU.mult))
                dve.wait_ge(s_done, g + 1)
                nc.vector.scalar_tensor_tensor(out=p_w[:, i, i * P:S], in0=SCORES[:, 0:n],
                                               scalar=float(MD ** -0.5), in1=w[:, 0:n], op0=ALU.mult, op1=ALU.mult
                                               ).then_inc(w_done, 1)
                side(0)
                if h + 1 < H:
                    vector_conv(dve, h + 1, i)
                side(1)
            neg, top, inv, var, root, rstd = (h_st[:, i, :] for i in range(6))
            col = lambda a: a.unsqueeze(2).broadcast_to([P, MT, MD])
            dve.wait_ge(num_ready, h + 1)
            dlink(nc.vector.tensor_scalar(neg, DEN[:, 0:MT], -1.0, None, ALU.mult))
            dlink(nc.vector.tensor_tensor(out=top, in0=DEN[:, 0:MT], in1=neg, op=ALU.max))
            dlink(nc.vector.tensor_tensor(out=top, in0=top, in1=c_e[:, 0:MT, h], op=ALU.max))
            dlink(nc.vector.reciprocal(inv, top))
            if h:
                dve.wait_ge(h_stored, 16 * h)
            for t in range(2):
                ins = nc.vector.tensor_tensor(out=h_o[:, 2 * t:2 * t + 2, :],
                                              in0=NUM[t][:, :].rearrange("p (m d) -> p m d", m=2),
                                              in1=col(inv)[:, 2 * t:2 * t + 2, :], op=ALU.mult)
            ins.then_inc(h_done, 1)
            dve.wait_ge(h_done, h + 1)
            for m in range(MT):
                last = nc.vector.bn_stats(h_bn[:, m, :], h_o[:, m, :])
            dlink(last)
            for m in range(MT):
                last = nc.vector.bn_aggr(h_mv[:, m, :], h_bn[:, m, :])
            dlink(last)
            nc.vector.tensor_scalar(var, h_mv[:, :, 1], LN_EPS, None, ALU.add).then_inc(var_m, 1)
            counts["norm"] += 1
            dve.wait_ge(h_sqrt, counts["norm"])
            rsqrt_refined(var, root, rstd)
            dlink(nc.vector.tensor_tensor(out=h_o, in0=h_o, in1=col(h_mv[:, :, 0]), op=ALU.subtract))
            dlink(nc.vector.tensor_tensor(out=h_o, in0=h_o, in1=col(rstd), op=ALU.mult))
            dve.wait_ge(gates_mixed, 2 * (h + 1))
            nc.vector.tensor_tensor(out=h_o, in0=h_o, in1=z_h[h % 2][:, 2, :, :], op=ALU.mult).then_inc(h_out, 1)

        conv_silu = sem("conv_silu")
        var_m = sem("var_m")

        def normalise_head(dve, bank, n, floor, out, gate, done, g):
            s = st_m[0:n, :]
            den = bank[0:n, MD:MD + 1]
            dlink(nc.vector.tensor_scalar(s[:, 0:1], den, -1.0, None, ALU.mult))
            dlink(nc.vector.scalar_tensor_tensor(out=s[:, 0:1], in0=den, scalar=s[:, 0:1], in1=floor,
                                                 op0=ALU.max, op1=ALU.max))
            dlink(nc.vector.reciprocal(s[:, 1:2], s[:, 0:1]))
            ins = nc.vector.tensor_scalar(out, bank[0:n, 0:MD], s[:, 1:2], None, ALU.mult)
            ins.then_inc(done, 1)
            dve.wait_ge(done, g + 1)
            dlink(nc.vector.bn_stats(bn_o[0:n, 0:6], out))
            dlink(nc.vector.bn_aggr(s[:, 2:4], bn_o[0:n, 0:6]))
            nc.vector.tensor_scalar(s[:, 4:5], s[:, 3:4], LN_EPS, None, ALU.add).then_inc(var_m, 1)
            counts["norm"] += 1
            dve.wait_ge(h_sqrt, counts["norm"])
            rsqrt_refined(s[:, 4:5], s[:, 6:7], s[:, 5:6])
            dlink(nc.vector.tensor_scalar(out, out, s[:, 2:3], s[:, 5:6], ALU.subtract, ALU.mult))
            nc.vector.tensor_tensor(out=out, in0=out, in1=gate, op=ALU.mult).then_inc(hs_out, 1)

        def scalar_sqrt(act, n):
            counts["sqrt"] += 1
            act.wait_ge(var_m, counts["sqrt"])
            nc.scalar.activation(st_m[0:n, 6:7], st_m[0:n, 4:5], ACT.Sqrt).then_inc(h_sqrt, 1)

        def scalar_mlstm_head(act, h, side):
            q_k = qk_t[h % 2]
            for u in range(2):
                act.wait_ge(kn_turned, 2 * h + u + 1)
                if h:
                    act.wait_ge(c_done, 2 * h)
                for i in range(2):
                    m = 2 * u + i
                    last = nc.scalar.activation(k_n[:, m, :], SCORES[:, i * MD:(i + 1) * MD], ACT.Copy,
                                                scale=c_w[:, m, h:h + 1])
                last.then_inc(kn_done, 1)
            for i in range(MT):
                g, n = MT * h + i, S - i * P
                act.wait_ge(w_arg, g + 1)
                nc.scalar.activation(w_t[i % 2][:, 0:n], w_t[i % 2][:, 0:n], ACT.Exp, scale=-1.0).then_inc(w_exp, 1)
                side(0)
                side(1)
                if h + 1 < H:
                    scalar_conv(act, h + 1, i)
            z = z_h[h % 2]
            act.wait_ge(zh_in[h % 2], zh_count(h))
            nc.scalar.activation(z[:, 2, :, :], z[:, 2, :, :], ACT.Sigmoid).then_inc(gate_m, 1)
            nc.scalar.activation(z[:, 3, :, :], z[:, 3, :, :], ACT.Silu).then_inc(gate_m, 1)
            counts["sqrt"] += 1
            act.wait_ge(var_m, counts["sqrt"])
            nc.scalar.activation(h_st[:, 4, :], h_st[:, 3, :], ACT.Sqrt).then_inc(h_sqrt, 1)
            if h:
                act.wait_ge(c_stored, 32 * h)
            act.wait_ge(c_done, 2 * h + 1)
            nc.scalar.copy(c_o, STATE[:, :].rearrange("p (e d) -> p e d", e=2)).then_inc(c_copied, 1)
            act.wait_ge(c_done, 2 * h + 2)
            nc.scalar.copy(n_o, n_row).then_inc(c_copied, 1)

        def sync_mlstm_out(sp, h):
            sp.wait_ge(h_out, h + 1)
            sp.dma_start(mix_p[:, h * MD:(h + 1) * MD].rearrange("(m p) c -> p m c", p=P), h_o).then_inc(h_stored, 16)
            sp.wait_ge(c_copied, 2 * h + 2)
            sp.dma_start(O["p_C"][0, 0, h].rearrange("(e p) d -> p e d", p=P), c_o).then_inc(c_stored, 16)
            sp.dma_start(O["p_n"][0, 0, h:h + 1, :], n_o).then_inc(c_stored, 16)

        XW = NQ + CK - 1
        HB = H * NB
        rows_of = lambda v, n: v[0:n]
        XN = 1104
        s_nat = rows_of(part(xh_free, XN, [5 * MW]), R)
        k_ns = rows_of(part(xh_free, XN, [MW]), R)
        n_in8 = rows_of(part(xh_free, XN + MW, [H, MD]), NB)
        QS = NB * (R + NQ)
        q_spr = part(xh_free, XN + 5 * MW, [2 * H, QS])
        s_hist = rows_of(part(xh_free, XN + 5 * MW, [2 * MW]), NB * (CK - 1))
        XT = XN + 5 * MW + 2 * H * QS
        n_nat = rows_of(part(xh_free, XT, [MD]), HB)
        am_bc = part(xh_free, XT + MD, [H, R])
        wt_s = rows_of(part(xh_free, XT + MD + H * R, [H, R]), R)
        p_ws = rows_of(part(xh_free, XT + MD + 2 * H * R, [H, R]), R)
        assert XT + MD + 3 * H * R <= KT * (S + 2 * R)
        s_low = rows_of(part(zt_free, 0, [5 * MW // 2]), R)
        x_ext = part(zt_free, 0, [KT, NB, XW])
        cv_s = part(zt_free, 896, [KT, NB, NQ])
        cv_t = part(zt_free, 1408, [KT, NB, NQ])
        decay = part(zt_free, 1408, [HB])
        n_t = part(zt_free, 1440, [2, HB])
        ct = [part(xl_free, 7176, [2, MD + 1]), part(zt_free, 1920, [2, MD + 1])]
        mk_free = mem_kv[:, :, :].rearrange("p t n -> p (t n)")
        c_in = [part(mk_free, i * 2 * MD, [2, MD]) for i in range(4)]
        for w in range(2):
            c_in += [part(between, X_HI_N + X_LO_N + w * W_N + W_N // 2 + i * 2 * MD, [2, MD]) for i in range(2)]
        NCR = len(c_in)
        vwb = rows_of(part(w_raw[:, RAWS - 1, :, :].rearrange("p k n -> p (k n)"), 0, [2, MD]), R)
        va_s = [place(M0 + 4096 + h * (MD + 1), [MD + 1], R) for h in range(3)] + [place(M0 + 15244, [MD + 1], R)]
        S_TURN, S_UPD, S_OUT = acc[3], acc[4], ps_c
        causal_s = keep_p[0:R, 0:R]
        (sm_in, sconv_out, hist_in, sx_turned, ks_turned, ks_copied, s_gate, s_added, late_in,
            ctt, ct_copied, inter_done, vwb_ready, u_done, upd_done, hs_done, sn_done, sn_copied) = (
            sem(n) for n in ("sm_in", "sconv_out", "hist_in", "sx_turned", "ks_turned", "ks_copied", "s_gate",
            "s_added", "late_in", "ctt", "ct_copied", "inter_done", "vwb_ready", "u_done",
            "upd_done", "hs_done", "sn_done", "sn_copied"))
        cin_in = [sem(f"cin_in{i}") for i in range(NCR)]
        cst_out = [sem(f"cst_out{i}") for i in range(NCR)]
        sn_out, hs_out, spread_set = sem("sn_out"), sem("hs_out"), sem("spread_set")

        def sync_mlstm_s(sp):
            sp.wait_ge(mem_out, 16 * 2 * NMEM // P)
            sp.wait_ge(mix_stored, 2 * 16 * H)
            sp.dma_start(s_nat, z_s[0:R, 0:5 * MW]).then_inc(sm_in, 16)
            sp.dma_start(s_low, z_s[R:2 * R, 0:5 * MW // 2]).then_inc(sm_in, 16)
            sp.dma_start(causal_s, C["causal_s"]).then_inc(sm_in, 16)
            sp.wait_ge(s_added, 1)
            sp.dma_start(s_low, z_s[R:2 * R, 5 * MW // 2:5 * MW]).then_inc(sm_in, 16)
            sp.dma_start(s_hist, I["state_conv"][0].rearrange("b j c -> (b j) c")).then_inc(hist_in, 16)
            sp.dma_start(n_nat, I["state_mlstm_n"][0].rearrange("b h d -> (b h) d")).then_inc(hist_in, 16)
            sp.wait_ge(*at("sm_ready"))
            for b in range(NB):
                sp.dma_start(O["s_conv"][0, b], s_nat[b * NQ + NQ - CK + 1:(b + 1) * NQ, 0:2 * MW]).then_inc(sconv_out, 16)
            sp.wait_ge(sx_turned, 2)
            sp.wait_ge(sconv_out, 16 * NB)
            sp.dma_start(n_in8, I["state_mlstm_n"][0]).then_inc(late_in, 16)
            for p in range(NCR - 1):
                sync_state_in(sp, p)

        def sync_state_in(sp, p):
            h, b = p // NB, p % NB
            if p >= NCR:
                sp.wait_ge(cst_out[p % NCR], 16 * (p // NCR))
            sp.dma_start(c_in[p % NCR], I["state_mlstm_C"][0, b, h].rearrange("(e p) d -> p e d", p=P)
                         ).then_inc(cin_in[p % NCR], 16)

        def sync_state_out(sp, p):
            h, b = p // NB, p % NB
            sp.wait_ge(upd_done, p + 1)
            sp.dma_start(O["s_C"][0, b, h].rearrange("(e p) d -> p e d", p=P), c_in[p % NCR]
                         ).then_inc(cst_out[p % NCR], 16)

        def sync_states(sp, h):
            for p in range(h * NB, (h + 1) * NB):
                sync_state_out(sp, p)
                if p + NCR - 1 < HB:
                    sync_state_in(sp, p + NCR - 1)

        def sync_states_end(sp):
            sp.wait_ge(sn_copied, H)
            sp.dma_start(O["s_n"][0], n_in8).then_inc(sn_out, 16)
            sp.wait_ge(hs_out, H)
            sp.dma_start(mix_s[:, 0:MW], s_nat[:, 3 * MW:4 * MW]).then_inc(sn_out, 16)

        def vector_mlstm_s_prep(dve):
            half = 5 * MW // 2
            dve.wait_ge(sm_in, 48)
            nc.vector.tensor_tensor(out=s_nat[:, 0:half], in0=s_nat[:, 0:half], in1=s_low, op=ALU.add).then_inc(s_added, 1)
            dve.wait_ge(sm_in, 64)
            nc.vector.tensor_tensor(out=s_nat[:, half:], in0=s_nat[:, half:], in1=s_low, op=ALU.add).then_inc(reached("sm_ready"), 1)
            yield
            yield
            dve.wait_ge(sx_turned, 2)
            nc.vector.tensor_copy(x_ext[:, :, :, CK - 1:XW], S_TURN[:, :].rearrange("p (k b t) -> p k b t", k=KT, b=NB))
            dlink(nc.vector.tensor_copy(x_ext[:, :, :, 0:CK - 1],
                                        S_UPD[:, 0:KT * NB * (CK - 1)].rearrange("p (k b j) -> p k b j", k=KT, b=NB)))
            tap = lambda j: conv_c[:, :, j:j + 1].unsqueeze(3).broadcast_to([P, KT, NB, NQ])
            dlink(nc.vector.tensor_tensor(out=cv_s, in0=x_ext[:, :, :, 0:NQ], in1=tap(0), op=ALU.mult))
            for j in range(1, CK):
                dlink(nc.vector.tensor_tensor(out=cv_t, in0=x_ext[:, :, :, j:j + NQ], in1=tap(j), op=ALU.mult))
                dlink(nc.vector.tensor_tensor(out=cv_s, in0=cv_s, in1=cv_t, op=ALU.add))
            nc.vector.tensor_tensor(out=cv_s, in0=cv_s, in1=tap(CK), op=ALU.add).then_inc(reached("scv_ready"), 1)
            dlink(nc.vector.tensor_tensor(out=w_b, in0=batch_of.unsqueeze(1).broadcast_to([R, H, NB]),
                                          in1=c_w[0:R, MT, :].unsqueeze(2).broadcast_to([R, H, NB]), op=ALU.mult))
            yield
            dve.wait_ge(*at("scv_silu"))
            nc.vector.tensor_scalar(cv_s[:, KT // 2:KT, :, :], cv_s[:, KT // 2:KT, :, :], float(MD ** -0.5), None,
                                    ALU.mult).then_inc(reached("ks_scaled"), 1)
            dve.wait_ge(*at("bc_done"))
            nc.vector.tensor_copy(am_bc, S_OUT[:, 0:H * R].rearrange("p (h r) -> p h r", h=H))
            nc.vector.tensor_copy(decay, S_OUT[:, 128:128 + HB])
            nc.vector.tensor_copy(n_t, S_OUT[:, 160:160 + 2 * HB].rearrange("p (d x) -> p d x", d=2))
            for h in range(H):
                last = nc.vector.tensor_scalar(wt_s[:, h, :], S_OUT[0:R, 224 + h * R:224 + (h + 1) * R], c_a[0:R, MT, h:h + 1],
                                               0.0, ALU.subtract, ALU.max)
            last.then_inc(reached("bc_copied"), 1)
            yield
            dve.wait_ge(*at("bc_copied"))
            dve.wait_ge(spread_set, 1)
            q5 = cv_s[:, 0:2 * H, :, :].rearrange("p (h d) b t -> p h d b t", d=2)
            o5 = q_spr.rearrange("p (h d) (b x) -> p h d b x", d=2, x=R + NQ)
            for h in range(H):
                for d in range(2):
                    last = nc.vector.tensor_tensor(out=o5[:, h, d, :, 0:NQ], in0=q5[:, h, d, :, :],
                                                   in1=am_bc[:, h, :].rearrange("p (b t) -> p b t", t=NQ), op=ALU.mult)
            last.then_inc(reached("qspr_ready"), 1)
            dve.wait_ge(s_gate, 2)
            dve.wait_ge(late_in, 16)
            so, sg = s_nat[:, 3 * MW:4 * MW], s_nat[:, 4 * MW:5 * MW]
            dlink(nc.vector.tensor_tensor(out=sg, in0=sg, in1=so, op=ALU.mult))
            dlink(nc.vector.tensor_tensor(out=sg, in0=sg, in1=hn[0:R, :], op=ALU.mult))
            yield
            dve.wait_ge(*at("sw_exp"))
            dlink(nc.vector.tensor_tensor(out=wt_s, in0=wt_s, in1=causal_s.unsqueeze(1).broadcast_to([R, H, R]), op=ALU.mult))
            dve.wait_ge(*at("ss_done"))
            nc.vector.tensor_tensor(out=p_ws, in0=S_TURN[0:R, 0:H * R].rearrange("p (h r) -> p h r", h=H), in1=wt_s,
                                    op=ALU.mult).then_inc(reached("pws_ready"), 1)
            yield

        def gpsimd_mlstm_s_prep(pool):
            pool.wait_ge(*at("sm_ready"))
            for h in range(H):
                nc.gpsimd.memset(va_s[h][:, MD:MD + 1], 1.0)
                nc.gpsimd.tensor_copy(va_s[h][:, 0:MD], s_nat[:, 2 * MW + h * MD:2 * MW + (h + 1) * MD])
            pool.wait_ge(sx_turned, 2)
            nc.gpsimd.memset(q_spr, 0.0).then_inc(spread_set, 1)

        def scalar_mlstm_s_prep(act):
            act.wait_ge(*at("sm_ready"))
            nc.scalar.activation(s_nat[:, 3 * MW:4 * MW], s_nat[:, 3 * MW:4 * MW], ACT.Sigmoid).then_inc(s_gate, 1)
            nc.scalar.activation(s_nat[:, 4 * MW:5 * MW], s_nat[:, 4 * MW:5 * MW], ACT.Silu).then_inc(s_gate, 1)
            yield
            yield
            act.wait_ge(*at("scv_ready"))
            nc.scalar.activation(cv_s, cv_s, ACT.Silu).then_inc(reached("scv_silu"), 1)
            yield
            for u in range(2):
                act.wait_ge(ks_turned, u + 1)
                act.wait_ge(sconv_out, 16 * NB)
                nc.scalar.copy(k_ns[:, u * 512:(u + 1) * 512], (S_TURN, S_UPD)[u][0:R, :]).then_inc(ks_copied, 1)
            act.wait_ge(*at("bc_copied"))
            nc.scalar.activation(wt_s, wt_s, ACT.Exp, scale=-1.0).then_inc(reached("sw_exp"), 1)
            yield

        def tensor_mlstm_s_prep(pe):
            pe.wait_ge(*at("sm_ready"))
            for k in range(KT):
                last = nc.tensor.transpose(S_TURN[:, k * R:(k + 1) * R], s_nat[:, k * P:(k + 1) * P], ident[0:R, 0:R])
            last.then_inc(sx_turned, 1)
            pe.wait_ge(hist_in, 32)
            n = NB * (CK - 1)
            for k in range(KT):
                last = nc.tensor.transpose(S_UPD[:, k * n:(k + 1) * n], s_hist[:, k * P:(k + 1) * P], ident[0:n, 0:n])
            last.then_inc(sx_turned, 1)
            for h in range(H):
                nc.tensor.matmul(S_OUT[:, h * R:(h + 1) * R], hr[:, h * P:(h + 1) * P], g_t[:, S:GW], start=True, stop=True)
                nc.tensor.matmul(S_OUT[:, 128 + h * NB:128 + (h + 1) * NB], hr[:, h * P:(h + 1) * P], a_T,
                                 start=True, stop=True)
                nc.tensor.matmul(S_OUT[0:R, 224 + h * R:224 + (h + 1) * R], hr[:, h * P:h * P + R], g_M[:, S:GW],
                                 start=True, stop=True)
            for d in range(2):
                last = nc.tensor.transpose(S_OUT[:, 160 + d * HB:160 + (d + 1) * HB], n_nat[:, d * P:(d + 1) * P],
                                           ident[0:HB, 0:HB])
            last.then_inc(reached("bc_done"), 1)
            yield
            yield
            pe.wait_ge(*at("ks_scaled"))
            for u in range(2):
                for i in range(4):
                    k = KT // 2 + 4 * u + i
                    last = nc.tensor.transpose((S_TURN, S_UPD)[u][0:R, i * P:(i + 1) * P],
                                               cv_s[:, k, :, :].rearrange("p b t -> p (b t)"), ident[:, :])
                last.then_inc(ks_turned, 1)
            yield
            pe.wait_ge(ks_copied, 2)
            for h in range(H):
                for d in range(2):
                    last = nc.tensor.matmul(S_TURN[0:R, h * R:(h + 1) * R],
                                            cv_s[:, KT // 2 + 2 * h + d, :, :].rearrange("p b t -> p (b t)"),
                                            cv_s[:, 2 * h + d, :, :].rearrange("p b t -> p (b t)"),
                                            start=d == 0, stop=d == 1)
            last.then_inc(reached("ss_done"), 1)
            yield

        def tensor_state_turn(pe, p):
            pe.wait_ge(cin_in[p % NCR], 16 * (p // NCR + 1))
            if p:
                pe.wait_ge(ct_copied, p)
            else:
                pe.wait_ge(*at("pws_ready"))
            for d in range(2):
                for e in range(2):
                    i = 2 * d + e
                    last = nc.tensor.transpose(S_TURN[:, i * P:(i + 1) * P], c_in[p % NCR][:, e, d * P:(d + 1) * P],
                                               ident[:, :])
            last.then_inc(ctt, 1)

        def tensor_mlstm_s(pe):
            pe.wait_ge(*at("qspr_ready"))
            pe.wait_ge(spread_set, 1)
            tensor_state_turn(pe, 0)
            for p in range(HB):
                h, b = p // NB, p % NB
                if b == 0:
                    if h:
                        pe.wait_ge(hs_done, h)
                    nc.tensor.matmul(S_OUT[0:R, 0:MD + 1], p_ws[:, h, :], va_s[h], start=True, stop=False)
                pe.wait_ge(vwb_ready, p + 1)
                if p:
                    pe.wait_ge(upd_done, p)
                for e in range(2):
                    last = nc.tensor.matmul(S_UPD[:, e * MD:(e + 1) * MD], vwb[:, p % 2, e * P:(e + 1) * P],
                                            k_ns[:, h * MD:(h + 1) * MD], start=True, stop=True)
                last.then_inc(u_done, 1)
                pe.wait_ge(ct_copied, p + 1)
                for d in range(2):
                    last = nc.tensor.matmul(S_OUT[0:R, 0:MD + 1], q_spr[:, 2 * h + d, b * R:(b + 1) * R], ct[p % 2][:, d, :],
                                            start=False, stop=b == NB - 1 and d == 1)
                last.then_inc(inter_done, 1)
                if p + 1 < HB:
                    tensor_state_turn(pe, p + 1)
                if b == NB - 1:
                    pe.wait_ge(upd_done, p + 1)
                    nc.tensor.matmul(S_UPD[0:NB, 0:MD], w_b[:, h, :], k_ns[:, h * MD:(h + 1) * MD],
                                     start=True, stop=True).then_inc(sn_done, 1)
                    pe.wait_ge(sn_copied, h + 1)
                yield

        def scalar_mlstm_s(act):
            for p in range(HB):
                h, b = p // NB, p % NB
                act.wait_ge(ctt, p + 1)
                if p >= 2:
                    act.wait_ge(inter_done, p - 1)
                nc.scalar.copy(ct[p % 2][:, :, 0:MD], S_TURN[:, :].rearrange("p (d e) -> p d e", d=2))
                nc.scalar.copy(ct[p % 2][:, :, MD], n_t[:, :, b * H + h]).then_inc(ct_copied, 1)
                if b == NB - 1:
                    scalar_sqrt(act, R)
                yield

        def vector_mlstm_s(dve):
            def weigh_values(p):
                h, b = p // NB, p % NB
                if p >= 2:
                    dve.wait_ge(u_done, p - 1)
                nc.vector.tensor_scalar(vwb[:, p % 2, :], s_nat[:, 2 * MW + h * MD:2 * MW + (h + 1) * MD],
                                        w_b[:, h, b:b + 1], None, ALU.mult).then_inc(vwb_ready, 1)

            weigh_values(0)
            for p in range(HB):
                h, b = p // NB, p % NB
                if p + 1 < HB:
                    weigh_values(p + 1)
                dve.wait_ge(u_done, p + 1)
                dve.wait_ge(ctt, p + 1)
                nc.vector.scalar_tensor_tensor(out=c_in[p % NCR], in0=c_in[p % NCR],
                                               scalar=decay[:, p:p + 1],
                                               in1=S_UPD[:, :].rearrange("p (e d) -> p e d", e=2),
                                               op0=ALU.mult, op1=ALU.add).then_inc(upd_done, 1)
                if b == NB - 1:
                    dve.wait_ge(inter_done, p + 1)
                    cols = slice(h * MD, (h + 1) * MD)
                    normalise_head(dve, S_OUT, R, c_e[0:R, MT, h:h + 1], s_nat[:, 3 * MW:4 * MW][:, cols],
                                   s_nat[:, 4 * MW:5 * MW][:, cols], hs_done, h)
                    dve.wait_ge(sn_done, h + 1)
                    nc.vector.scalar_tensor_tensor(out=n_in8[:, h, :], in0=n_in8[:, h, :], scalar=aT8[:, h:h + 1],
                                                   in1=S_UPD[0:NB, 0:MD], op0=ALU.mult, op1=ALU.add).then_inc(sn_copied, 1)
                yield

        y_t = place(0, [MT + 1, D])
        x_res = [place(10240, [D]), place(12288, [D]), place(16384, [D]), place(18432, [D])]
        x_res.append(rows_of(mk_free, R))
        y_buf = place(16384, [2, D])
        g_post = place(14336, [D])
        y_sum = small[:, 32:32 + NY * (MT + 1)].rearrange("p (m n) -> p m n", m=MT + 1)
        y_st = small[:, 52:57]
        y_root = small[:, 57:62]
        y_inv = keep[:, 1040:1045]
        y_rows = lambda m: y_t[:, m, :]
        y_in = lambda u: y_buf[:, u % 2, :]
        (gp_in, res_in, y_part, y_var, y_std, y_ready, y_out) = (
            sem(n) for n in ("gp_in", "res_in", "y_part", "y_var", "y_std", "y_ready", "y_out"))

        def sync_y_early(sp):
            sp.wait_ge(c_stored, 32 * H)
            sp.wait_ge(h_stored, 16 * H)
            sync_rows(sp, NU_NORM, NU_NORM + 2)
            sp.dma_start(g_post, I["norm_post"][0:1, :].broadcast_to([P, D])).then_inc(gp_in, 16)

        def sync_y_in(sp):
            sp.wait_ge(sn_out, 32)
            for i in range(NCR):
                sp.wait_ge(cst_out[i], 16 * len(range(i, HB, NCR)))
            sync_rows(sp, NU_NORM + 2, NU_ALL)
            for m in (0, 1, MT, 2, 3):
                n, x, y = y_place(m)
                if m == 2:
                    sp.wait_ge(rows_turned, NGRP * NU_ALL)
                sp.dma_start(x_res[m][0:n, :], x).then_inc(res_in, 16)

        def y_place(m):
            n = P if m < MT else R
            rows = slice(m * P, (m + 1) * P)
            if m < MT:
                return n, I["x_prompt"][0, rows, :], O["y_prompt"][0, rows, :]
            return n, I["x_sample"].rearrange("b t d -> (b t) d"), O["y_sample"].rearrange("b t d -> (b t) d")

        def sync_y_out(sp):
            for m in range(MT + 1):
                n, _, y = y_place(m)
                sp.wait_ge(y_ready, m + 1)
                sp.dma_start(y, y_t[0:n, m, :]).then_inc(y_out, 16)
            sp.wait_ge(y_out, 16 * (MT + 1))

        def scalar_y(act):
            act.wait_ge(y_var, 1)
            nc.scalar.activation(y_root, y_st, ACT.Sqrt).then_inc(y_std, 1)

        def vector_y(dve):
            dve.wait_ge(gp_in, 16)
            dve.wait_ge(lo_taken, NGRP * NU_ALL)
            dlink(nc.vector.memset(y_sum[:, MT, :], 0.0))

            def body(n):
                cols = bass.ds((n - N_Y0) * TN, TN)
                part_of = y_sum[0:R, MT, bass.ds(n - N_Y0, 1)]
                for m in range(MT):
                    dve.wait_ge(acc_read, acc_base(n) + m + 1)
                    nc.vector.tensor_tensor(out=y_t[:, m, cols], in0=y_t[:, m, cols], in1=g_post[:, cols], op=ALU.mult)
                dve.wait_ge(acc_read, acc_base(n) + MT + 1)
                low, sq = z_tile[0:R, 1, :], z_tile[0:R, 2, :]
                ys = y_t[0:R, MT, cols]
                nc.vector.tensor_copy(low, y_t[R:2 * R, MT, cols]).then_inc(y_part, 1)
                dve.wait_ge(y_part, 4 * (n - N_Y0) + 1)
                nc.vector.tensor_tensor(out=ys, in0=ys, in1=low, op=ALU.add).then_inc(y_part, 1)
                dve.wait_ge(y_part, 4 * (n - N_Y0) + 2)
                nc.vector.tensor_tensor(out=sq, in0=ys, in1=ys, op=ALU.mult).then_inc(y_part, 1)
                dve.wait_ge(y_part, 4 * (n - N_Y0) + 3)
                nc.vector.tensor_reduce(out=part_of, in_=sq, axis=AX.X, op=ALU.add)
                nc.vector.tensor_tensor(out=ys, in0=ys, in1=g_post[0:R, cols], op=ALU.mult).then_inc(y_part, 1)
                dve.wait_ge(y_part, 4 * (n - N_Y0) + 4)
            tile_loop(dve, N_Y0, N_END, body)
            dlink(nc.vector.tensor_reduce(out=y_st, in_=y_sum, axis=AX.X, op=ALU.add))
            nc.vector.tensor_scalar(y_st, y_st, 1.0 / D, RMS_EPS, ALU.mult, ALU.add).then_inc(y_var, 1)
            dve.wait_ge(y_std, 1)
            rsqrt_refined(y_st, y_root, y_inv)
            dve.wait_ge(res_in, 16 * (MT + 1))
            for m in range(MT + 1):
                n = y_place(m)[0]
                nc.vector.scalar_tensor_tensor(out=y_t[0:n, m, :], in0=y_t[0:n, m, :], scalar=y_inv[0:n, m:m + 1],
                                               in1=x_res[m][0:n, :], op0=ALU.mult, op1=ALU.add).then_inc(y_ready, 1)
        mem_out = sem("mem_out")
        block = ctx.enter_context(nc.Block())

        N_HOST = N_A0 + IXT
        TK0 = 25
        TKR = KSEL_S // 8
        CK0 = TKR - TK0 + 3

        def run(steps):
            for _ in steps:
                pass

        def beside_memory(mem_s, gates, places):
            for i, _ in enumerate(mem_s):
                if i in places:
                    next(gates)
            run(gates)

        def beside_head(h, prep, pairs):
            assert NB == 2 * MT
            def side(part):
                if h:
                    next(pairs)
                elif part == 0:
                    next(prep, None)
            return side

        def chain(*stages):
            for s in stages:
                yield from s

        def tensor_index_stage(pe):
            yield from hosted_pause(IX_PAUSE)
            yield from tensor_sample_turn(pe)
            yield from tensor_indexer(pe)

        def scalar_index_stage(act):
            yield from hosted_pause(IX_PAUSE + 1)
            yield from scalar_sample_turn(act)
            yield from scalar_indexer(act)
        IX_PAUSE = 10

        def tensor_prompt(pe):
            yield from hosted_pause(PROMPT_PAUSE)
            for m in range(MT):
                yield from tensor_prompt_turn(pe, m)
                if m:
                    yield from tensor_prompt_index(pe, m)
                yield from tensor_prompt_attend(pe, m)

        def scalar_prompt(act):
            yield from hosted_pause(PROMPT_PAUSE)
            for m in range(MT):
                yield from scalar_prompt_turn(act, m)
                if m:
                    yield from scalar_prompt_index(act, m)
                yield from scalar_prompt_attend(act, m)

        def vector_prompt(dve):
            yield from hosted_pause(PROMPT_PAUSE)
            for m in range(MT):
                yield from vector_prompt_prep(dve, m)
                yield from vector_prompt_select(dve, m)
                yield from vector_prompt_attend(dve, m)
        PROMPT_PAUSE = 8

        def tensor_rows(pe):
            yield from hosted_pause(TKR - TK0 + 1)
            yield from tensor_physical(pe)

        def vector_rows(dve):
            for i in range(TK0, TKR):
                vector_topk_sample(dve, i, i + 1)
                yield
            yield from vector_physical(dve)

        @block.sync
        def _(sp):
            sync_rows(sp, 0, 1)
            sp.dma_start(ident[:, :], C["ident"]).then_inc(consts_in, 16)
            sp.dma_start(g_row[:, :], I["mem_norm"][0:1, :].broadcast_to([P, D])).then_inc(g_loaded, 16)
            sync_rows(sp, 1, NU_NORM)
            sync_tables(sp)
            sp.wait_ge(pages_in, 16)
            sp.wait_ge(chunk_used, CH * N_A0)
            sp.wait_ge(lo_taken, NGRP * NU_NORM)
            sync_idx_pages(sp, 0, NB * NPG - POOL_PAGES)
            sp.wait_ge(acc_read, acc_base(N_A0))
            for t in range(NMEM // P):
                rows = slice(t * P, (t + 1) * P)
                sp.dma_start(O["p_mem_k"].rearrange("l b m h d -> (l b m) (h d)")[rows, :], mem_kv[:, t, 0:AW]).then_inc(mem_out, 16)
                sp.dma_start(O["p_mem_v"].rearrange("l b m h d -> (l b m) (h d)")[rows, :], mem_kv[:, t, AW:2 * AW]).then_inc(mem_out, 16)
            sync_index_in(sp)
            sync_sample_in(sp)
            for m in range(MT):
                sync_prompt_in(sp, m)
                sync_prompt_kv(sp, m)
                if m == 1:
                    sync_new_keys(sp)
                sync_prompt_out(sp, m)
            sp.wait_ge(*at("mixed_s"))
            store_mix_s(sp, o_s, MW)
            sync_mlstm_consts(sp)
            sync_mlstm_head(sp, 0)
            sync_mlstm_head(sp, 1)
            sp.wait_ge(*at("mixed_c"))
            store_mix_s(sp, o_c, MW + AW)
            sync_mlstm_m(sp)
            sync_mlstm_s(sp)
            for h in range(H):
                if h:
                    sync_states(sp, h - 1)
                sync_mlstm_out(sp, h)
                if h + 2 < H:
                    sync_mlstm_head(sp, h + 2)
            sync_y_early(sp)
            sync_states(sp, H - 1)
            sync_states_end(sp)
            sync_y_in(sp)
            sync_y_out(sp)
            sp.wait_ge(mem_out, 16 * 2 * NMEM // P)
            sp.wait_ge(conv_out, 48)

        @block.gpsimd
        def _(pool):
            tile_loop(pool, 0, N_A0, lambda n: gpsimd_tile(pool, n))
            pool.wait_ge(pages_in, 16)

            def with_pages(n):
                for c in range(CH):
                    gpsimd_lo(pool, n, c)
                    if isinstance(n, int) and c == 0:
                        pool.wait_ge(chunk_used, CH * N_A0)
                        pool.wait_ge(lo_taken, NGRP * NU_NORM)
                    for t in range(2):
                        gpsimd_page(pool, NB * NPG - POOL_PAGES + 2 * (CH * (n - N_A0) + c) + t)
            tile_loop(pool, N_A0, N_HOST, with_pages)
            tile_loop(pool, N_HOST, N_REST - 1, lambda n: gpsimd_tile(pool, n))
            for n in (N_REST - 1, N_REST):
                gpsimd_tile(pool, n)
            gathers = gpsimd_gathers(pool)
            for n in range(N_B0, N_Y0):
                gpsimd_tile(pool, n, gathers)
            run(gathers)
            gpsimd_mem_in(pool)
            gpsimd_mlstm_s_prep(pool)
            for h in range(H):
                gpsimd_mlstm_head(pool, h)
            tile_loop(pool, N_Y0, N_END, lambda n: gpsimd_tile(pool, n))

        @block.scalar
        def _(act):
            scalar_row_scale(act, 0)
            scalar_load(act, 0, 0)
            scalar_load(act, 0, 1)
            for u in range(1, NU_MEM):
                scalar_row_scale(act, u)
            for u in range(NU_MEM):
                run(scalar_take_hi(act, u))
            scalar_hi(act, 0, 0)
            scalar_row_scale(act, NU_MEM)
            norms = (chain(hosted_pause(1), *(scalar_take_hi(act, u) for u in range(NU_MEM, NU_NORM))), iter(()))
            for n in range(N_A0):
                scalar_tile(act, n, "mem", norms)
            run(norms[0])
            for n in range(N_A0, N_HOST):
                scalar_tile(act, n, "a")
            index = (scalar_index_stage(act), iter(()))
            for n in range(N_HOST, N_B0):
                scalar_tile(act, n, "a", index, often=True)
            run(index[0])
            steps = (chain(hosted_pause(1), scalar_prompt(act)), chain(hosted_pause(1), scalar_gather(act)))
            for n in range(N_B0, N_Y0):
                scalar_tile(act, n, "b", steps)
            run(steps[0])
            run(steps[1])
            beside_memory(scalar_mem_s(act), scalar_mlstm_gates(act), (4, 6, 8, 9))
            for u in range(4):
                scalar_conv(act, 0, u)
            prep, pairs = scalar_mlstm_s_prep(act), scalar_mlstm_s(act)
            for h in range(H):
                scalar_mlstm_head(act, h, beside_head(h, prep, pairs))
                run(prep)
            run(pairs)
            for u in range(NU_NORM, NU_ALL):
                run(scalar_take_hi(act, u))
            tile_loop(act, N_Y0, N_END - 1, lambda n: scalar_tile(act, n, "y"))
            scalar_tile(act, N_END - 1, "y")
            scalar_y(act)

        @block.vector
        def _(dve):
            for u in range(NU_MEM):
                vector_row_scale(dve, u)
            for u in range(NU_MEM):
                vector_take_lo(dve, u)
            vector_row_scale(dve, NU_MEM)
            for u in range(NU_MEM, NU_NORM):
                vector_take_lo(dve, u)
            vector_index_prep(dve)
            vector_scores(dve)
            vector_topk_sample(dve, 0, TK0)
            vector_sample_prep(dve)
            prompt, rows = vector_prompt(dve), chain(vector_rows(dve), hosted_pause(1), vector_gather(dve))
            for _ in range(CH * NBT):
                next(prompt, None)
                next(rows, None)
                next(prompt, None)
            run(prompt)
            run(rows)
            vector_gather_out(dve)
            mem_s = vector_mem_s(dve)
            next(mem_s)
            vector_mlstm_gates(dve)
            run(mem_s)
            for u in range(4):
                vector_conv(dve, 0, u)
            prep, pairs = vector_mlstm_s_prep(dve), vector_mlstm_s(dve)
            next(prep)
            for h in range(H):
                vector_mlstm_head(dve, h, beside_head(h, prep, pairs))
                run(prep)
            run(pairs)
            for u in range(NU_NORM, NU_ALL):
                vector_take_lo(dve, u)
            vector_y(dve)

        @block.tensor
        def _(pe):
            pe.wait_ge(consts_in, 16)
            for u in range(NU_MEM):
                run(tensor_turn(pe, u))
            norms = (chain(*(tensor_turn(pe, u) for u in range(NU_MEM, NU_NORM))), iter(()))
            for n in range(N_A0):
                tensor_tile(pe, n, "mem", norms)
            run(norms[0])
            for n in range(N_A0, N_HOST):
                tensor_tile(pe, n, "a")
            index = (tensor_index_stage(pe), iter(()))
            for n in range(N_HOST, N_B0):
                tensor_tile(pe, n, "a", index, often=True)
            run(index[0])
            steps = (tensor_prompt(pe), chain(tensor_rows(pe), tensor_gather(pe)))
            for n in range(N_B0, N_Y0):
                tensor_tile(pe, n, "b", steps)
            run(steps[0])
            run(steps[1])
            tensor_gather_out(pe)
            beside_memory(tensor_mem_s(pe), tensor_mlstm_gates(pe), (4, 6, 9))
            for u in range(4):
                tensor_conv_turn(pe, 0, u)
            prep, pairs = tensor_mlstm_s_prep(pe), tensor_mlstm_s(pe)
            for h in range(H):
                tensor_mlstm_head(pe, h, beside_head(h, prep, pairs))
                run(prep)
            run(pairs)
            for u in range(NU_NORM, NU_ALL):
                run(tensor_turn(pe, u))
            tile_loop(pe, N_Y0, N_END, lambda n: tensor_tile(pe, n, "y"))

_INS = ["x_prompt", "x_sample", "cache_attn_k", "cache_attn_v", "cache_idx_k", "state_mlstm_C", "state_mlstm_n",
        "state_mlstm_m", "state_conv", "cache_mem_k", "cache_mem_v", "page_table", "mem_prompt", "norm_pre", "w_in",
        "b_if", "conv_w", "conv_b", "mlstm_head_norm", "mem_norm", "w_mem_kv", "w_out", "norm_post"]
_OUTS = [("y_prompt", (1, 512, 2048)), ("y_sample", (8, 4, 2048)), ("p_attn_k", (1, 1, 512, 4, 128)),
         ("p_attn_v", (1, 1, 512, 4, 128)), ("p_idx_k", (1, 1, 512, 64)), ("p_C", (1, 1, 4, 256, 256)),
         ("p_n", (1, 1, 4, 256)), ("p_m", (1, 1, 4)), ("p_conv", (1, 1, 3, 2048)), ("p_mem_k", (1, 1, 256, 4, 128)),
         ("p_mem_v", (1, 1, 256, 4, 128)), ("s_attn_k", (1, 8, 4, 4, 128)), ("s_attn_v", (1, 8, 4, 4, 128)),
         ("s_idx_k", (1, 8, 4, 64)), ("s_C", (1, 8, 4, 256, 256)), ("s_n", (1, 8, 4, 256)), ("s_m", (1, 8, 4)),
         ("s_conv", (1, 8, 3, 2048))]

def constants():
    import numpy as np
    f = np.float32
    s, nb, nq, past, heads, ih = 512, 8, 4, 2048, 4, 16
    pos = np.concatenate([np.arange(s), np.tile(past + np.arange(nq), nb)]).astype(f)

    def angles(half):
        inv = np.power(f(500000.0), -np.arange(half, dtype=f) / f(half)).astype(f)
        a = (pos[:, None] * inv[None, :]).astype(f)
        return np.cos(a).astype(f), np.sin(a).astype(f)

    r = np.arange(nb * nq)
    same = (r[:, None] // nq) == (r[None, :] // nq)
    c = {"ident": np.eye(128, dtype=f), "rope": np.concatenate(angles(16) + angles(8), axis=1)}
    t = np.arange(128)
    c["causal"] = (t[:, None] <= t[None, :]).astype(f)
    c["causal_s"] = (same & (r[:, None] <= r[None, :])).astype(f)
    c["future"] = np.where(t[None, :] <= t[:, None], f(0), f(-1e30)).astype(f)
    c["future_s"] = np.where(np.arange(nq)[None, :] <= (r % nq)[:, None], f(0), f(-1e30)).astype(f)
    row_q = np.arange(ih * nq) % nq
    e = (row_q[:, None, None] == (r % nq)[None, None, :]) & (np.arange(nb)[None, :, None] == (r // nq)[None, None, :])
    c["pick"] = e.reshape(ih * nq, nb * nb * nq).astype(f)
    c["head_row"] = np.repeat(np.eye(heads, dtype=f), 128, axis=1)
    c["batch_of"] = ((r[:, None] // nq) == np.arange(nb)[None, :]).astype(f)
    carry = np.ones((heads, s + nb * nq), f)
    carry[:, 0] = 0
    carry[:, s::nq] = 0
    c["carry"], c["zeros"] = carry, np.zeros((heads, s + nb * nq), f)
    return c

def kernel(**inputs):
    import numpy as _np
    import concourse.bacc as _bacc
    from concourse import mybir as _mybir
    from concourse.bass_utils import run_bass_kernel_spmd as _run

    nc = _bacc.Bacc("TRN2", target_bir_lowering=False, num_devices=1)
    arrays, ins, consts, outs = {}, {}, {}, {}
    for name in _INS:
        a = _np.ascontiguousarray(inputs[name])
        arrays[f"in_{name}"] = a
        ins[name] = nc.dram_tensor(f"in_{name}", a.shape, _mybir.dt.from_np(a.dtype), kind="ExternalInput").ap()
    for name, a in constants().items():
        arrays[f"const_{name}"] = _np.ascontiguousarray(a)
        consts[name] = nc.dram_tensor(f"const_{name}", a.shape, _mybir.dt.float32, kind="ExternalInput").ap()
    for name, shape in _OUTS:
        outs[name] = nc.dram_tensor(f"out_{name}", shape, _mybir.dt.float32, kind="ExternalOutput").ap()
    hybrid_decoder_step(nc, ins, consts, outs)
    r = _run(nc, [arrays], core_ids=[0])
    return tuple(r.results[0][f"out_{name}"] for name, _ in _OUTS)
```
